# Optimizing a Trainium2 kernel written in Bass

```python
import jax
import jax.numpy as jnp
from jax import lax
import numpy as np
import math
import jax, jax.numpy as jnp

D_MODEL = 1024
BATCH = 1
SEQ = 512
DEPTH = 1

PLE_DIM = 256
D_FF = 2816
N_HEADS = 8
N_KV_HEADS = 2
HEAD_DIM = 64
HEADS_PER_GROUP = N_HEADS // N_KV_HEADS
NSA_WIDTH = N_HEADS * HEAD_DIM
KV_WIDTH = N_KV_HEADS * HEAD_DIM
S5_WIDTH = D_MODEL - NSA_WIDTH
S5_GROUP = 16
S5_GROUPS = S5_WIDTH // S5_GROUP
S5_STATE = 64
CMP_LEN = 32
CMP_STRIDE = 16
CMP_HIDDEN = 256
SEL_BLOCK = 64
SEL_TOPK = 16
WINDOW = 512
Q_BLOCK = 128
ROPE_THETA = 10000.0
RMS_EPS = 1e-6
NEG = -1e30
BIG = 1e9
IN_COLS = NSA_WIDTH + 6 * KV_WIDTH + 3 * N_HEADS + S5_WIDTH


def rmsnorm(x, g):
    xf = x.astype(jnp.float32)
    y = xf * lax.rsqrt(jnp.mean(xf * xf, axis=-1, keepdims=True) + RMS_EPS)
    return (y * g.astype(jnp.float32)).astype(x.dtype)

def swiglu(x, w1, w3, w2):
    return (jax.nn.silu(x @ w1) * (x @ w3)) @ w2

def rope(x, pos):
    half = HEAD_DIM // 2
    inv = ROPE_THETA ** (-jnp.arange(half, dtype=jnp.float32) / half)
    ang = pos[:, None] * inv[None, :]
    cos = jnp.cos(ang)[None, :, None, :]
    sin = jnp.sin(ang)[None, :, None, :]
    xf = x.astype(jnp.float32)
    x1, x2 = xf[..., :half], xf[..., half:]
    return jnp.concatenate([x1 * cos - x2 * sin, x1 * sin + x2 * cos], axis=-1).astype(x.dtype)

def masked_softmax(s, mask):
    s = jnp.where(mask, s, NEG)
    m = jnp.max(s, axis=-1, keepdims=True)
    e = jnp.where(mask, jnp.exp(s - m), 0.0)
    return e / jnp.maximum(jnp.sum(e, axis=-1, keepdims=True), 1e-30)

def compress(kv, pe, w1, w2):
    B, L = kv.shape[:2]
    n_cmp = (L - CMP_LEN) // CMP_STRIDE + 1
    tok = jnp.arange(n_cmp)[:, None] * CMP_STRIDE + jnp.arange(CMP_LEN)[None, :]
    blk = kv[:, tok] + pe[None, None, :, None, :]
    blk = jnp.transpose(blk, (0, 1, 3, 2, 4)).reshape(B, n_cmp, N_KV_HEADS, CMP_LEN * HEAD_DIM)
    return jax.nn.gelu(blk @ w1) @ w2

def nsa_attention(q, k_cmp, v_cmp, k_slc, v_slc, k_win, v_win, gates, pe_k, pe_v, wk1, wk2, wv1, wv2):
    B, L = q.shape[:2]
    G, HPG, DK = N_KV_HEADS, HEADS_PER_GROUP, HEAD_DIM
    n_cmp = (L - CMP_LEN) // CMP_STRIDE + 1
    n_sel = L // SEL_BLOCK
    n_qb = L // Q_BLOCK
    top_k = min(SEL_TOPK, n_sel)
    scale = DK ** -0.5

    kc = compress(k_cmp, pe_k, wk1, wk2)
    vc = compress(v_cmp, pe_v, wv1, wv2)
    c_start = jnp.arange(n_cmp) * CMP_STRIDE
    c_end = c_start + CMP_LEN - 1
    s_start = jnp.arange(n_sel) * SEL_BLOCK
    overlap = ((c_start[:, None] < s_start[None, :] + SEL_BLOCK)
               & (c_start[:, None] + CMP_LEN > s_start[None, :])).astype(jnp.float32)

    ks_blk = jnp.transpose(k_slc.reshape(B, n_sel, SEL_BLOCK, G, DK), (0, 3, 1, 2, 4))
    vs_blk = jnp.transpose(v_slc.reshape(B, n_sel, SEL_BLOCK, G, DK), (0, 3, 1, 2, 4))
    kw_pad = jnp.pad(k_win, ((0, 0), (WINDOW, 0), (0, 0), (0, 0)))
    vw_pad = jnp.pad(v_win, ((0, 0), (WINDOW, 0), (0, 0), (0, 0)))
    b_ix = jnp.arange(B)[:, None, None, None]
    g_ix = jnp.arange(G)[None, :, None, None]
    blk_ids = jnp.arange(n_sel)

    q_blocks = jnp.transpose(q.reshape(B, n_qb, Q_BLOCK, G, HPG, DK), (1, 0, 2, 3, 4, 5))
    g_blocks = jnp.transpose(gates.reshape(B, n_qb, Q_BLOCK, G, HPG, 3), (1, 0, 2, 3, 4, 5))

    def one_block(args):
        c, qc, gc = args
        t = c * Q_BLOCK + jnp.arange(Q_BLOCK)
        s = jnp.einsum('bqghd,bcgd->bghqc', qc, kc).astype(jnp.float32) * scale
        p_cmp = masked_softmax(s, c_end[None, :] <= t[:, None])
        o_cmp = jnp.einsum('bghqc,bcgd->bqghd', p_cmp.astype(vc.dtype), vc)
        imp = jnp.einsum('bghqc,cs->bgqs', p_cmp, overlap)
        cur = (t // SEL_BLOCK)[:, None]
        valid = blk_ids[None, :] <= cur
        forced = (blk_ids[None, :] == 0) | (blk_ids[None, :] == cur) | (blk_ids[None, :] == cur - 1)
        score = jnp.where(valid & forced, BIG, jnp.where(valid, imp, -BIG))
        _, idx = lax.top_k(score, top_k)
        k_sel = ks_blk[b_ix, g_ix, idx]
        v_sel = vs_blk[b_ix, g_ix, idx].reshape(B, G, Q_BLOCK, top_k * SEL_BLOCK, DK)
        s = jnp.einsum('bqghd,bgqkrd->bghqkr', qc, k_sel).astype(jnp.float32) * scale
        s = s.reshape(B, G, HPG, Q_BLOCK, top_k * SEL_BLOCK)
        kpos = (idx[..., None] * SEL_BLOCK + jnp.arange(SEL_BLOCK)).reshape(B, G, 1, Q_BLOCK, top_k * SEL_BLOCK)
        p_slc = masked_softmax(s, kpos <= t[:, None])
        o_slc = jnp.einsum('bghqn,bgqnd->bqghd', p_slc.astype(v_sel.dtype), v_sel)
        start = c * Q_BLOCK
        k_w = lax.dynamic_slice_in_dim(kw_pad, start, WINDOW + Q_BLOCK, axis=1)
        v_w = lax.dynamic_slice_in_dim(vw_pad, start, WINDOW + Q_BLOCK, axis=1)
        spos = start - WINDOW + jnp.arange(WINDOW + Q_BLOCK)
        dist = t[:, None] - spos[None, :]
        wmask = (spos[None, :] >= 0) & (dist >= 0) & (dist < WINDOW)
        s = jnp.einsum('bqghd,bsgd->bghqs', qc, k_w).astype(jnp.float32) * scale
        p_win = masked_softmax(s, wmask)
        o_win = jnp.einsum('bghqs,bsgd->bqghd', p_win.astype(v_w.dtype), v_w)
        o = gc[..., 0:1] * o_cmp + gc[..., 1:2] * o_slc + gc[..., 2:3] * o_win
        return o.astype(qc.dtype)

    out = lax.map(one_block, (jnp.arange(n_qb), q_blocks, g_blocks))
    return jnp.transpose(out, (1, 0, 2, 3, 4, 5)).reshape(B, L, NSA_WIDTH)

def s5_mixer(u, a_re, a_im, log_dt, b_re, b_im, c_re, c_im, d_skip, w_glu, b_glu):
    B, L = u.shape[:2]
    f32 = jnp.float32
    uf = u.astype(f32).reshape(B, L, S5_GROUPS, S5_GROUP)
    lam = lax.complex(a_re.astype(f32), a_im.astype(f32))
    dt = jnp.exp(log_dt.astype(f32))[:, None]
    a_bar = jnp.exp(lam * dt)
    b_coef = (a_bar - 1.0) / lam
    bu_re = jnp.einsum('blgi,gni->blgn', uf, b_re.astype(f32))
    bu_im = jnp.einsum('blgi,gni->blgn', uf, b_im.astype(f32))
    bu = lax.complex(bu_re, bu_im) * b_coef
    a_seq = jnp.broadcast_to(a_bar, (1, L) + a_bar.shape)

    def combine(e1, e2):
        a1, x1 = e1
        a2, x2 = e2
        return a2 * a1, a2 * x1 + x2

    _, state = lax.associative_scan(combine, (a_seq, bu), axis=1)
    y = (jnp.einsum('blgn,gon->blgo', jnp.real(state), c_re.astype(f32))
         - jnp.einsum('blgn,gon->blgo', jnp.imag(state), c_im.astype(f32))
         + d_skip.astype(f32) * uf)
    y = jax.nn.gelu(y.reshape(B, L, S5_WIDTH))
    out = y * jax.nn.sigmoid(y @ w_glu.astype(f32) + b_glu.astype(f32))
    return out.astype(u.dtype)

def first_inputs(seed: int = 0) -> dict:
    key = jax.random.key(seed)
    ks = jax.random.split(key, 40)
    f32 = jnp.float32

    def nrm(k, shape, fan_in):
        return jax.random.normal(k, shape, f32) * (fan_in ** -0.5)

    def gain(k, shape):
        return 1.0 + 0.05 * jax.random.normal(k, shape, f32)

    n_idx = jnp.arange(S5_STATE, dtype=f32)
    return {
        "x": jax.random.normal(ks[0], (BATCH, SEQ, D_MODEL), f32),
        "p": jax.random.normal(ks[1], (DEPTH, BATCH, SEQ, PLE_DIM), f32),
        "norm_ffn1": gain(ks[2], (DEPTH, D_MODEL)),
        "ffn1_w1": nrm(ks[3], (DEPTH, D_MODEL, D_FF), D_MODEL),
        "ffn1_w3": nrm(ks[4], (DEPTH, D_MODEL, D_FF), D_MODEL),
        "ffn1_w2": nrm(ks[5], (DEPTH, D_FF, D_MODEL), D_FF),
        "norm_mix": gain(ks[6], (DEPTH, D_MODEL)),
        "w_in": nrm(ks[7], (DEPTH, D_MODEL, IN_COLS), D_MODEL),
        "cmp_pe_k": 0.1 * jax.random.normal(ks[8], (DEPTH, CMP_LEN, HEAD_DIM), f32),
        "cmp_pe_v": 0.1 * jax.random.normal(ks[9], (DEPTH, CMP_LEN, HEAD_DIM), f32),
        "cmp_wk1": nrm(ks[10], (DEPTH, CMP_LEN * HEAD_DIM, CMP_HIDDEN), CMP_LEN * HEAD_DIM),
        "cmp_wk2": nrm(ks[11], (DEPTH, CMP_HIDDEN, HEAD_DIM), CMP_HIDDEN),
        "cmp_wv1": nrm(ks[12], (DEPTH, CMP_LEN * HEAD_DIM, CMP_HIDDEN), CMP_LEN * HEAD_DIM),
        "cmp_wv2": nrm(ks[13], (DEPTH, CMP_HIDDEN, HEAD_DIM), CMP_HIDDEN),
        "s5_a_re": -0.5 + 0.01 * jax.random.normal(ks[14], (DEPTH, S5_GROUPS, S5_STATE), f32),
        "s5_a_im": jnp.pi * n_idx + 0.01 * jax.random.normal(ks[15], (DEPTH, S5_GROUPS, S5_STATE), f32),
        "s5_log_dt": jax.random.uniform(ks[16], (DEPTH, S5_GROUPS), f32, jnp.log(0.001), jnp.log(0.1)),
        "s5_b_re": nrm(ks[17], (DEPTH, S5_GROUPS, S5_STATE, S5_GROUP), 2 * S5_GROUP),
        "s5_b_im": nrm(ks[18], (DEPTH, S5_GROUPS, S5_STATE, S5_GROUP), 2 * S5_GROUP),
        "s5_c_re": nrm(ks[19], (DEPTH, S5_GROUPS, S5_GROUP, S5_STATE), S5_STATE),
        "s5_c_im": nrm(ks[20], (DEPTH, S5_GROUPS, S5_GROUP, S5_STATE), S5_STATE),
        "s5_d": jax.random.normal(ks[21], (DEPTH, S5_GROUPS, S5_GROUP), f32),
        "s5_w_glu": nrm(ks[22], (DEPTH, S5_WIDTH, S5_WIDTH), S5_WIDTH),
        "s5_b_glu": 0.01 * jax.random.normal(ks[23], (DEPTH, S5_WIDTH), f32),
        "w_out": nrm(ks[24], (DEPTH, D_MODEL, D_MODEL), D_MODEL),
        "norm_ffn2": gain(ks[25], (DEPTH, D_MODEL)),
        "ffn2_w1": nrm(ks[26], (DEPTH, D_MODEL, D_FF), D_MODEL),
        "ffn2_w3": nrm(ks[27], (DEPTH, D_MODEL, D_FF), D_MODEL),
        "ffn2_w2": nrm(ks[28], (DEPTH, D_FF, D_MODEL), D_FF),
        "norm_ple": gain(ks[29], (DEPTH, D_MODEL)),
        "w_ple_gate": nrm(ks[30], (DEPTH, D_MODEL, D_MODEL), D_MODEL),
        "w_ple": nrm(ks[31], (DEPTH, PLE_DIM, D_MODEL), PLE_DIM),
        "norm_final": gain(ks[32], (D_MODEL,)),
    }

def first_block(x, p, norm_ffn1, ffn1_w1, ffn1_w3, ffn1_w2, norm_mix, w_in,
              cmp_pe_k, cmp_pe_v, cmp_wk1, cmp_wk2, cmp_wv1, cmp_wv2,
              s5_a_re, s5_a_im, s5_log_dt, s5_b_re, s5_b_im, s5_c_re, s5_c_im, s5_d,
              s5_w_glu, s5_b_glu, w_out, norm_ffn2, ffn2_w1, ffn2_w3, ffn2_w2,
              norm_ple, w_ple_gate, w_ple, norm_final):
    B, L = x.shape[:2]
    pos = jnp.arange(L, dtype=jnp.float32)
    split_at = [NSA_WIDTH + k * KV_WIDTH for k in range(7)] + [NSA_WIDTH + 6 * KV_WIDTH + 3 * N_HEADS]
    h = x
    for i in range(DEPTH):
        h = h + 0.5 * swiglu(rmsnorm(h, norm_ffn1[i]), ffn1_w1[i], ffn1_w3[i], ffn1_w2[i])
        z = rmsnorm(h, norm_mix[i]) @ w_in[i]
        q, kc, vc, ksl, vsl, kw, vw, g, u = jnp.split(z, split_at, axis=-1)
        kvshape = (B, L, N_KV_HEADS, HEAD_DIM)
        q = rope(q.reshape(B, L, N_HEADS, HEAD_DIM), pos)
        kc = rope(kc.reshape(kvshape), pos)
        ksl = rope(ksl.reshape(kvshape), pos)
        kw = rope(kw.reshape(kvshape), pos)
        gates = jax.nn.sigmoid(g.reshape(B, L, N_HEADS, 3))
        o_nsa = nsa_attention(q, kc, vc.reshape(kvshape), ksl, vsl.reshape(kvshape), kw, vw.reshape(kvshape),
                              gates, cmp_pe_k[i], cmp_pe_v[i], cmp_wk1[i], cmp_wk2[i], cmp_wv1[i], cmp_wv2[i])
        o_s5 = s5_mixer(u, s5_a_re[i], s5_a_im[i], s5_log_dt[i], s5_b_re[i], s5_b_im[i],
                        s5_c_re[i], s5_c_im[i], s5_d[i], s5_w_glu[i], s5_b_glu[i])
        h = h + jnp.concatenate([o_nsa, o_s5], axis=-1) @ w_out[i]
        h = h + 0.5 * swiglu(rmsnorm(h, norm_ffn2[i]), ffn2_w1[i], ffn2_w3[i], ffn2_w2[i])
        gate = jax.nn.sigmoid(rmsnorm(h, norm_ple[i]) @ w_ple_gate[i])
        h = h + gate * (p[i] @ w_ple[i])
    return rmsnorm(h, norm_final)


DEPTH_2 = 2

D_RG = D_MODEL
RG_HEADS = 8
RG_HEAD_DIM = D_RG // RG_HEADS
D_ML = D_MODEL
ML_HEADS = 4
ML_HEAD_DIM = D_ML // ML_HEADS
D_MIX = D_RG + D_ML
D_IN = 2 * D_RG + 3 * D_ML
CONV_WIDTH = 4
RG_C = 8.0
ML_CHUNK = 128
EPS = 1e-6


def rms_norm(x, g):
    x32 = x.astype(jnp.float32)
    y = x32 * lax.rsqrt(jnp.mean(x32 * x32, axis=-1, keepdims=True) + EPS)
    return (y * g.astype(jnp.float32)).astype(x.dtype)

def causal_depthwise_conv(x, w, b):
    ch = x.shape[-1]
    y = lax.conv_general_dilated(
        x, w[:, None, :].astype(x.dtype), window_strides=(1,),
        padding=[(CONV_WIDTH - 1, 0)], dimension_numbers=("NWC", "WIO", "NWC"),
        feature_group_count=ch)
    return y + b.astype(x.dtype)

def block_diag(x, w):
    h, dh, dout = w.shape
    xb = x.reshape(x.shape[:-1] + (h, dh))
    return jnp.einsum("bshd,hde->bshe", xb, w).reshape(x.shape[:-1] + (h * dout,))

def rglru(x, w_a, b_a, w_x, b_x, lam):
    r = jax.nn.sigmoid(block_diag(x, w_a) + b_a).astype(jnp.float32)
    i = jax.nn.sigmoid(block_diag(x, w_x) + b_x).astype(jnp.float32)
    log_a = -RG_C * r * jax.nn.softplus(-lam.astype(jnp.float32))
    a = jnp.exp(log_a)
    u = jnp.sqrt(-jnp.expm1(2.0 * log_a)) * (i * x.astype(jnp.float32))

    def combine(lhs, rhs):
        a1, b1 = lhs
        a2, b2 = rhs
        return a1 * a2, a2 * b1 + b2

    _, h = lax.associative_scan(combine, (a, u), axis=1)
    return h.astype(x.dtype)

def mlstm_chunkwise(q, k, v, log_i, log_f):
    bsz, s_len, nh, dh = q.shape
    nc = s_len // ML_CHUNK

    def to_chunks(t):
        return t.reshape(bsz, nc, ML_CHUNK, nh, dh).transpose(1, 0, 3, 2, 4)

    def gate_chunks(t):
        return t.reshape(bsz, nc, ML_CHUNK, nh).transpose(1, 0, 3, 2)

    causal = jnp.tril(jnp.ones((ML_CHUNK, ML_CHUNK), dtype=bool))

    def step(carry, xs):
        c_st, n_st, m_st = carry
        qc, kc, vc, li, lf = xs
        b = jnp.cumsum(lf, axis=-1)
        b_last = b[..., -1]
        d = jnp.where(causal, b[..., :, None] - b[..., None, :] + li[..., None, :], -jnp.inf)
        m_inter = b + m_st[..., None]
        m_t = jnp.maximum(m_inter, jnp.max(d, axis=-1))
        w_intra = jnp.exp(d - m_t[..., None])
        w_inter = jnp.exp(m_inter - m_t)
        s = jnp.einsum("bhtk,bhsk->bhts", qc, kc) * w_intra
        num = (jnp.einsum("bhts,bhsv->bhtv", s, vc)
               + w_inter[..., None] * jnp.einsum("bhtk,bhkv->bhtv", qc, c_st))
        den = jnp.sum(s, axis=-1) + w_inter * jnp.einsum("bhtk,bhk->bht", qc, n_st)
        h = num / jnp.maximum(jnp.abs(den), jnp.exp(-m_t))[..., None]
        g = b_last[..., None] - b + li
        m_new = jnp.maximum(b_last + m_st, jnp.max(g, axis=-1))
        w_state = jnp.exp(g - m_new[..., None])
        decay = jnp.exp(b_last + m_st - m_new)
        kw = kc * w_state[..., None]
        c_new = decay[..., None, None] * c_st + jnp.einsum("bhsk,bhsv->bhkv", kw, vc)
        n_new = decay[..., None] * n_st + jnp.sum(kw, axis=2)
        return (c_new, n_new, m_new), h

    init = (jnp.zeros((bsz, nh, dh, dh), jnp.float32),
            jnp.zeros((bsz, nh, dh), jnp.float32),
            jnp.zeros((bsz, nh), jnp.float32))
    _, h = lax.scan(step, init, (to_chunks(q), to_chunks(k), to_chunks(v),
                                 gate_chunks(log_i), gate_chunks(log_f)))
    return h.transpose(1, 0, 3, 2, 4).reshape(bsz, s_len, nh, dh)

def mlstm_branch(xm, o_pre, conv_w, conv_b, w_q, w_k, w_v, w_if, b_if, head_g):
    bsz, s_len, _ = xm.shape
    xc = jax.nn.silu(causal_depthwise_conv(xm, conv_w, conv_b))
    q = block_diag(xc, w_q)
    k = block_diag(xc, w_k)
    v = block_diag(xm, w_v)
    gates = (jnp.concatenate([q, k, v], axis=-1) @ w_if + b_if).astype(jnp.float32)
    log_i = gates[..., :ML_HEADS]
    log_f = jax.nn.log_sigmoid(gates[..., ML_HEADS:])

    def heads(t):
        return t.reshape(bsz, s_len, ML_HEADS, ML_HEAD_DIM).astype(jnp.float32)

    cell = mlstm_chunkwise(heads(q), heads(k) * (ML_HEAD_DIM ** -0.5), heads(v), log_i, log_f)
    h = jax.nn.sigmoid(heads(o_pre)) * cell
    h = h * lax.rsqrt(jnp.mean(h * h, axis=-1, keepdims=True) + EPS)
    return (h.reshape(bsz, s_len, D_ML) * head_g.astype(jnp.float32)).astype(xm.dtype)

def second_inputs(seed: int = 0) -> dict:
    key = jax.random.key(seed)
    ks = jax.random.split(key, 24)
    f32 = jnp.float32

    def nrm(k, shape, scale):
        return jax.random.normal(k, shape, f32) * scale

    x = jax.random.normal(ks[0], (BATCH, SEQ, D_MODEL), f32)
    c = jax.random.normal(ks[1], (BATCH, D_MODEL), f32)
    norm_g = 1.0 + nrm(ks[2], (DEPTH_2, D_MODEL), 0.02)
    w_ada = nrm(ks[3], (DEPTH_2, D_MODEL, 3 * D_MODEL), 0.3 * D_MODEL ** -0.5)
    b_ada = nrm(ks[4], (DEPTH_2, 3 * D_MODEL), 0.02)
    w_in = nrm(ks[5], (DEPTH_2, D_MODEL, D_IN), D_MODEL ** -0.5)
    rg_conv_w = nrm(ks[6], (DEPTH_2, CONV_WIDTH, D_RG), CONV_WIDTH ** -0.5)
    rg_conv_b = nrm(ks[7], (DEPTH_2, D_RG), 0.02)
    rg_w_a = nrm(ks[8], (DEPTH_2, RG_HEADS, RG_HEAD_DIM, RG_HEAD_DIM), RG_HEAD_DIM ** -0.5)
    rg_b_a = nrm(ks[9], (DEPTH_2, D_RG), 0.02)
    rg_w_x = nrm(ks[10], (DEPTH_2, RG_HEADS, RG_HEAD_DIM, RG_HEAD_DIM), RG_HEAD_DIM ** -0.5)
    rg_b_x = nrm(ks[11], (DEPTH_2, D_RG), 0.02)
    a_c = jax.random.uniform(ks[12], (DEPTH_2, D_RG), f32, 0.9, 0.999)
    a0 = a_c ** (1.0 / RG_C)
    rg_lambda = jnp.log(a0) - jnp.log1p(-a0)
    ml_conv_w = nrm(ks[13], (DEPTH_2, CONV_WIDTH, D_ML), CONV_WIDTH ** -0.5)
    ml_conv_b = nrm(ks[14], (DEPTH_2, D_ML), 0.02)
    ml_w_q = nrm(ks[15], (DEPTH_2, ML_HEADS, ML_HEAD_DIM, ML_HEAD_DIM), ML_HEAD_DIM ** -0.5)
    ml_w_k = nrm(ks[16], (DEPTH_2, ML_HEADS, ML_HEAD_DIM, ML_HEAD_DIM), ML_HEAD_DIM ** -0.5)
    ml_w_v = nrm(ks[17], (DEPTH_2, ML_HEADS, ML_HEAD_DIM, ML_HEAD_DIM), ML_HEAD_DIM ** -0.5)
    ml_w_if = nrm(ks[18], (DEPTH_2, 3 * D_ML, 2 * ML_HEADS), 0.1 * (3 * D_ML) ** -0.5)
    b_i = nrm(ks[19], (DEPTH_2, ML_HEADS), 0.1) - 1.0
    b_f = jnp.linspace(3.0, 6.0, ML_HEADS, dtype=f32)[None, :] + nrm(ks[20], (DEPTH_2, ML_HEADS), 0.1)
    ml_b_if = jnp.concatenate([b_i, b_f], axis=-1)
    ml_norm_g = 1.0 + nrm(ks[21], (DEPTH_2, D_ML), 0.02)
    w_out = nrm(ks[22], (DEPTH_2, D_MIX, D_MODEL), D_MIX ** -0.5)
    final_g = 1.0 + nrm(ks[23], (D_MODEL,), 0.02)
    return {"x": x, "c": c, "norm_g": norm_g, "w_ada": w_ada, "b_ada": b_ada,
            "w_in": w_in, "rg_conv_w": rg_conv_w, "rg_conv_b": rg_conv_b,
            "rg_w_a": rg_w_a, "rg_b_a": rg_b_a, "rg_w_x": rg_w_x, "rg_b_x": rg_b_x,
            "rg_lambda": rg_lambda, "ml_conv_w": ml_conv_w, "ml_conv_b": ml_conv_b,
            "ml_w_q": ml_w_q, "ml_w_k": ml_w_k, "ml_w_v": ml_w_v, "ml_w_if": ml_w_if,
            "ml_b_if": ml_b_if, "ml_norm_g": ml_norm_g, "w_out": w_out, "final_g": final_g}

def second_block(x, c, norm_g, w_ada, b_ada, w_in, rg_conv_w, rg_conv_b, rg_w_a, rg_b_a,
              rg_w_x, rg_b_x, rg_lambda, ml_conv_w, ml_conv_b, ml_w_q, ml_w_k, ml_w_v,
              ml_w_if, ml_b_if, ml_norm_g, w_out, final_g):
    split_pts = [D_RG, 2 * D_RG, 2 * D_RG + D_ML, 2 * D_RG + 2 * D_ML]
    c_act = jax.nn.silu(c)
    for l in range(DEPTH_2):
        mod = c_act @ w_ada[l] + b_ada[l]
        shift, scale, gate = jnp.split(mod, 3, axis=-1)
        h = rms_norm(x, norm_g[l]) * (1.0 + scale[:, None, :]) + shift[:, None, :]
        u = h @ w_in[l]
        rg_x, rg_z, ml_x, ml_o, ml_z = jnp.split(u, split_pts, axis=-1)
        y_rg = rglru(causal_depthwise_conv(rg_x, rg_conv_w[l], rg_conv_b[l]),
                     rg_w_a[l], rg_b_a[l], rg_w_x[l], rg_b_x[l], rg_lambda[l]) * jax.nn.silu(rg_z)
        y_ml = mlstm_branch(ml_x, ml_o, ml_conv_w[l], ml_conv_b[l], ml_w_q[l], ml_w_k[l],
                            ml_w_v[l], ml_w_if[l], ml_b_if[l], ml_norm_g[l]) * jax.nn.silu(ml_z)
        y = jnp.concatenate([y_rg, y_ml], axis=-1) @ w_out[l]
        x = x + gate[:, None, :] * y
    return rms_norm(x, final_g)


def setup_inputs(seed=0):
    out = dict(first_inputs(seed))
    for name, value in second_inputs(seed + 1).items():
        if name != "x":
            out[name + "_2"] = value
    return out


def reference(
    x, p, norm_ffn1, ffn1_w1, ffn1_w3, ffn1_w2, norm_mix, w_in, cmp_pe_k, cmp_pe_v, cmp_wk1,
    cmp_wk2, cmp_wv1, cmp_wv2, s5_a_re, s5_a_im, s5_log_dt, s5_b_re, s5_b_im, s5_c_re, s5_c_im,
    s5_d, s5_w_glu, s5_b_glu, w_out, norm_ffn2, ffn2_w1, ffn2_w3, ffn2_w2, norm_ple, w_ple_gate,
    w_ple, norm_final, c_2, norm_g_2, w_ada_2, b_ada_2, w_in_2, rg_conv_w_2, rg_conv_b_2,
    rg_w_a_2, rg_b_a_2, rg_w_x_2, rg_b_x_2, rg_lambda_2, ml_conv_w_2, ml_conv_b_2, ml_w_q_2,
    ml_w_k_2, ml_w_v_2, ml_w_if_2, ml_b_if_2, ml_norm_g_2, w_out_2, final_g_2,
):
    x = first_block(
        x, p, norm_ffn1, ffn1_w1, ffn1_w3, ffn1_w2, norm_mix, w_in, cmp_pe_k, cmp_pe_v, cmp_wk1,
        cmp_wk2, cmp_wv1, cmp_wv2, s5_a_re, s5_a_im, s5_log_dt, s5_b_re, s5_b_im, s5_c_re,
        s5_c_im, s5_d, s5_w_glu, s5_b_glu, w_out, norm_ffn2, ffn2_w1, ffn2_w3, ffn2_w2,
        norm_ple, w_ple_gate, w_ple, norm_final,
    )
    return second_block(
        x, c_2, norm_g_2, w_ada_2, b_ada_2, w_in_2, rg_conv_w_2, rg_conv_b_2, rg_w_a_2,
        rg_b_a_2, rg_w_x_2, rg_b_x_2, rg_lambda_2, ml_conv_w_2, ml_conv_b_2, ml_w_q_2, ml_w_k_2,
        ml_w_v_2, ml_w_if_2, ml_b_if_2, ml_norm_g_2, w_out_2, final_g_2,
    )


_drawn_inputs = setup_inputs


def setup_inputs(seed=0):
    import zlib

    import numpy as np

    out = dict(_drawn_inputs(seed))
    spreads = {}
    factors = {'norm_ffn1': 2.755,
     'norm_mix': 3.773,
     'cmp_pe_k': 8.0,
     'cmp_pe_v': 3.057,
     's5_a_re': 64.0,
     's5_a_im': 2.874,
     's5_log_dt': 2.899,
     's5_b_re': 4.05,
     's5_b_im': 4.067,
     's5_c_re': 4.102,
     's5_c_im': 4.021,
     's5_b_glu': 8.0,
     'norm_ffn2': 3.112,
     'norm_ple': 6.803,
     'norm_g_2': 8.0,
     'rg_conv_b_2': 5.302,
     'rg_w_a_2': 2.871,
     'rg_b_a_2': 23.766,
     'rg_b_x_2': 8.0,
     'ml_conv_b_2': 8.0,
     'ml_w_if_2': 8.0,
     'ml_norm_g_2': 8.0,
     'final_g_2': 8.15}
    for name, (base, spread) in spreads.items():
        noise = np.random.default_rng([zlib.crc32(name.encode()), seed]).standard_normal(out[name].shape)
        drawn = base * np.exp(spread * noise) if base else spread * noise
        out[name] = jnp.asarray(drawn.astype(out[name].dtype))
    for name, factor in factors.items():
        out[name] = (out[name] * factor).astype(out[name].dtype)
    return out
```

```python
from contextlib import ExitStack

import numpy as np

import concourse.bass as bass
from concourse import mybir

ALU = mybir.AluOpType
ACT = mybir.ActivationFunctionType
F32 = mybir.dt.float32
AXX = mybir.AxisListType.X

P = 128
T = 512
KD = 8
NEG = -1e30
EPS = 1e-6

VEC_COLS = [
    ("norm_ffn1", 8), ("norm_mix", 8), ("norm_ffn2", 8), ("norm_ple", 8), ("norm_final", 8),
    ("a_re", 16), ("a_im", 16), ("log_dt", 16), ("s5_d", 4), ("b_glu", 4), ("pe_k", 16), ("pe_v", 16),
    ("norm_g", 16), ("b_ada", 48), ("rg_conv_w", 64), ("rg_conv_b", 16), ("rg_b_a", 16), ("rg_b_x", 16),
    ("rg_lam", 16), ("ml_conv_w", 64), ("ml_conv_b", 16), ("ml_norm_g", 16), ("final_g", 8), ("b_if", 2),
]
VEC_AT = {}
_n = 0
for _name, _w in VEC_COLS:
    VEC_AT[_name] = (_n, _w)
    _n += _w
NVEC = _n

CONST_COLS = [("cos", T), ("sin", T), ("ident", P), ("ones", P), ("rot", P), ("causal", P),
              ("cneg", 128), ("c01", 128), ("sel_i", P), ("sel_f", P)]
CONST_AT = {}
_n = 0
for _name, _w in CONST_COLS:
    CONST_AT[_name] = (_n, _w)
    _n += _w
NCONST = _n


class Queue:

    def __init__(self, sem):
        self.sem, self.n, self.ops, self.seen = sem, 0, [], {}

    def wait(self, *tokens):
        for t in tokens:
            if t is None:
                continue
            if isinstance(t, list):
                self.wait(*t)
                continue
            sem, value = t
            if self.seen.get(id(sem), 0) < value:
                self.seen[id(sem)] = value
                self.ops.append(lambda e, s=sem, v=value: e.wait_ge(s, v))

    def __call__(self, fn, *tokens, sig=True):
        self.wait(*tokens)
        if sig:
            self.n += 1
            self.ops.append(lambda e: fn(e).then_inc(self.sem, 1))
            return (self.sem, self.n)
        self.ops.append(fn)
        return None

    @property
    def last(self):
        return (self.sem, self.n)


def program(nc, D, out):
    ctx = ExitStack()
    with ctx:
        def sb(name, n):
            return ctx.enter_context(nc.sbuf_tensor(name, [P, n], F32))

        def sem(name):
            return ctx.enter_context(nc.semaphore(name))

        H = sb("H", KD * T)[:, :].rearrange("p (k t) -> p k t", t=T)
        HNf = sb("HN", KD * T)
        HN = HNf[:, :].rearrange("p (k t) -> p k t", t=T)
        TMPf = sb("TMP", 4 * T)
        TMP = TMPf[:, :].rearrange("p (k t) -> p k t", t=T)
        SQ = sb("SQ", 2 * T)[:, :].rearrange("p (k t) -> p k t", t=T)
        RS = sb("RS", 2 * T)[:, :].rearrange("p (k t) -> p k t", t=T)
        CONST = sb("CONST", NCONST)
        VEC = sb("VEC", NVEC)
        MOD = sb("MOD", 48)
        GS = sb("GS", 16)
        LA = sb("LA", 6 * 16)
        NAR = 25088
        AR = sb("AR", NAR)
        NSLOT, SLOT = 6, 2048
        RING = sb("RING", NSLOT * SLOT)
        PS = [ctx.enter_context(nc.psum_tensor(f"PS{b}", [P, T], F32)) for b in range(8)]

        def const(name):
            a, w = CONST_AT[name]
            return CONST[:, a:a + w]

        def vec(name, i=None, n=1):
            a, w = VEC_AT[name]
            return VEC[:, a:a + w] if i is None else VEC[:, a + i:a + i + n]

        COS, SIN, IDENT, ONES, ROT = (const(n) for n in ("cos", "sin", "ident", "ones", "rot"))

        pe, act, dve, pool = (Queue(sem(f"s_{n}")) for n in ("pe", "act", "dve", "pool"))
        sp = Queue(sem("s_sp"))
        s_out = sem("s_out")

        slot_sem = [sem(f"s_slot{i}") for i in range(NSLOT)]
        slot_n = [0] * NSLOT
        slot_free = [[] for _ in range(NSLOT)]
        ring_at = [0]

        def chunk(src, shape):
            s = ring_at[0] % NSLOT
            ring_at[0] += 1
            n = int(np.prod(shape))
            dst = RING[:, s * SLOT:s * SLOT + n]
            assert slot_free[s] is not None
            sp.wait(slot_free[s])
            slot_free[s] = None
            slot_n[s] += 16
            sp.ops.append(lambda e: e.dma_start(dst, src).then_inc(slot_sem[s], 16))
            view = dst
            if len(shape) == 2:
                view = dst.rearrange("p (a b) -> p a b", b=shape[1])
            if len(shape) == 3:
                view = dst.rearrange("p (a b c) -> p a b c", b=shape[1], c=shape[2])
            return view, s, (slot_sem[s], slot_n[s])

        def release(s, *tokens):
            slot_free[s] = list(tokens)

        own = [0]

        def load(dst, src, q=sp, *tokens):
            s = sem(f"s_ld{own[0]}")
            own[0] += 1
            q.wait(*tokens)
            q.ops.append(lambda e: e.dma_start(dst, src).then_inc(s, 16))
            return (s, 16)

        banks = [(b, []) for b in range(7)]
        STAT = PS[7]

        def take():
            b, tokens = banks.pop(0)
            pe.wait(*tokens)
            return b

        def give(b, *tokens):
            banks.append((b, list(tokens)))

        def mm(o, l, r, start=True, stop=True, *tokens, sig=False):
            return pe(lambda e: e.matmul(o, l, r, start=start, stop=stop, skip_group_check=True), *tokens, sig=sig)

        def tr(o, i, ident, *tokens, sig=False):
            return pe(lambda e: e.transpose(o, i, ident), *tokens, sig=sig)

        def dense(o, lhs, rhs, wtok, xtoks):
            n = len(lhs)
            t = None
            for k in range(n):
                t = mm(o, lhs[k], rhs[k], k == 0, k == n - 1, wtok if k == 0 else None, xtoks[k], sig=k == n - 1)
            return t

        def A(q, o, i, f, *tokens, **kw):
            return q(lambda e: e.activation(o, i, f, **kw), *tokens)

        def TT(q, o, a, b, op, *tokens):
            return q(lambda e: e.tensor_tensor(o, a, b, op), *tokens)

        def TS(q, o, a, s1, s2, op0, op1, *tokens):
            if op1 is None:
                return q(lambda e: e.tensor_scalar(o, a, s1, None, op0), *tokens)
            return q(lambda e: e.tensor_scalar(o, a, s1, s2, op0, op1), *tokens)

        def STT(o, a, s, b, op0, op1, *tokens):
            return dve(lambda e: e.scalar_tensor_tensor(out=o, in0=a, scalar=s, in1=b, op0=op0, op1=op1), *tokens)

        def RECIP(o, i, *tokens):
            return dve(lambda e: e.reciprocal(o, i), *tokens)

        def bc(ap, axis, shape):
            return ap.unsqueeze(axis).to_broadcast(shape)

        M_, A_, S_ = ALU.mult, ALU.add, ALU.subtract

        def everyone():
            return [pe.last, act.last, dve.last, pool.last]

        def ar(at, *shape):
            n = int(np.prod(shape))
            assert at + n <= NAR, (at, shape)
            v = AR[:, at:at + n]
            if len(shape) == 2:
                v = v.rearrange("p (a b) -> p a b", b=shape[1])
            if len(shape) == 3:
                v = v.rearrange("p (a b c) -> p a b c", b=shape[1], c=shape[2])
            return v

        t_vec = load(VEC[:, :], D["vecs"])
        t_x = load(H, D["xT"])
        t_const = load(CONST[:, :], D["consts"], act)
        HT = [t_x] * KD

        stat = {"first": True, "queue": [], "sq": [None, None], "i": 0, "free": []}

        def stat_square(src, tok):
            i = stat["i"] % 2
            stat["i"] += 1
            t = A(act, SQ[:, i, :], src, ACT.Square, tok, stat["sq"][i])
            stat["queue"].append((i, t))

        def stat_flush(upto=0, n=KD):
            while len(stat["queue"]) > upto:
                i, t = stat["queue"].pop(0)
                c = stat.setdefault("c", 0)
                tok = mm(STAT[:, :], ONES, SQ[:, i, :], c == 0, c == n - 1, t, t_const,
                         stat["free"] if c == 0 else None, sig=True)
                stat["sq"][i] = tok
                stat["c"] = (c + 1) % n
                stat["tok"] = tok

        def rstd(dst, src, n, *tokens):
            t = TS(dve, dst, src, 1.0 / n, EPS, M_, A_, *tokens)
            back = t
            t = A(act, dst, dst, ACT.Sqrt, t)
            return RECIP(dst, dst, t), back

        rs_readers = [[]]

        def norm(gain, dst, waits, shift=None):
            t, back = rstd(RS[:, 0, :], STAT[:, :], 1024.0, stat["tok"], rs_readers[0])
            stat["free"] = [back]
            toks = []
            for k in range(KD):
                t2 = STT(dst[:, k, :], H[:, k, :], gain(k), RS[:, 0, :], M_, M_, t, t_vec, HT[k], waits)
                if shift is not None:
                    t2 = A(act, dst[:, k, :], dst[:, k, :], ACT.Identity, t2, bias=shift(k))
                toks.append(t2)
            rs_readers[0] = [dve.last]
            return toks

        CB = ar(20480, 1024)
        JUNK = ar(21504, 1024)
        t_c = load(CB, D["c"].partition_broadcast(P), act)
        t_cs = A(act, JUNK, CB, ACT.Sigmoid, t_c)
        t_cs = TT(dve, CB, CB, JUNK, M_, t_cs)
        ada_at = [0]

        def ada(n):
            for _ in range(n):
                c = ada_at[0]
                if c >= 24:
                    return
                ada_at[0] += 1
                w, s, wt = chunk(D["w_ada"][c], (2, 1024))
                for j in range(2):
                    t = dve(lambda e, j=j, c=c, w=w: e.tensor_tensor_reduce(
                        out=JUNK, in0=w[:, j, :], in1=CB, scale=1.0, scalar=0.0, op0=M_, op1=A_,
                        accum_out=MOD[:, 2 * c + j:2 * c + j + 1]), wt, t_cs, dve.last)
                release(s, t)

        HID = ar(12288, 11, T)
        tmp_free = [[], [], [], []]

        def ffn(w13, w2, hnt, side=lambda: None):
            hid_free = [[]] * 11
            for half in range(2):
                hidt = []
                for mi in range(11):
                    w, s, wt = chunk(D[w13][half * 11 + mi], (2, 8, P))
                    side()
                    bA, = (take(),)
                    tA = dense(PS[bA][:, :], [w[:, 0, k, :] for k in range(8)], [HN[:, k, :] for k in range(8)], wt, hnt)
                    bB = take()
                    tB = dense(PS[bB][:, :], [w[:, 1, k, :] for k in range(8)], [HN[:, k, :] for k in range(8)], wt, hnt)
                    release(s, tB)
                    q = mi % 2
                    a = A(act, TMP[:, q, :], PS[bA][:, :], ACT.Silu, tA, tmp_free[q])
                    give(bA, a)
                    d = TT(dve, HID[:, mi, :], TMP[:, q, :], PS[bB][:, :], M_, a, tB, hid_free[mi])
                    tmp_free[q] = [d]
                    give(bB, d)
                    hidt.append(d)
                for m in range(KD):
                    w, s, wt = chunk(D[w2][half * 8 + m], (11, P))
                    b = take()
                    t = dense(PS[b][:, :], [w[:, k, :] for k in range(11)], [HID[:, k, :] for k in range(11)], wt, hidt)
                    release(s, t)
                    HT[m] = STT(H[:, m, :], PS[b][:, :], 0.5, H[:, m, :], M_, A_, t, HT[m])
                    give(b, HT[m])
                    if half:
                        stat_flush()
                        stat_square(H[:, m, :], HT[m])
                hid_free = [[t]] * 11
            stat_flush()
            return t

        TC, TSN = ar(0, 16, P), ar(2048, 16, P)
        SBr, SBi = ar(4096, 4, P), ar(4608, 4, P)
        CR, CI = ar(5120, 16, 32), ar(5632, 16, 32)
        CpR, CpI = ar(6144, 16, 32), ar(6656, 16, 32)
        U = ar(7168, 4, T)
        SMALL = AR[:, 22528:22528 + 512]
        RHO = AR[:, 23040:23056]
        t_sb = load(AR[:, 4096:6144], D["s5_bc"], act)

        def sm(i):
            return SMALL[:, 16 * i:16 * i + 16]

        def s5_params():
            dt, x, th, k, r, cs, sn, t1, t2, arr, aii, br, bi, den = (sm(i) for i in range(14))
            lr, li = vec("a_re"), vec("a_im")
            t = A(act, dt, vec("log_dt"), ACT.Exp, t_vec)
            t = TT(dve, x, lr, dt, M_, t)
            t_rho = A(act, RHO, x, ACT.Exp, t)
            t = TT(dve, th, li, dt, M_, dve.last)
            magic = 1.5 * 2.0 ** 23
            t = TS(dve, k, th, float(1 / (2 * np.pi)), None, M_, None, t)
            t = TS(dve, k, k, magic, None, A_, None, t)
            t = TS(dve, k, k, magic, None, S_, None, t)
            c1 = 6.28125
            c2 = float(np.float32(2 * np.pi - c1))
            c2 = float(np.frombuffer((np.frombuffer(np.float32(c2).tobytes(), np.uint32) & np.uint32(0xFFFFE000)).tobytes(), np.float32)[0])
            c3 = float(2 * np.pi - c1 - c2)
            t = STT(r, k, -c1, th, M_, A_, t)
            t = STT(r, k, -c2, r, M_, A_, t)
            t = STT(r, k, -c3, r, M_, A_, t)
            t = TS(dve, r, r, 3.1415925, -3.1415925, ALU.min, ALU.max, t)
            t_s = A(act, sn, r, ACT.Sin, t)
            t = A(act, t1, r, ACT.Abs, t)
            t = TS(dve, t1, t1, -1.0, float(np.pi / 2), M_, A_, t)
            t = A(act, cs, t1, ACT.Sin, t)
            t = TT(dve, arr, RHO, cs, M_, t, t_rho)
            t = TT(dve, aii, RHO, sn, M_, t_s, t)
            t = TS(dve, arr, arr, -1.0, None, A_, None, t)
            t = TT(dve, t1, lr, lr, M_, t)
            t = TT(dve, t2, li, li, M_, t)
            t = TT(dve, den, t1, t2, A_, t)
            t = RECIP(den, den, t)
            t = TT(dve, t1, arr, lr, M_, t)
            t = TT(dve, t2, aii, li, M_, t)
            t = TT(dve, br, t1, t2, A_, t)
            t = TT(dve, br, br, den, M_, t)
            t = TT(dve, t1, aii, lr, M_, t)
            t = TT(dve, t2, arr, li, M_, t)
            t = TT(dve, bi, t1, t2, S_, t)
            t = TT(dve, bi, bi, den, M_, t)
            b3 = [P, 16, 32]
            w1 = TMPf[:, 1024:1536].rearrange("p (a b) -> p a b", b=32)
            w2 = TMPf[:, 1536:2048].rearrange("p (a b) -> p a b", b=32)
            t = TT(dve, w1, CR, bc(br, 2, b3), M_, t, t_sb)
            t = TT(dve, w2, CI, bc(bi, 2, b3), M_, t)
            t = TT(dve, CpR, w1, w2, S_, t)
            t = TT(dve, w1, CR, bc(bi, 2, b3), M_, t)
            t = TT(dve, w2, CI, bc(br, 2, b3), M_, t)
            t = TT(dve, CpI, w1, w2, A_, t)
            t = TS(dve, CpI, CpI, -1.0, None, M_, None, t)
            t = dve(lambda e: e.tensor_copy(TC[:, :, 0:1], cs.unsqueeze(2)), t)
            t = dve(lambda e: e.tensor_copy(TSN[:, :, 0:1], sn.unsqueeze(2)), t)
            d = 1
            while d < P:
                sh = [P, 16, d]
                v1 = TMPf[:, 0:16 * d].rearrange("p (a b) -> p a b", b=d)
                v2 = TMPf[:, 1024:1024 + 16 * d].rearrange("p (a b) -> p a b", b=d)
                c0, s0, c1_, s1_ = TC[:, :, 0:d], TSN[:, :, 0:d], TC[:, :, d - 1:d], TSN[:, :, d - 1:d]
                cw, sw = c1_.to_broadcast(sh), s1_.to_broadcast(sh)
                for o, (x1, x2), op in ((TC, (cw, sw), S_), (TSN, (sw, cw), A_)):
                    t = TT(dve, v1, c0, x1, M_, t)
                    t = TT(dve, v2, s0, x2, M_, t)
                    t = TT(dve, o[:, :, d:2 * d], v1, v2, op, t)
                d *= 2
            return t

        t_s5 = s5_params()
        tmp_free = [[t_s5] for _ in range(4)]

        def softplus_neg(dst, x):
            y, z, z2, acc, t1 = (LA[:, 16 * i:16 * i + 16] for i in range(5))
            t = A(act, y, x, ACT.Abs, t_vec, dve.last)
            t = A(act, y, y, ACT.Exp, t, scale=-1.0)
            t = TS(dve, z, y, 2.0, None, A_, None, t)
            t = RECIP(z, z, t)
            t = TT(dve, z, z, y, M_, t)
            t = TT(dve, z2, z, z, M_, t)
            t = TS(dve, acc, z2, 1.0 / 19, 1.0 / 17, M_, A_, t)
            for n in (15, 13, 11, 9, 7, 5, 3, 1):
                t = TT(dve, acc, acc, z2, M_, t)
                t = TS(dve, acc, acc, 1.0 / n, None, A_, None, t)
            t = TT(dve, acc, acc, z, M_, t)
            t = TS(dve, t1, x, -1.0, 0.0, M_, ALU.max, t)
            return STT(dst, acc, 2.0, t1, M_, A_, t)

        CA = LA[:, 80:96]
        t_ca = softplus_neg(CA, vec("rg_lam"))
        t_ca = TS(dve, CA, CA, -8.0, None, M_, None, t_ca)

        for k in range(KD):
            stat_square(H[:, k, :], HT[k])
            stat_flush()
        hnt = norm(lambda k: vec("norm_ffn1", k), HN, None)
        t_ffn = ffn("w13a", "w2a", hnt, side=lambda: ada(1))
        ada(24)
        hnt = norm(lambda k: vec("norm_mix", k), HN, pe.last)
        t_pre = everyone()

        V_ = ar(9216, 2, 4, T)
        S5T = ar(13312, 2, T)
        Q = ar(14336, 4, T)
        KC, KSL, KW, VCT = (AR[:, 16384 + T * i:16384 + T * (i + 1)] for i in range(4))
        VT = ar(18432, 4, 256)
        PB = ar(19456, 4, T)
        CE = ar(21504, 4, 8, )if False else AR[:, 21504:22528].rearrange("p (a b c) -> p a b c", b=8, c=32)
        PTC = AR[:, 23168:24192].rearrange("p (a b) -> p a b", b=T)
        GT = AR[:, 22528:22624].rearrange("p (a b) -> p a b", b=24)
        GX = AR[:, 24192:24288].rearrange("p (a b) -> p a b", b=24)
        CM, CS = AR[:, 22624:22656], AR[:, 22656:22688]
        HIDc = AR[:, 22688:22816].rearrange("p (a b) -> p a b", b=64)
        KCC = AR[:, 22816:22880]
        VC = AR[:, 22880:23008]
        ST4 = AR[:, 23056:23168].rearrange("p (a b) -> p a b", b=4)
        WG = AR[:, 24288:24480].rearrange("p (a b) -> p a b", b=24)
        WK2 = AR[:, 24480:24736].rearrange("p (a b) -> p a b", b=128)
        WV2 = AR[:, 24736:24864].rearrange("p (a b) -> p a b", b=64)
        PT = HNf[:, :].rearrange("p (h k t) -> p h k t", h=2, k=4)
        t_wg = load(AR[:, 24288:24864], D["small_w"], act, t_pre)

        def w_in_tiles():
            for c in range(6):
                w, s, wt = chunk(D["w_inA"][c], (8, 256))
                for j in range(2):
                    b = take()
                    t = dense(PS[b][:, :], [w[:, k, P * j:P * j + P] for k in range(8)], [HN[:, k, :] for k in range(8)], wt, hnt)
                    if j:
                        release(s, t)
                    yield b, t

        tiles = w_in_tiles()
        ut = []
        for m in range(4):
            b, t = next(tiles)
            a = A(act, U[:, m, :], PS[b][:, :], ACT.Copy, t, t_pre)
            give(b, a)
            ut.append(a)

        ot = [None] * 8

        def s5():
            vfree = []
            s5t_free = [[], []]
            for y4 in range(4):
                vt = []
                for j in range(4):
                    t16 = 4 * y4 + j
                    rows = slice(32 * j, 32 * j + 32)
                    bR = take()
                    tR = mm(PS[bR][:, :], SBr[rows, y4, :], U[rows, y4, :], True, True, ut[y4], t_sb, sig=True)
                    bI = take()
                    tI = mm(PS[bI][:, :], SBi[rows, y4, :], U[rows, y4, :], True, True, sig=True)
                    vr, vi = V_[:, 0, j, :], V_[:, 1, j, :]
                    sh = [P, 4, P]
                    c4, s4 = bc(TC[:, t16, :], 1, sh), bc(TSN[:, t16, :], 1, sh)

                    def f4(x):
                        return x.rearrange("p (c t) -> p c t", t=P)
                    t1, t2 = S5T[:, 0, :], S5T[:, 1, :]
                    d1 = TT(dve, f4(vr), f4(PS[bR][:, :]), c4, M_, tR, vfree, t_s5, t_pre)
                    d2 = TT(dve, f4(t1), f4(PS[bI][:, :]), s4, M_, tI, s5t_free[0])
                    d3 = TT(dve, f4(vi), f4(PS[bI][:, :]), c4, M_, vfree)
                    d4 = TT(dve, f4(t2), f4(PS[bR][:, :]), s4, M_, s5t_free[1])
                    give(bR, d4)
                    give(bI, d3)
                    e1 = TT(dve, vr, vr, t1, A_, d1, d2)
                    e2 = TT(dve, vi, vi, t2, S_, d3, d4)
                    s5t_free = [[e1], [e2]]
                    vt.append((e1, e2))
                    yield
                init = [[0.0] * 4, [0.0] * 4]
                it = None
                E1, E2 = AR[:, 24864:24872].rearrange("p (a b) -> p a b", b=4), AR[:, 24872:24880].rearrange("p (a b) -> p a b", b=4)
                E3 = AR[:, 24880:24888].rearrange("p (a b) -> p a b", b=4)
                sc = None
                for c in range(4):
                    cols = slice(P * c, P * c + P)
                    for j in range(4):
                        rho = RHO[:, 4 * y4 + j:4 * y4 + j + 1].to_broadcast([P, P])
                        for z in range(2):
                            ini = 0.0 if c == 0 else E3[:, z, j:j + 1]
                            sc = dve(lambda e, z=z, j=j, rho=rho, ini=ini, cols=cols: e.tensor_tensor_scan(
                                out=V_[:, z, j, cols], data0=rho, data1=V_[:, z, j, cols], initial=ini, op0=M_, op1=A_),
                                vt[j][z], it)
                    if c < 3:
                        lr_, li_ = V_[:, 0, :, P * c + P - 1], V_[:, 1, :, P * c + P - 1]
                        ce, se = TC[:, 4 * y4:4 * y4 + 4, P - 1], TSN[:, 4 * y4:4 * y4 + 4, P - 1]
                        TT(dve, E1[:, 0, :], lr_, ce, M_, sc)
                        TT(dve, E1[:, 1, :], lr_, se, M_)
                        TT(dve, E2[:, 0, :], li_, se, M_)
                        t = TT(dve, E2[:, 1, :], li_, ce, M_)
                        TT(dve, E3[:, 0, :], E1[:, 0, :], E2[:, 0, :], S_, t)
                        it = TT(dve, E3[:, 1, :], E1[:, 1, :], E2[:, 1, :], A_)
                    yield
                bY = None
                for j in range(4):
                    t16 = 4 * y4 + j
                    vr, vi = V_[:, 0, j, :], V_[:, 1, j, :]
                    c4, s4 = bc(TC[:, t16, :], 1, [P, 4, P]), bc(TSN[:, t16, :], 1, [P, 4, P])
                    t1, t2 = S5T[:, 0, :], S5T[:, 1, :]
                    d1 = TT(pool, f4(t1), f4(vr), s4, M_, sc, s5t_free[0])
                    d2 = TT(dve, f4(t2), f4(vi), s4, M_, sc, s5t_free[1])
                    d3 = TT(dve, f4(vr), f4(vr), c4, M_, d1)
                    d4 = TT(dve, f4(vi), f4(vi), c4, M_, d2)
                    e1 = TT(dve, vr, vr, t2, S_, d3)
                    e2 = TT(dve, vi, vi, t1, A_, d4)
                    s5t_free = [[e2], [e1]]
                    yield
                    if j == 0:
                        bY = take()
                    o = PS[bY][32 * j:32 * j + 32, :]
                    mm(o, CpR[:, t16, :], vr, True, False, e1)
                    tY = mm(o, CpI[:, t16, :], vi, False, True, e2, sig=True)
                vfree = [tY]
                g = STT(U[:, y4, :], U[:, y4, :], vec("s5_d", y4), PS[bY][:, :], M_, A_, tY)
                give(bY, g)
                ot[4 + y4] = g
                yield

        s5g = s5()

        def s5_step(n=1):
            for _ in range(n):
                next(s5g, None)

        def rope(b, t, dst, scale, q):
            a = A(act, TMP[:, q, :], PS[b][:, :], ACT.Copy, t, tmp_free[q], scale=scale)
            give(b, a)
            b2 = take()
            t2 = mm(PS[b2][:, :], ROT, TMP[:, q, :], True, True, a, t_const, sig=True)
            p1 = TT(pool, dst, TMP[:, q, :], COS, M_, a, t_pre)
            d = TT(dve, TMP[:, q, :], PS[b2][:, :], SIN, M_, t2, p1)
            give(b2, d)
            d2 = TT(pool, dst, dst, TMP[:, q, :], A_, d)
            tmp_free[q] = [d2]
            return d2

        s5_step(2)
        qt_, kt = [], {}
        names = [("q", 0), ("q", 1), ("q", 2), ("q", 3), ("kc", KC), ("ksl", KSL), ("kw", KW), ("vc", VCT)]
        pend = None
        for i, (nm, dst) in enumerate(names):
            b, t = next(tiles)
            if pend is not None:
                pend()
            s5_step(2)
            if nm == "vc":
                a = A(act, VCT, PS[b][:, :], ACT.Copy, t, t_pre)
                give(b, a)
                kt["vc"] = a
                pend = None
            elif nm == "q":
                def pend(b=b, t=t, m=dst, i=i):
                    qt_.append(rope(b, t, Q[:, m, :], 0.125, i % 4))
            else:
                def pend(b=b, t=t, d=dst, nm=nm, i=i):
                    kt[nm] = rope(b, t, d, 1.0, i % 4)
        w, s, wt = chunk(D["w_inV"], (8, 256))
        vtt = []
        for tt in range(4):
            b = take()
            for k in range(8):
                l = HN[:, k, P * tt:P * tt + P]
                mm(PS[b][:, 0:256], l, w[:, k, :], k == 0, k == 7, wt, hnt[k])
            for k in range(8):
                l = HN[:, k, P * tt:P * tt + P]
                t = mm(PS[b][:, 256:280], l, WG[:, k, :], k == 0, k == 7, t_wg, sig=k == 7)
            a = A(act, VT[:, tt, :], PS[b][:, 0:256], ACT.Copy, t, t_pre)
            a2 = A(act, GX[:, tt, :], PS[b][:, 256:280], ACT.Copy, t, t_pre)
            give(b, a2)
            vtt.append(a)
            s5_step(2)
        release(s, t)
        t_z = t
        gt = A(act, GT, GX, ACT.Sigmoid, a2)

        XAB = PB.rearrange("p a t -> p (a t)")
        XB = {}
        XAp = AR[:, 19456:20480].rearrange("p (g t) -> p g t", t=T)
        XBp = HNf[:, 0:992 * 2].rearrange("p (s i g c) -> p s i g c", s=2, i=16, g=2)
        xa_free = None
        hid_free = None
        kc_t = vc_t = None
        for z, (src, tok, pe_name, wname) in enumerate((("kc", kt["kc"], "pe_k", "wk1"), ("vc", kt["vc"], "pe_v", "wv1"))):
            srct = KC if z == 0 else VCT
            lt = []
            for g in range(2):
                lt.append(load(XAp[0:64, g, :], srct[64 * g:64 * g + 64, :], act, tok, xa_free, t_pre))
                lt.append(load(XAp[64:128, g, 0:T - 1], srct[64 * g:64 * g + 64, 1:T], act))
            for g in range(2):
                for a_ in range(2):
                    v = XAp[:, g, :].rearrange("p (c r two) -> p r c two", r=8, two=2)[:, :, a_:a_ + 31, 0]
                    xa_free = TT(dve, XBp[:, z, 8 * a_:8 * a_ + 8, g, :], v,
                                 bc(vec(pe_name, 8 * a_, 8), 2, [P, 8, 31]), A_, lt, t_z)
            s5_step(2)
            bs = [take(), take()]
            for c in range(2):
                w, s, wt = chunk(D[wname][c], (8, 256))
                for mt in range(2):
                    for i in range(8):
                        ii = 8 * c + i
                        t = mm(PS[bs[mt]][:, 0:62], w[:, i, P * mt:P * mt + P],
                               XBp[:, z, ii, :, :].rearrange("p g c -> p (g c)"), ii == 0, ii == 15, wt, xa_free, sig=i == 7)
                release(s, t)
            for mt in range(2):
                hc = A(act, HIDc[:, mt, 0:62], PS[bs[mt]][:, 0:62], ACT.Gelu_apprx_tanh, t, hid_free, t_pre)
                give(bs[mt], hc)
            b = take()
            if z == 0:
                for mt in range(2):
                    t = mm(PS[b][:, 0:62], WK2[:, mt, :], HIDc[:, mt, 0:62], mt == 0, mt == 1, hc, t_wg, sig=mt == 1)
                kc_t = A(act, KCC[:, 0:62], PS[b][:, 0:62], ACT.Copy, t, t_pre)
                give(b, kc_t)
            else:
                for g in range(2):
                    for mt in range(2):
                        t = mm(PS[b][0:31, 64 * g:64 * g + 64], HIDc[:, mt, 31 * g:31 * g + 31], WV2[:, mt, :],
                               mt == 0, mt == 1, hc, t_wg, sig=mt == 1)
                vc_t = A(act, VC[0:31, :], PS[b][0:31, 0:128], ACT.Copy, t, t_pre)
                give(b, vc_t)
            hid_free = t
            s5_step(2)

        cneg = const("cneg").rearrange("p (q c) -> p q c", c=32)
        c01 = const("c01").rearrange("p (q c) -> p q c", c=32)
        cet = []
        for qt in range(4):
            ce = CE[:, qt, :, :].rearrange("p (i f) c -> p f i c", f=2)
            for hf in range(2):
                b = take()
                r = slice(64 * hf, 64 * hf + 64)
                for i in range(4):
                    t = mm(PS[b][:, 32 * i:32 * i + 31], Q[r, i, P * qt:P * qt + P], KCC[r, 31 * hf:31 * hf + 31],
                           True, True, qt_[i], kc_t, sig=i == 3)
                v = PS[b][:, 0:128].rearrange("p (h c) -> p h c", c=32)[:, :, 0:31]
                d = TT(dve, ce[:, hf, :, 0:31], v, bc(cneg[:, qt, 0:31], 1, [P, 4, 31]), A_, t, t_pre)
                give(b, d)
        CEa = AR[:, 21504:22528].rearrange("p (a c) -> p a c", c=32)[:, :, 0:31]
        sh = [P, 32, 31]
        t = dve(lambda e: e.tensor_reduce(CM, CEa, AXX, ALU.max), d)
        t = TT(dve, CEa, CEa, bc(CM, 2, sh), S_, t)
        t = A(act, CEa, CEa, ACT.Exp, t)
        for qt in range(4):
            t2 = TT(dve, CE[:, qt, :, 0:31], CE[:, qt, :, 0:31], bc(c01[:, qt, 0:31], 1, [P, 8, 31]), M_, t)
        t = dve(lambda e: e.tensor_reduce(CS, CEa, AXX, A_), t2)
        t = TS(dve, CS, CS, 1e-30, None, ALU.max, None, t)
        t = RECIP(CS, CS, t)
        CS4 = CS.rearrange("p (q h) -> p q h", h=8)
        t = TT(dve, CS4, CS4, GT[:, :, 0:8], M_, t, gt)
        ce_t = TT(dve, CEa, CEa, bc(CS, 2, sh), M_, t)
        s5_step(2)

        xb_done = pe.last
        pt_free = [[xb_done], [xb_done]]
        ptc_free = [None, None]
        p_free = [[t_pre, xa_free] for _ in range(4)]
        unit = [0]
        for i in range(4):
            for hf in range(2):
                b = take()
                for qt in range(4):
                    t = tr(PS[b][0:31, P * qt:P * qt + P], CE[:, qt, 2 * i + hf, 0:31], IDENT, ce_t, t_const, sig=qt == 3)
                a = A(act, PTC[0:31, hf, :], PS[b][0:31, :], ACT.Copy, t, ptc_free[hf], t_pre)
                give(b, a)
                if hf == 0:
                    a0 = a
            bO = take()
            for hf in range(2):
                ptc_free[hf] = mm(PS[bO][64 * hf:64 * hf + 64, :], VC[0:31, 64 * hf:64 * hf + 64], PTC[0:31, hf, :],
                                  True, False, a, a0, vc_t, sig=True)
            work = [(kind, qt, hf) for kind in (1, 2) for qt in range(4) for hf in range(2)]
            ptt = {}
            stage = []

            def scores(kind, qt, hf):
                nk = P * (qt + 1)
                r = slice(64 * hf, 64 * hf + 64)
                K_ = KSL if kind == 1 else KW
                b = take()
                t = mm(PS[b][:, 0:nk], Q[r, i, P * qt:P * qt + P], K_[r, 0:nk], True, True,
                       kt["ksl"], kt["kw"], qt_[i], sig=True)
                u = unit[0] % 4
                unit[0] += 1
                st = ST4[:, u, :]
                d = TT(dve, PS[b][:, nk - P:nk], PS[b][:, nk - P:nk], const("causal"), A_, t)
                d = dve(lambda e: e.tensor_reduce(st[:, 0:1], PS[b][:, 0:nk], AXX, ALU.max, negate=True), d, p_free[u])
                a = A(act, PB[:, u, 0:nk], PS[b][:, 0:nk], ACT.Exp, d, p_free[u], bias=st[:, 0:1], accum_out=st[:, 1:2])
                give(b, a)
                d = RECIP(st[:, 2:3], st[:, 1:2], a)
                d = TT(dve, st[:, 3:4], st[:, 2:3], GT[:, qt, 8 * kind + 2 * i + hf:8 * kind + 2 * i + hf + 1], M_, d, gt)
                return u, TS(dve, PB[:, u, 0:nk], PB[:, u, 0:nk], st[:, 3:4], None, M_, None, d)

            def flip(kind, qt, hf, u, tok):
                b = take()
                for kb in range(qt + 1):
                    t = tr(PS[b][:, P * kb:P * kb + P], PB[:, u, P * kb:P * kb + P], IDENT, tok, sig=kb == qt)
                p_free[u] = [t]
                a = A(act, PT[:, hf, 0:qt + 1, P * qt:P * qt + P],
                      PS[b][:, 0:P * (qt + 1)].rearrange("p (k t) -> p k t", t=P), ACT.Copy, t, pt_free[hf])
                give(b, a)
                ptt[hf] = a
                if qt == 3:
                    for kb in range(4):
                        t = mm(PS[bO][64 * hf:64 * hf + 64, P * kb:T], VT[:, kb, P * (kind - 1) + 64 * hf:P * (kind - 1) + 64 * hf + 64],
                               PT[:, hf, kb, P * kb:T], False, kind == 2 and kb == 3, a, vtt[kb], sig=kb == 3)
                    pt_free[hf] = [t]
                    return t

            for x in work:
                stage.append(x + scores(*x))
                if len(stage) > 2:
                    flip(*stage.pop(0))
                if x[2]:
                    s5_step()
            while stage:
                t = flip(*stage.pop(0))
            ot[i] = A(act, Q[:, i, :], PS[bO][:, :], ACT.Copy, t, pt_free[0], pt_free[1])
            give(bO, ot[i])
        s5_step(100)

        for m in range(4):
            ot[4 + m] = A(act, U[:, m, :], U[:, m, :], ACT.Gelu_apprx_tanh, ot[4 + m])
        w, s, wt = chunk(D["w_glu"], (4, T))
        sg = []
        for m in range(4):
            b = take()
            t = dense(PS[b][:, :], [w[:, k, P * m:P * m + P] for k in range(4)], [U[:, k, :] for k in range(4)], wt, ot[4:8])
            a = A(act, TMP[:, m, :], PS[b][:, :], ACT.Sigmoid, t, tmp_free[m], bias=vec("b_glu", m))
            give(b, a)
            sg.append(a)
        release(s, t)
        for m in range(4):
            ot[4 + m] = TT(dve, U[:, m, :], U[:, m, :], TMP[:, m, :], M_, sg[m], t)
            tmp_free[m] = [ot[4 + m]]

        def residual(wname, shape, rhs, toks, gate=None, per=2):
            nk = len(rhs)
            for c in range(KD // per):
                w, s, wt = chunk(D[wname][c], shape)
                for j in range(per):
                    m = per * c + j
                    b = take()
                    t = dense(PS[b][:, :], [w[:, k, P * j:P * j + P] for k in range(nk)], rhs, wt, toks)
                    if j == per - 1:
                        release(s, t)
                    if gate is None:
                        HT[m] = TT(dve, H[:, m, :], PS[b][:, :], H[:, m, :], A_, t, HT[m])
                    else:
                        HT[m] = STT(H[:, m, :], PS[b][:, :], gate(m), H[:, m, :], M_, A_, t, HT[m])
                    give(b, HT[m])
                    stat_flush()
                    stat_square(H[:, m, :], HT[m])
            stat_flush()

        residual("w_out", (8, 256), [Q[:, i, :] for i in range(4)] + [U[:, i, :] for i in range(4)], ot)
        hnt = norm(lambda k: vec("norm_ffn2", k), HN, pe.last)
        ffn("w13b", "w2b", hnt)

        hnt = norm(lambda k: vec("norm_ple", k), HN, pe.last)
        PT_ = ar(0, 2, T)
        t_p = load(PT_, D["pT"], act, everyone())
        wp, sp_, wpt = chunk(D["w_ple"], (2, 1024))
        for c in range(4):
            w, s, wt = chunk(D["w_pg"][c], (8, 256))
            for j in range(2):
                m = 2 * c + j
                b2 = take()
                t2 = dense(PS[b2][:, :], [wp[:, k, P * m:P * m + P] for k in range(2)], [PT_[:, k, :] for k in range(2)], wpt, [t_p] * 2)
                b = take()
                t = dense(PS[b][:, :], [w[:, k, P * j:P * j + P] for k in range(8)], [HN[:, k, :] for k in range(8)], wt, hnt)
                if j:
                    release(s, t)
                q = m % 4
                a = A(act, TMP[:, q, :], PS[b][:, :], ACT.Sigmoid, t, tmp_free[q])
                give(b, a)
                d = TT(dve, TMP[:, q, :], PS[b2][:, :], TMP[:, q, :], M_, a, t2)
                give(b2, d)
                HT[m] = TT(dve, H[:, m, :], H[:, m, :], TMP[:, q, :], A_, d, HT[m])
                tmp_free[q] = [HT[m]]
                stat_flush()
                stat_square(H[:, m, :], HT[m])
        release(sp_, t2)
        stat_flush()
        HT = norm(lambda k: vec("norm_final", k), H, None)
        for k in range(KD):
            stat_square(H[:, k, :], HT[k])
            stat_flush()

        t = TT(dve, MOD[:, :], MOD[:, :], vec("b_ada"), A_, dve.last)
        for l in range(2):
            t = TS(dve, GS[:, 8 * l:8 * l + 8], MOD[:, 24 * l + 8:24 * l + 16], 1.0, None, A_, None, t)
            t = TT(dve, GS[:, 8 * l:8 * l + 8], GS[:, 8 * l:8 * l + 8], vec("norm_g", 8 * l, 8), M_, t)
        t_mod = t

        for l in range(2):
            hnt = norm(lambda k: GS[:, 8 * l + k:8 * l + k + 1], HN, [pe.last, t_mod],
                       shift=lambda k: MOD[:, 24 * l + k:24 * l + k + 1])
            start = everyone()
            Y = ar(0, 8, T)
            XM = ar(4096, 8, 515)
            XC = ar(8224, 8, T)
            Q2 = ar(12320, 8, T)
            K2 = ar(16416, 8, T)
            V2 = ar(20512, 4, 1024)
            YM = AR[:, 4096:8192].rearrange("p (a b) -> p a b", b=T)
            G_ = AR[:, 24608:24608 + 320]
            WIF = AR[:, 24608:24800].rearrange("p (a b) -> p a b", b=8)
            GV = AR[:, 24800:24864].rearrange("p (a b) -> p a b", b=8)
            ET = AR[:, 24864:24880].rearrange("p (a b) -> p a b", b=4)
            t_wif = load(AR[:, 24608:24800], D["w_if"][l], act, start)

            def cols(c):
                return chunk(D["w_in2"][20 * l + c], (8, 256))

            def proj(w, wt, j):
                b = take()
                return b, dense(PS[b][:, :], [w[:, k, P * j:P * j + P] for k in range(8)], [HN[:, k, :] for k in range(8)], wt, hnt)

            t_pad = pool(lambda e: e.memset(XM[:, :, 0:3], 0.0), start)

            def conv(dst, x, kind, m, *tokens):
                cw = lambda i: vec(kind + "_conv_w", 32 * l + 8 * i + m)
                t = TS(dve, dst, x[:, 3:3 + T], cw(3), vec(kind + "_conv_b", 8 * l + m), M_, A_, *tokens)
                for i in range(3):
                    t = STT(dst, x[:, i:i + T], cw(i), dst, M_, A_, t)
                return t

            RX = Q2
            IX = K2
            CX = V2.rearrange("p a b -> p (a b)").rearrange("p (a b) -> p a b", b=T)
            XP = [XC[:, 0:2, :].rearrange("p a b -> p (a b)")[:, 0:515], XC[:, 2:4, :].rearrange("p a b -> p (a b)")[:, 0:515]]
            for x in XP:
                t_xp = pool(lambda e, x=x: e.memset(x[:, 0:3], 0.0), start)
            wax_f = XC[:, 4:8, :].rearrange("p a b -> p (a b)")
            wax_t = load(wax_f, D["rg_w"][l], act, start)
            wax = wax_f.rearrange("p (z h d) -> p z h d", z=2, h=8)
            xp_free = [[], []]
            rt, itk, ct, yt = [], [], [], []
            pend = []

            def gates(hh, c):
                for z, (dst, bn, lst) in enumerate(((RX, "rg_b_a", rt), (IX, "rg_b_x", itk))):
                    b = take()
                    t = mm(PS[b][:, :], wax[:, z, hh, :], CX[:, hh, :], True, True, c, wax_t, sig=True)
                    a = A(act, dst[:, hh, :], PS[b][:, :], ACT.Sigmoid, t, start, bias=vec(bn, 8 * l + hh))
                    give(b, a)
                    lst.append(a)
                return t

            for c in range(4):
                w, s, wt = cols(c)
                for j in range(2):
                    hh = 2 * c + j
                    b, t = proj(w, wt, j)
                    x = XP[hh % 2]
                    a = A(act, x[:, 3:515], PS[b][:, :], ACT.Copy, t, t_xp, xp_free[hh % 2], start)
                    give(b, a)
                    d = conv(CX[:, hh, :], x, "rg", hh, a, start)
                    xp_free[hh % 2] = [d]
                    ct.append(d)
                    pend.append((hh, d))
                    if len(pend) > 1:
                        gates(*pend.pop(0))
                release(s, t)
                w, s, wt = cols(4 + c)
                for j in range(2):
                    hh = 2 * c + j
                    b, t = proj(w, wt, j)
                    a = A(act, Y[:, hh, :], PS[b][:, :], ACT.Sigmoid, t, start)
                    d = TT(dve, Y[:, hh, :], Y[:, hh, :], PS[b][:, :], M_, a)
                    give(b, d)
                    yt.append(d)
                release(s, t)
            t_g = gates(*pend.pop(0))

            xmt, xct = [], []
            sig_free = [[], []]
            for c in range(4):
                w, s, wt = cols(8 + c)
                for j in range(2):
                    m = 2 * c + j
                    b, t = proj(w, wt, j)
                    a = A(act, XM[:, m, 3:515], PS[b][:, :], ACT.Copy, t, t_pad, start)
                    give(b, a)
                    xmt.append(a)
                    d = conv(XC[:, m, :], XM[:, m, :], "ml", m, a, xp_free, t_g)
                    q = m % 2
                    a2 = A(act, TMP[:, q, :], XC[:, m, :], ACT.Sigmoid, d, tmp_free[q])
                    tmp_free[q] = [TT(pool, XC[:, m, :], XC[:, m, :], TMP[:, q, :], M_, a2)]
                    xct.append(tmp_free[q][0])
                release(s, t)
            rg_done = []
            ax = []
            for hh in range(8):
                ca = CA[:, 8 * l + hh:8 * l + hh + 1]
                p1 = TT(pool, IX[:, hh, :], IX[:, hh, :], CX[:, hh, :], M_, itk[hh], ct[hh])
                q = 2 + hh % 2
                th = A(act, TMP[:, q, :], RX[:, hh, :], ACT.Tanh, rt[hh], t_ca, tmp_free[q], scale=ca)
                a = A(act, RX[:, hh, :], RX[:, hh, :], ACT.Exp, th, scale=ca)
                d = TT(pool, CX[:, hh, :], RX[:, hh, :], RX[:, hh, :], M_, a, p1, t_g)
                d = STT(CX[:, hh, :], CX[:, hh, :], 1.0, TMP[:, q, :], A_, M_, d)
                tmp_free[q] = [d]
                ax.append((d, p1, a))
            for hh in range(8):
                d, p1, a = ax[hh]
                a2 = A(act, CX[:, hh, :], CX[:, hh, :], ACT.Sqrt, d, scale=-1.0)
                p2 = TT(pool, IX[:, hh, :], IX[:, hh, :], CX[:, hh, :], M_, a2, p1)
                d = dve(lambda e, hh=hh: e.tensor_tensor_scan(out=CX[:, hh, :], data0=RX[:, hh, :], data1=IX[:, hh, :],
                                                              initial=0.0, op0=M_, op1=A_), p2, a)
                yt[hh] = TT(pool, Y[:, hh, :], Y[:, hh, :], CX[:, hh, :], M_, d, yt[hh])
                rg_done = [d, yt[hh]]

            qtk, ktk = [], []
            for z, (dst, lst) in enumerate(((Q2, qtk), (K2, ktk))):
                w, s, wt = chunk(D["ml_wqk"][2 * l + z], (8, 256))
                for m in range(8):
                    h, mt = m // 2, m % 2
                    b = take()
                    t = dense(PS[b][:, :], [w[:, 2 * h + kk, P * mt:P * mt + P] for kk in range(2)],
                              [XC[:, 2 * h + kk, :] for kk in range(2)], wt, [xct[2 * h], xct[2 * h + 1]])
                    a = A(act, dst[:, m, :], PS[b][:, :], ACT.Copy, t, rg_done)
                    give(b, a)
                    lst.append(a)
                release(s, t)
            w, s, wt = chunk(D["ml_wv"][l], (8, 256))
            v2t = []
            for tt in range(4):
                for h2 in range(2):
                    b = take()
                    for h in (2 * h2, 2 * h2 + 1):
                        for kk in range(2):
                            t = mm(PS[b][:, 256 * (h % 2):256 * (h % 2) + 256], XM[:, 2 * h + kk, 3 + P * tt:3 + P * tt + P],
                                   w[:, 2 * h + kk, :], kk == 0, kk == 1, wt, xmt[2 * h + kk], sig=kk == 1)
                    a = A(act, V2[:, tt, T * h2:T * h2 + T], PS[b][:, :], ACT.Copy, t, rg_done)
                    give(b, a)
                v2t.append(a)
            release(s, t)
            w, s, wt = chunk(D["ml_wvT"][l], (8, 256))
            b = take()
            for m in range(8):
                h, mt = m // 2, m % 2
                for kk in range(2):
                    t = mm(PS[b][:, 8 * m:8 * m + 8], w[:, 2 * h + kk, P * mt:P * mt + P], WIF[:, 16 + 2 * h + kk, :],
                           kk == 0, kk == 1, wt, t_wif, sig=kk == 1)
            release(s, t)
            gv = A(act, GV, PS[b][:, 0:64].rearrange("p (a b) -> p a b", b=8), ACT.Copy, t, start)
            give(b, gv)
            b = take()
            lhs = [WIF[:, k, :] for k in range(16)] + [GV[:, k, :] for k in range(8)]
            rhs = [Q2[:, k, :] for k in range(8)] + [K2[:, k, :] for k in range(8)] + [XM[:, k, 3:515] for k in range(8)]
            t = dense(PS[b][0:8, :], lhs, rhs, t_wif, qtk + ktk + [gv] + xmt[1:])
            t_qkv = t
            GB = XC[0:8, 0, :]
            FE, FC, EE, MM, NM, ZR = (XC[:, i, :] for i in range(1, 7))
            ln_ = XC[:, 7, :]
            a = A(act, GB, PS[b][0:8, :], ACT.Identity, t, bias=VEC[0:8, VEC_AT["b_if"][0] + l:VEC_AT["b_if"][0] + l + 1])
            give(b, a)
            bi, bf = take(), take()
            ti = mm(PS[bi][:, :], const("sel_i")[0:8, :], GB, True, True, a, t_const, sig=True)
            tf = mm(PS[bf][:, :], const("sel_f")[0:8, :], GB, True, True, sig=True)
            zt = pool(lambda e: e.memset(ZR, 0.0), t_qkv)
            d = A(act, ln_, PS[bf][:, :], ACT.Abs, tf, t_qkv)
            a = A(act, ln_, ln_, ACT.Exp, d, scale=-1.0)
            a = A(act, ln_, ln_, ACT.Ln, a, bias=1.0)
            d = STT(FE, PS[bf][:, :], 0.0, ln_, ALU.min, S_, a)
            give(bf, d)
            d = dve(lambda e: e.tensor_tensor_scan(out=FC, data0=FE, data1=ZR, initial=0.0, op0=A_, op1=A_), d, zt)
            te = TT(dve, EE, PS[bi][:, :], FC, S_, ti, d)
            give(bi, te)
            d = dve(lambda e: e.tensor_tensor_scan(out=MM, data0=EE, data1=ZR, initial=0.0, op0=ALU.max, op1=ALU.max), te)
            nmt = TS(dve, NM, MM, -1.0, None, M_, None, d)
            mt_ = TT(dve, MM, MM, FC, A_, nmt)
            b = take()
            for j in range(4):
                t = tr(PS[b][:, P * j:P * j + P], EE[:, P * j:P * j + P], IDENT, te, sig=j == 3)
            et = A(act, ET, PS[b][:, :].rearrange("p (j h x) -> p j h x", j=4, h=4)[:, :, :, 0], ACT.Copy, t, start)
            give(b, et)

            WB = [XC[:, 0, :], XC[:, 1, :]]
            SBF = [XC[:, 6, :], XC[:, 7, :]]
            w_free = [[nmt, ti, tf], [nmt]]
            s_free = [[d, zt, nmt], [nmt]]
            n = 0
            cellt = []
            for h in range(4):
                r = slice(32 * h, 32 * h + 1)
                bM, bE = take(), take()
                tM = mm(PS[bM][:, :], const("ones")[r, :], NM[r, :], True, True, nmt, sig=True)
                tE = mm(PS[bE][:, :], const("ones")[r, :], MM[r, :], True, True, mt_, sig=True)
                em = A(act, TMP[:, 2, :], PS[bE][:, :], ACT.Exp, tE, tmp_free[2], scale=-1.0)
                give(bE, em)
                bD, bN0, bN1 = take(), take(), take()
                jobs = []

                def score(j):
                    b = take()
                    for kk in range(2):
                        t = mm(PS[b][:, P * j:T], K2[:, 2 * h + kk, P * j:P * j + P], Q2[:, 2 * h + kk, P * j:T], kk == 0, kk == 1,
                               qtk[2 * h + kk], ktk[2 * h + kk], sig=kk == 1)
                    q = (4 * h + j) % 2
                    diag = WB[q][:, P * j:P * j + P]
                    d = TS(dve, diag, PS[bM][:, P * j:P * j + P], ET[:, j, h:h + 1], 0.0, A_, ALU.min, tM, et, w_free[q])
                    a = A(act, diag, diag, ACT.Exp, d)
                    a0 = a
                    if j < 3:
                        a0 = A(act, WB[q][:, P * j + P:T], PS[bM][:, P * j + P:T], ACT.Exp, tM, et, w_free[q], bias=ET[:, j, h:h + 1])
                    p = pool(lambda e: e.affine_select(out=WB[q][:, P * j:P * j + P], in_=WB[q][:, P * j:P * j + P],
                                                       compare_op=ALU.is_ge, fill=0.0, base=0, pattern=[[1, P]],
                                                       channel_multiplier=-1), a)
                    a = [a0, d]
                    d = STT(SBF[q][:, P * j:T], PS[b][:, P * j:T], 1.0 / 16, WB[q][:, P * j:T], M_, M_, t, p, a0, s_free[q])
                    w_free[q] = [d]
                    give(b, d)
                    return j, q, d, a

                def reduce_(j, q, d, a):
                    x = SBF[q][:, P * j:T]
                    mm(PS[bD][:, P * j:T], ONES, x, j == 0, j == 3, d)
                    mm(PS[bN0][:, P * j:T], V2[:, j, 256 * h:256 * h + P], x, j == 0, j == 3, v2t[j])
                    t = mm(PS[bN1][:, P * j:T], V2[:, j, 256 * h + P:256 * h + 256], x, j == 0, j == 3, sig=True)
                    s_free[q] = [t]
                    return t

                for j in range(4):
                    jobs.append(score(j))
                    if j:
                        reduce_(*jobs.pop(0))
                give(bM, jobs[0][3])
                t = reduce_(*jobs.pop(0))
                ab = A(act, TMP[:, 3, :], PS[bD][:, :], ACT.Abs, t, tmp_free[3])
                give(bD, ab)
                d = TT(dve, TMP[:, 2, :], TMP[:, 2, :], TMP[:, 3, :], ALU.max, ab, em)
                tmp_free[3] = [d]
                d = RECIP(TMP[:, 2, :], TMP[:, 2, :], d)
                for z, bN in enumerate((bN0, bN1)):
                    d = TT(dve, Q2[:, 2 * h + z, :], PS[bN][:, :], TMP[:, 2, :], M_, d, t)
                    give(bN, d)
                    cellt.append(d)
                tmp_free[2] = [d]
            cells_done = pe.last

            hst = []
            zt_ = []
            for h in range(4):
                w, s, wt = cols(12 + h)
                for j in range(2):
                    m = 2 * h + j
                    b, t = proj(w, wt, j)
                    q = m % 2
                    a = A(act, TMP[:, q, :], PS[b][:, :], ACT.Sigmoid, t, tmp_free[q])
                    give(b, a)
                    p = TT(pool, Q2[:, m, :], Q2[:, m, :], TMP[:, q, :], M_, a, cellt[m], cells_done)
                    tmp_free[q] = [p]
                    hst.append(p)
                release(s, t)
                w, s, wt = cols(16 + h)
                for j in range(2):
                    m = 2 * h + j
                    b, t = proj(w, wt, j)
                    a = A(act, K2[:, m, :], PS[b][:, :], ACT.Sigmoid, t, cells_done)
                    d = TT(dve, K2[:, m, :], K2[:, m, :], PS[b][:, :], M_, a)
                    give(b, d)
                    zt_.append(d)
                release(s, t)
                b = take()
                for j in range(2):
                    a = A(act, SQ[:, j, :], Q2[:, 2 * h + j, :], ACT.Square, hst[2 * h + j], stat["sq"][j])
                    stat["sq"][j] = mm(PS[b][:, :], ONES, SQ[:, j, :], j == 0, j == 1, a, sig=True)
                RH = V2[:, h, 0:T]
                t = TS(dve, RH, PS[b][:, :], 1.0 / 256, EPS, M_, A_, stat["sq"][1], cells_done)
                give(b, t)
                hst[2 * h] = hst[2 * h + 1] = [hst[2 * h], hst[2 * h + 1], t]
            for h in range(4):
                RH = V2[:, h, 0:T]
                a = A(act, RH, RH, ACT.Sqrt, hst[2 * h])
                d = RECIP(RH, RH, a)
                for j in range(2):
                    m = 2 * h + j
                    d2 = STT(Q2[:, m, :], Q2[:, m, :], vec("ml_norm_g", 8 * l + m), RH, M_, M_, d, stat["sq"][j])
                    yt.append(TT(pool, YM[:, m, :], Q2[:, m, :], K2[:, m, :], M_, d2, zt_[m], t_qkv))
            residual("w_out2" + "ab"[l], (16, P), [Y[:, i, :] for i in range(8)] + [YM[:, i, :] for i in range(8)], yt,
                     gate=lambda m: MOD[:, 24 * l + 16 + m:24 * l + 17 + m], per=1)

        HT = norm(lambda k: vec("final_g", k), HN, pe.last)
        nout = 0
        for c in range(4):
            sp.wait(HT[2 * c], HT[2 * c + 1])
            sp.ops.append(lambda e, c=c: e.dma_start(out[:, 2 * c:2 * c + 2, :], HN[:, 2 * c:2 * c + 2, :]).then_inc(s_out, 16))
            nout += 16
        sp.ops.append(lambda e: e.wait_ge(s_out, nout))

        block = ctx.enter_context(nc.Block())

        def play(q):
            def run(e):
                for op in q.ops:
                    op(e)
            return run

        block.sync(play(sp))
        block.scalar(play(act))
        block.vector(play(dve))
        block.gpsimd(play(pool))
        block.tensor(play(pe))


def _tiles(w, mc):
    k, m = w.shape
    return np.ascontiguousarray(w.reshape(k // P, P, m // mc, mc).transpose(2, 1, 0, 3).reshape(m // mc, P, -1))


def _cols(v):
    return v.reshape(-1, P).T


def _consts():
    half = 32
    inv = (np.float32(10000.0) ** (-np.arange(half, dtype=np.float32) / np.float32(half))).astype(np.float32)
    ang = (np.arange(T, dtype=np.float32)[:, None] * inv[None, :]).astype(np.float64)
    cos, sin = np.cos(ang).T, np.sin(ang).T
    c = {}
    c["cos"] = np.tile(cos, (4, 1))
    c["sin"] = np.concatenate([-sin, sin, -sin, sin], 0)
    c["ident"] = np.eye(P)
    c["ones"] = np.ones((P, P))
    c["rot"] = np.eye(P)[np.arange(P) ^ 32]
    i = np.arange(P)
    c["causal"] = np.where(i[None, :] <= i[:, None], 0.0, NEG)
    tok = np.arange(4)[None, :, None] * P + i[:, None, None]
    end = np.arange(32)[None, None, :] * 16 + 31
    ok = (end <= tok) & (np.arange(32)[None, None, :] < 31)
    c["cneg"] = np.where(ok, 0.0, NEG).reshape(P, 128)
    c["c01"] = ok.astype(np.float32).reshape(P, 128)
    for z, n in enumerate(("sel_i", "sel_f")):
        s = np.zeros((P, P))
        for h in range(4):
            s[4 * z + h, 32 * h] = 1.0
        c[n] = s
    return np.ascontiguousarray(np.concatenate([c[n] for n, _ in CONST_COLS], 1).astype(np.float32))


def _layout(I):
    f = np.float32
    A = {}
    A["xT"] = np.ascontiguousarray(I["x"][0].T.reshape(8, P, T).transpose(1, 0, 2))
    A["pT"] = np.ascontiguousarray(I["p"][0, 0].T.reshape(2, P, T).transpose(1, 0, 2))
    for z, n in (("a", "ffn1"), ("b", "ffn2")):
        w1, w3 = (_tiles(I[f"{n}_w{k}"][0], P) for k in (1, 3))
        A["w13" + z] = np.ascontiguousarray(np.stack([w1, w3], 2).reshape(22, P, 2, 1024).reshape(22, P, 2048))
        w2 = I[f"{n}_w2"][0]
        A["w2" + z] = np.concatenate([_tiles(w2[1408 * k:1408 * k + 1408], P) for k in range(2)], 0)
    perm = np.concatenate([h * 64 + np.arange(64) for i in range(4) for h in (i, 4 + i)])
    heads = [h for i in range(4) for h in (i, 4 + i)]
    w = I["w_in"][0]
    part = lambda k: w[:, 512 + 128 * k:640 + 128 * k]
    A["w_inA"] = _tiles(np.concatenate([w[:, 1304:1816], w[:, perm], part(0), part(2), part(4), part(1)], 1), 256)
    A["w_inV"] = _tiles(np.concatenate([part(3), part(5)], 1), 256)[0]
    wg = w[:, 1280:1304].reshape(1024, 8, 3)[:, heads, :].transpose(0, 2, 1).reshape(1024, 24)
    wk2 = I["cmp_wk2"][0]
    A["small_w"] = np.ascontiguousarray(np.concatenate(
        [_tiles(wg, 24)[0], _tiles(np.concatenate([wk2, wk2], 1), P)[0], _tiles(I["cmp_wv2"][0], 64)[0]], 1))
    for n in ("wk1", "wv1"):
        a = I["cmp_" + n][0]
        A[n] = np.concatenate([_tiles(a[1024 * k:1024 * k + 1024], 256) for k in range(2)], 0)
    bc = np.zeros((P, 2048), f)
    for z, n in enumerate(("s5_b_re", "s5_b_im")):
        b = I[n][0]
        for g in range(32):
            y4, j, g2 = g // 8, (g % 8) // 2, g % 2
            bc[32 * j + 16 * g2:32 * j + 16 * g2 + 16, 512 * z + P * y4 + 64 * g2:512 * z + P * y4 + 64 * g2 + 64] = b[g].T
    for z, n in enumerate(("s5_c_re", "s5_c_im")):
        c = I[n][0]
        for g in range(32):
            t, g2 = g // 2, g % 2
            at = 1024 + 512 * z + 32 * t + 16 * g2
            bc[64 * g2:64 * g2 + 64, at:at + 16] = c[g].T
    A["s5_bc"] = bc
    A["w_glu"] = _tiles(I["s5_w_glu"][0], 512)[0]
    wo = I["w_out"][0]
    A["w_out"] = _tiles(np.concatenate([wo[:512][perm], wo[512:]], 0), 256)
    A["w_pg"] = _tiles(I["w_ple_gate"][0], 256)
    A["w_ple"] = _tiles(I["w_ple"][0], 1024)[0]
    A["c"] = np.ascontiguousarray(I["c_2"].reshape(1024))
    wa = np.concatenate([I["w_ada_2"][l].T.reshape(12, 2, P, 1024).transpose(0, 2, 1, 3).reshape(12, P, 2048) for l in range(2)], 0)
    A["w_ada"] = np.ascontiguousarray(wa)
    A["w_in2"] = np.concatenate([_tiles(I["w_in_2"][l], 256) for l in range(2)], 0)
    A["rg_w"] = np.ascontiguousarray(np.stack([np.concatenate(
        [I[n][l].transpose(1, 0, 2).reshape(P, 1024) for n in ("rg_w_a_2", "rg_w_x_2")], 1) for l in range(2)]))

    def heads4(a):
        return a.reshape(4, 2, P, 256).transpose(2, 0, 1, 3).reshape(P, 2048)
    A["ml_wqk"] = np.ascontiguousarray(np.stack([heads4(I[n][l]) for l in range(2) for n in ("ml_w_q_2", "ml_w_k_2")]))
    A["ml_wv"] = np.ascontiguousarray(np.stack([heads4(I["ml_w_v_2"][l]) for l in range(2)]))
    A["ml_wvT"] = np.ascontiguousarray(np.stack([heads4(I["ml_w_v_2"][l].transpose(0, 2, 1)) for l in range(2)]))
    A["w_if"] = np.ascontiguousarray(np.stack([I["ml_w_if_2"][l].reshape(24, P, 8).transpose(1, 0, 2).reshape(P, 192) for l in range(2)]))
    for l in range(2):
        A["w_out2" + "ab"[l]] = _tiles(I["w_out_2"][l], P)
    two = lambda a: np.concatenate([_cols(a[l]) for l in range(2)], 1)
    conv = lambda a: np.concatenate([_cols(a[l, i]) for l in range(2) for i in range(4)], 1)
    bif = np.zeros((P, 2), f)
    bif[0:8, :] = I["ml_b_if_2"].T
    V = {
        "norm_ffn1": _cols(I["norm_ffn1"][0]), "norm_mix": _cols(I["norm_mix"][0]), "norm_ffn2": _cols(I["norm_ffn2"][0]),
        "norm_ple": _cols(I["norm_ple"][0]), "norm_final": _cols(I["norm_final"]),
        "a_re": _cols(I["s5_a_re"][0]), "a_im": _cols(I["s5_a_im"][0]), "log_dt": _cols(np.repeat(I["s5_log_dt"][0], 64)),
        "s5_d": _cols(I["s5_d"][0]), "b_glu": _cols(I["s5_b_glu"][0]), "pe_k": _cols(I["cmp_pe_k"][0]), "pe_v": _cols(I["cmp_pe_v"][0]),
        "norm_g": two(I["norm_g_2"]), "b_ada": two(I["b_ada_2"]),
        "rg_conv_w": conv(I["rg_conv_w_2"]), "rg_conv_b": two(I["rg_conv_b_2"]), "rg_b_a": two(I["rg_b_a_2"]), "rg_b_x": two(I["rg_b_x_2"]),
        "rg_lam": two(I["rg_lambda_2"]), "ml_conv_w": conv(I["ml_conv_w_2"]), "ml_conv_b": two(I["ml_conv_b_2"]),
        "ml_norm_g": two(I["ml_norm_g_2"]), "final_g": _cols(I["final_g_2"]), "b_if": bif,
    }
    A["vecs"] = np.ascontiguousarray(np.concatenate([V[n] for n, _ in VEC_COLS], 1))
    A["consts"] = _consts()
    return A


def kernel(**inputs):
    import concourse.bacc as bacc
    from concourse.bass_utils import run_bass_kernel_spmd

    I = {k: np.asarray(v) for k, v in inputs.items()}
    nc = bacc.Bacc("TRN2", target_bir_lowering=False, num_devices=1)
    arrays, D = {}, {}
    for name, a in _layout(I).items():
        arrays[f"in_{name}"] = a
        D[name] = nc.dram_tensor(f"in_{name}", a.shape, mybir.dt.from_np(a.dtype), kind="ExternalInput").ap()
    out = nc.dram_tensor("out_0", (P, 8, T), F32, kind="ExternalOutput").ap()
    program(nc, D, out)
    r = run_bass_kernel_spmd(nc, [arrays], core_ids=[0])
    o = r.results[0]["out_0"]
    return np.ascontiguousarray(o.transpose(1, 0, 2).reshape(1024, T).T)[None]
```

```python
from contextlib import ExitStack

import numpy as np

import concourse.bass as bass
from concourse import mybir

ALU = mybir.AluOpType
ACT = mybir.ActivationFunctionType
F32 = mybir.dt.float32
F32R = mybir.dt.float32r
AXX = mybir.AxisListType.X

P = 128
T = 512
KD = 8
NEG = -1e30
EPS = 1e-6

VEC_COLS = [
    ("norm_ffn1", 8), ("norm_mix", 8), ("norm_ffn2", 8), ("norm_ple", 8), ("norm_final", 8),
    ("a_re", 16), ("a_im", 16), ("log_dt", 16), ("s5_d", 4), ("b_glu", 4), ("pe_k", 16), ("pe_v", 16),
    ("norm_g", 16), ("b_ada", 48), ("rg_conv_w", 64), ("rg_conv_b", 16), ("rg_b_a", 16), ("rg_b_x", 16),
    ("rg_lam", 16), ("ml_conv_w", 64), ("ml_conv_b", 16), ("ml_norm_g", 16), ("final_g", 8), ("b_if", 2),
]
VEC_AT = {}
_n = 0
for _name, _w in VEC_COLS:
    VEC_AT[_name] = (_n, _w)
    _n += _w
NVEC = _n

CONST_COLS = [("cos", T), ("sin", T), ("ident", P), ("ones", P), ("rot", P), ("causal", P),
              ("cneg", 128), ("c01", 128), ("sel_i", P), ("sel_f", P)]
CONST_AT = {}
_n = 0
for _name, _w in CONST_COLS:
    CONST_AT[_name] = (_n, _w)
    _n += _w
NCONST = _n


def adas(half, i):
    if half == 0:
        return 2 if i >= 10 else 0
    return 0 if i > 10 else 3 if i < 8 else 2


def plan():
    out = []

    def ffn(z):
        for half in range(2):
            for mi in range(11):
                out.extend(("w13" + z, (half * 11 + mi) * 2 + x, 1024, True) for x in range(2))
            out.extend(("w2" + z, half * 8 + m, 1408, True) for m in range(8))

    ffn("a")
    out.extend(("w_inA", c, 1024, True) for c in range(12))
    out.extend((f"w_inV{z}", None, 1024 + 192 * z, True) for z in range(2))
    out.extend((n, c, 1024, False) for n in ("wk1", "wv1") for c in range(4))
    out.extend(("w_glu", m, 512, False) for m in range(4))
    out.extend(("w_out", m, 1024, False) for m in range(8))
    ffn("b")
    out.extend(("w_pg", m, 1024, True) for m in range(8))
    for l in range(2):
        for part in (0, 2, 1):
            out.extend(("w_in2", 40 * l + 8 * part + m, 1024, True) for m in range(8))
        out.extend(("ml_wqk", 4 * l + c, 1024, False) for c in range(4))
        out.extend(("ml_wv", 2 * l + c, 1024, False) for c in range(2))
        out.extend(("ml_wvT", 2 * l + c, 1024, False) for c in range(2))
        for h in range(4):
            out.extend(("w_in2", 40 * l + 8 * part + 2 * h + j, 1024, True) for part in (3, 4) for j in range(2))
        out.extend(("w_out2", 16 * l + c, 1024, True) for c in range(16))
    return out


class Queue:

    def __init__(self, sem):
        self.sem, self.n, self.ops, self.seen = sem, 0, [], {}

    def wait(self, *tokens):
        for t in tokens:
            if t is None:
                continue
            if isinstance(t, list):
                self.wait(*t)
                continue
            sem, value = t
            if self.seen.get(id(sem), 0) < value:
                self.seen[id(sem)] = value
                self.ops.append(lambda e, s=sem, v=value: e.wait_ge(s, v))

    def __call__(self, fn, *tokens, sig=True):
        self.wait(*tokens)
        if sig:
            self.n += 1
            self.ops.append(lambda e: fn(e).then_inc(self.sem, 1))
            return (self.sem, self.n)
        self.ops.append(fn)
        return None

    @property
    def last(self):
        return (self.sem, self.n)


def program(nc, D, out):
    ctx = ExitStack()
    with ctx:
        def sem(name):
            return ctx.enter_context(nc.semaphore(name))

        at = [0]
        base = (nc.sbuf_base + 31) // 32 * 32

        def place(name, offset, n, dt=F32):
            return nc.alloc_sbuf_tensor_at(name, [P, n], dt, offset=base + 4 * offset)

        def sb(name, n, dt=F32):
            at[0] += (n + 7) // 8 * 8
            return place(name, at[0] - (n + 7) // 8 * 8, n, dt)

        def tiles_(t):
            return t[:, :].rearrange("p (k t) -> p k t", t=T)

        H = tiles_(sb("H", KD * T))
        at_hn = at[0]
        HNH, HNL = tiles_(sb("HNH", KD * T, F32R)), tiles_(sb("HNL", KD * T, F32R))
        HX = place("HX", at_hn, 2 * KD * T)
        TMPf = sb("TMP", 4 * T)
        TMP = tiles_(TMPf)
        SQf = sb("SQ", 2 * T)
        SQ = tiles_(SQf)
        ACC = sb("ACC", T)[:, :]
        RSf = sb("RS", 2 * T)
        RS, RR = RSf[:, 0:T], RSf[:, T:2 * T]
        CONST = sb("CONST", NCONST)
        VEC = sb("VEC", NVEC)
        MOD = sb("MOD", 48)
        GS = sb("GS", 40)
        LA = sb("LA", 6 * 16)
        NAR = 20800
        at_ar = at[0]
        AR = sb("AR", NAR)
        NSLOT, SLOT = 3, 1408
        RAW = sb("RAW", NSLOT * SLOT)
        NW = 3
        WHI, WLO = sb("WHI", NW * SLOT, F32R), sb("WLO", NW * SLOT, F32R)
        assert base + 4 * at[0] <= 229344, at[0]
        HIDH, HIDL = tiles_(place("HIDH", at_ar + 7168, 11 * T, F32R)), tiles_(place("HIDL", at_ar + 7168 + 11 * T, 11 * T, F32R))
        YRH, YRL = tiles_(place("YRH", at_ar + 8224, 8 * T, F32R)), tiles_(place("YRL", at_ar, 8 * T, F32R))
        PS = [ctx.enter_context(nc.psum_tensor(f"PS{b}", [P, T], F32)) for b in range(8)]

        def const(name):
            a, w = CONST_AT[name]
            return CONST[:, a:a + w]

        def vec(name, i=None, n=1):
            a, w = VEC_AT[name]
            return VEC[:, a:a + w] if i is None else VEC[:, a + i:a + i + n]

        COS, SIN, IDENT, ONES, ROT = (const(n) for n in ("cos", "sin", "ident", "ones", "rot"))

        pe, act, dve, pool = (Queue(sem(f"s_{n}")) for n in ("pe", "act", "dve", "pool"))
        sp = Queue(sem("s_sp"))
        s_out = sem("s_out")

        slot_sem = [sem(f"s_slot{i}") for i in range(NSLOT)]
        slot_free = [[] for _ in range(NSLOT)]
        w_free = [[] for _ in range(NW)]
        order = plan()
        got = []
        asked = [0]
        nsplit = [0]

        def fetch():
            k = len(got)
            name, i, n, split = order[k]
            s = k % NSLOT
            assert slot_free[s] is not None, (k, name)
            src = D[name] if i is None else D[name][i]
            raw = RAW[:, s * SLOT:s * SLOT + n]
            sp.wait(slot_free[s])
            slot_free[s] = None
            sp.ops.append(lambda e: e.dma_start(raw, src).then_inc(slot_sem[s], 16))
            tok = (slot_sem[s], 16 * (k // NSLOT + 1))
            if not split:
                got.append((raw, s, tok))
                return
            w = nsplit[0] % NW
            nsplit[0] += 1
            assert w_free[w] is not None, (k, name)
            hi, lo = WHI[:, w * SLOT:w * SLOT + n], WLO[:, w * SLOT:w * SLOT + n]
            th = A(act, hi, raw, ACT.Copy, tok, w_free[w])
            tl = TT(dve, lo, raw, hi.bitcast(F32), ALU.subtract, th)
            w_free[w] = None
            slot_free[s] = [tl]
            got.append((hi, lo, w, th, tl))

        def ahead():
            k = asked[0]
            while len(got) < len(order) and len(got) < k + 3 and slot_free[len(got) % NSLOT] is not None:
                if order[len(got)][3] and w_free[nsplit[0] % NW] is None:
                    break
                fetch()

        def ask(name, i, split):
            k = asked[0]
            assert order[k][0] == name and order[k][1] == i and order[k][3] == split, (k, order[k], name, i)
            while len(got) <= k:
                fetch()
            asked[0] += 1
            ahead()
            return got[k]

        def shaped(v, shape):
            if len(shape) == 2:
                return v.rearrange("p (a b) -> p a b", b=shape[1])
            return v

        def chunk(name, i, shape):
            raw, s, tok = ask(name, i, False)
            return shaped(raw, shape), s, tok

        def release(s, *tokens):
            slot_free[s] = list(tokens)
            ahead()

        def wchunk(name, i, k, m=P):
            hi, lo, w, th, tl = ask(name, i, True)
            return shaped(hi, (k, m)), shaped(lo, (k, m)), w, th, tl

        def wrelease(w, *tokens):
            w_free[w] = list(tokens)
            ahead()

        own = [0]

        def load(dst, src, q=sp, *tokens):
            s = sem(f"s_ld{own[0]}")
            own[0] += 1
            q.wait(*tokens)
            q.ops.append(lambda e: e.dma_start(dst, src).then_inc(s, 16))
            return (s, 16)

        banks = [(b, []) for b in range(7)]
        STAT = PS[7]

        def take():
            b, tokens = banks.pop(0)
            pe.wait(*tokens)
            return b

        def give(b, *tokens):
            banks.append((b, list(tokens)))

        def mm(o, l, r, start=True, stop=True, *tokens, sig=False):
            return pe(lambda e: e.matmul(o, l, r, start=start, stop=stop, skip_group_check=True), *tokens, sig=sig)

        def tr(o, i, ident, *tokens, sig=False):
            return pe(lambda e: e.transpose(o, i, ident), *tokens, sig=sig)

        def dense(o, lhs, rhs, wtok, xtoks):
            n = len(lhs)
            t = None
            for k in range(n):
                t = mm(o, lhs[k], rhs[k], k == 0, k == n - 1, wtok if k == 0 else None, xtoks[k], sig=k == n - 1)
            return t

        def dense3(o, w, xh, xl, xt, off=0, n=None, start=True, stop=True):
            hi, lo, _, th, tl = w
            n = n or len(xh)
            for k in range(n):
                mm(o, hi[:, k, :], xh[off + k], start and k == 0, False, th, xt[off + k][0])
                mm(o, lo[:, k, :], xh[off + k], False, False, tl)
            for k in range(n):
                t = mm(o, hi[:, k, :], xl[off + k], False, stop and k == n - 1, xt[off + k][1], sig=k == n - 1)
            return t

        def A(q, o, i, f, *tokens, **kw):
            return q(lambda e: e.activation(o, i, f, **kw), *tokens)

        def TT(q, o, a, b, op, *tokens):
            return q(lambda e: e.tensor_tensor(o, a, b, op), *tokens)

        def TS(q, o, a, s1, s2, op0, op1, *tokens):
            if op1 is None:
                return q(lambda e: e.tensor_scalar(o, a, s1, None, op0), *tokens)
            return q(lambda e: e.tensor_scalar(o, a, s1, s2, op0, op1), *tokens)

        def STT(o, a, s, b, op0, op1, *tokens):
            return dve(lambda e: e.scalar_tensor_tensor(out=o, in0=a, scalar=s, in1=b, op0=op0, op1=op1), *tokens)

        def RECIP(o, i, *tokens):
            return dve(lambda e: e.reciprocal(o, i), *tokens)

        def bc(ap, axis, shape):
            return ap.unsqueeze(axis).to_broadcast(shape)

        M_, A_, S_ = ALU.mult, ALU.add, ALU.subtract

        def everyone():
            return [pe.last, act.last, dve.last, pool.last]

        def ar(at, *shape):
            n = int(np.prod(shape))
            assert at + n <= NAR, (at, shape)
            v = AR[:, at:at + n]
            if len(shape) == 2:
                v = v.rearrange("p (a b) -> p a b", b=shape[1])
            if len(shape) == 3:
                v = v.rearrange("p (a b c) -> p a b c", b=shape[1], c=shape[2])
            return v

        t_vec = load(VEC[:, :], D["vecs"])
        t_xs = [load(H[:, 2 * c:2 * c + 2, :], D["xT"][:, 2 * c:2 * c + 2, :], act) for c in range(4)]
        t_const = load(CONST[:, :], D["consts"], act)
        HT = [t_xs[k // 2] for k in range(KD)]
        HNHk, HNLk = [HNH[:, k, :] for k in range(KD)], [HNL[:, k, :] for k in range(KD)]

        sq_free = [None, None]
        acc_free = [None]
        first = {}

        def square(k, acc, tok, scale=1.0):
            if k == 0:
                first[id(acc)] = A(act, acc, H[:, k, :], ACT.Square, tok, acc_free[0], scale=scale)
                return first[id(acc)]
            t = A(act, SQ[:, k % 2, :], H[:, k, :], ACT.Square, tok, sq_free[k % 2], scale=scale)
            sq_free[k % 2] = TT(pool, acc, acc, SQ[:, k % 2, :], A_, t, first[id(acc)], pool.last)
            return sq_free[k % 2]

        stat_free = [None]

        def colsum(acc, tok):
            t = mm(STAT[:, :], ONES, acc, True, True, tok, t_const, stat_free[0], sig=True)
            return t

        def rstd(dst, src, n, *tokens):
            t = TS(dve, dst, src, 1.0 / n, EPS, M_, A_, *tokens)
            back = t
            t = A(act, dst, dst, ACT.Sqrt, t)
            return RECIP(dst, dst, t), back

        rs = {"tok": None, "acc": None}

        def split_x(k, gain, tok, *free):
            h = A(act, HNH[:, k, :], H[:, k, :], ACT.Copy, tok, t_vec, *free, scale=gain)
            l = STT(HNL[:, k, :], H[:, k, :], gain, HNH[:, k, :].bitcast(F32), M_, S_, h)
            return h, l

        def need_rs(*readers):
            if rs["acc"] is not None:
                t = colsum(ACC, rs["acc"])
                rs["acc"] = None
                rs["tok"], stat_free[0] = rstd(RS, STAT[:, :], 1024.0, t, *readers)
                acc_free[0] = t
            return rs["tok"]

        def next_norm(name, xt, free):
            def post(m):
                t = square(m, ACC, HT[m])
                xt[m] = split_x(m, vec(name, m), HT[m], free())
                if m == KD - 1:
                    rs["acc"] = t
            return post

        CB = ar(5120, 1024)
        ada_at = [0]
        ada_c = []

        def ada_start(t):
            t_c = load(CB, D["c"].partition_broadcast(P), act, t)
            t_cs = A(act, STMP[:, 0:1024], CB, ACT.Silu, t_c, t)
            ada_c.append(dve(lambda e: e.tensor_copy(CB, STMP[:, 0:1024]), t_cs))
            return ada_c[0]

        ada_sem = [sem(f"s_ada{i}") for i in range(2)]
        ada_free = [[], []]

        def ada():
            c = ada_at[0]
            ada_at[0] += 1
            w = STMP[:, 1024 * (c % 2):1024 * (c % 2) + 1024]
            pool.wait(ada_free[c % 2], ada_c)
            pool.ops.append(lambda e: e.dma_start(w, D["w_ada"][c]).then_inc(ada_sem[c % 2], 16))
            t = dve(lambda e: e.tensor_tensor_reduce(
                out=w, in0=w, in1=CB, scale=1.0, scalar=0.0, op0=M_, op1=A_,
                accum_out=MOD[:, c:c + 1]), (ada_sem[c % 2], 16 * (c // 2 + 1)), ada_c)
            ada_free[c % 2] = [t]

        tmp_free = [[], [], [], []]
        HIDHk, HIDLk = [HIDH[:, k, :] for k in range(11)], [HIDL[:, k, :] for k in range(11)]

        def ffn(w13, w2, xt, post, pre=None, side=lambda half, i: None):
            hid_free = pre
            for half in range(2):
                hidt = []
                for mi in range(11):
                    bs = []
                    for z in range(2):
                        w = wchunk(w13, (half * 11 + mi) * 2 + z, 8)
                        b = take()
                        t = dense3(PS[b][:, :], w, HNHk, HNLk, xt)
                        wrelease(w[2], t)
                        bs.append((b, t))
                    x13[0] = t
                    q = mi % 3
                    r = need_rs()
                    (bA, tA), (bB, tB) = bs
                    d = TT(dve, TMP[:, q, :], PS[bA][:, :], RS, M_, r, tA, tmp_free[q])
                    give(bA, d)
                    a = A(act, TMP[:, q, :], TMP[:, q, :], ACT.Silu, d)
                    d = TT(dve, TMP[:, q, :], TMP[:, q, :], PS[bB][:, :], M_, a, tB)
                    give(bB, d)
                    h = A(act, HIDH[:, mi, :], TMP[:, q, :], ACT.Copy, d, hid_free)
                    l = TT(dve, HIDL[:, mi, :], TMP[:, q, :], HIDH[:, mi, :].bitcast(F32), S_, h)
                    tmp_free[q] = [l]
                    hidt.append((h, l))
                    side(half, mi)
                for m in range(KD):
                    w = wchunk(w2, half * 8 + m, 11)
                    b = take()
                    t = dense3(PS[b][:, :], w, HIDHk, HIDLk, hidt)
                    wrelease(w[2], t)
                    d = TT(dve, TMP[:, 3, :], PS[b][:, :], RS, M_, t, tmp_free[3])
                    give(b, d)
                    HT[m] = STT(H[:, m, :], TMP[:, 3, :], 0.5, H[:, m, :], M_, A_, d, HT[m])
                    tmp_free[3] = [HT[m]]
                    if half:
                        post(m)
                    side(half, 11 + m)
                hid_free = t
            return t

        x13 = [None]

        TC, TSN = ar(0, 16, P), ar(2048, 16, P)
        SBr, SBi = ar(4096, 4, P), ar(4608, 4, P)
        CR, CI = ar(5120, 16, 32), ar(5632, 16, 32)
        CpR, CpI = ar(6144, 16, 32), ar(6656, 16, 32)
        U = ar(7168, 4, T)
        SMALL = AR[:, 20512:20512 + 256]
        RHO = AR[:, 20784:20800]
        t_sb = load(AR[:, 4096:6144], D["s5_bc"], act)

        def sm(i):
            return SMALL[:, 16 * i:16 * i + 16]

        STMP = ar(18432, 2048)

        def s5_params():
            dt, x, th, k, r, cs, sn, t1, t2, arr, aii, br, bi, den = (sm(i) for i in range(14))
            lr, li = vec("a_re"), vec("a_im")
            t = A(act, dt, vec("log_dt"), ACT.Exp, t_vec)
            t = TT(dve, x, lr, dt, M_, t)
            t_rho = A(act, RHO, x, ACT.Exp, t)
            t = TT(dve, th, li, dt, M_, t)
            yield
            magic = 1.5 * 2.0 ** 23
            t = TS(dve, k, th, float(1 / (2 * np.pi)), None, M_, None, t)
            t = TS(dve, k, k, magic, None, A_, None, t)
            t = TS(dve, k, k, magic, None, S_, None, t)
            c1 = 6.28125
            c2 = float(np.float32(2 * np.pi - c1))
            c2 = float(np.frombuffer((np.frombuffer(np.float32(c2).tobytes(), np.uint32) & np.uint32(0xFFFFE000)).tobytes(), np.float32)[0])
            c3 = float(2 * np.pi - c1 - c2)
            t = STT(r, k, -c1, th, M_, A_, t)
            t = STT(r, k, -c2, r, M_, A_, t)
            t = STT(r, k, -c3, r, M_, A_, t)
            t = TS(dve, r, r, 3.1415925, -3.1415925, ALU.min, ALU.max, t)
            yield
            t_s = A(act, sn, r, ACT.Sin, t)
            t = A(act, t1, r, ACT.Abs, t)
            t = TS(dve, t1, t1, -1.0, float(np.pi / 2), M_, A_, t)
            t = A(act, cs, t1, ACT.Sin, t)
            yield
            t = TT(dve, arr, RHO, cs, M_, t, t_rho)
            t = TT(dve, aii, RHO, sn, M_, t_s, t)
            t = TS(dve, arr, arr, -1.0, None, A_, None, t)
            t = TT(dve, t1, lr, lr, M_, t)
            t = TT(dve, t2, li, li, M_, t)
            t = TT(dve, den, t1, t2, A_, t)
            yield
            t = RECIP(den, den, t)
            t = TT(dve, t1, arr, lr, M_, t)
            t = TT(dve, t2, aii, li, M_, t)
            t = TT(dve, br, t1, t2, A_, t)
            t = TT(dve, br, br, den, M_, t)
            t = TT(dve, t1, aii, lr, M_, t)
            t = TT(dve, t2, arr, li, M_, t)
            t = TT(dve, bi, t1, t2, S_, t)
            t = TT(dve, bi, bi, den, M_, t)
            yield
            b3 = [P, 16, 32]
            w1 = STMP[:, 0:512].rearrange("p (a b) -> p a b", b=32)
            w2 = STMP[:, 512:1024].rearrange("p (a b) -> p a b", b=32)
            t = TT(dve, w1, CR, bc(br, 2, b3), M_, t, t_sb)
            t = TT(dve, w2, CI, bc(bi, 2, b3), M_, t)
            t = TT(dve, CpR, w1, w2, S_, t)
            t = TT(dve, w1, CR, bc(bi, 2, b3), M_, t)
            t = TT(dve, w2, CI, bc(br, 2, b3), M_, t)
            t = TT(dve, CpI, w1, w2, A_, t)
            t = TS(dve, CpI, CpI, -1.0, None, M_, None, t)
            yield
            t = dve(lambda e: e.tensor_copy(TC[:, :, 0:1], cs.unsqueeze(2)), t)
            t = dve(lambda e: e.tensor_copy(TSN[:, :, 0:1], sn.unsqueeze(2)), t)
            d = 1
            while d < P:
                sh = [P, 16, d]
                v1 = STMP[:, 0:16 * d].rearrange("p (a b) -> p a b", b=d)
                v2 = STMP[:, 1024:1024 + 16 * d].rearrange("p (a b) -> p a b", b=d)
                c0, s0, c1_, s1_ = TC[:, :, 0:d], TSN[:, :, 0:d], TC[:, :, d - 1:d], TSN[:, :, d - 1:d]
                cw, sw = c1_.to_broadcast(sh), s1_.to_broadcast(sh)
                for o, (x1, x2), op in ((TC, (cw, sw), S_), (TSN, (sw, cw), A_)):
                    t = TT(dve, v1, c0, x1, M_, t)
                    t = TT(dve, v2, s0, x2, M_, t)
                    t = TT(dve, o[:, :, d:2 * d], v1, v2, op, t)
                d *= 2
                yield
            s5_ready.append(t)

        def softplus_neg(dst, x):
            y, z, z2, acc, t1 = (LA[:, 16 * i:16 * i + 16] for i in range(5))
            t = A(act, y, x, ACT.Abs, t_vec, dve.last)
            t = A(act, y, y, ACT.Exp, t, scale=-1.0)
            t = TS(dve, z, y, 2.0, None, A_, None, t)
            t = RECIP(z, z, t)
            t = TT(dve, z, z, y, M_, t)
            t = TT(dve, z2, z, z, M_, t)
            t = TS(dve, acc, z2, 1.0 / 19, 1.0 / 17, M_, A_, t)
            for n in (15, 13, 11, 9, 7, 5, 3, 1):
                t = TT(dve, acc, acc, z2, M_, t)
                t = TS(dve, acc, acc, 1.0 / n, None, A_, None, t)
            t = TT(dve, acc, acc, z, M_, t)
            t = TS(dve, t1, x, -1.0, 0.0, M_, ALU.max, t)
            return STT(dst, acc, 2.0, t1, M_, A_, t)

        CA = LA[:, 80:96]
        xt = [None] * KD
        post = next_norm("norm_ffn1", xt, lambda: None)
        for k in range(KD):
            post(k)
        s5_ready = []
        params = s5_params()
        ca_ready = []

        def side(half, i):
            if half == 0 and i < 10:
                next(params, None)
                next(params, None)
            if (half, i) == (0, 9):
                ada_start(s5_ready)
                t = softplus_neg(CA, vec("rg_lam"))
                ca_ready.append(TS(dve, CA, CA, -8.0, None, M_, None, t))
            for _ in range(adas(half, i)):
                ada()

        xt_mix = [None] * KD
        ffn("w13a", "w2a", xt, next_norm("norm_mix", xt_mix, lambda: x13[0]), side=side)
        t_s5, t_ca = s5_ready[0], ca_ready[0]
        t_pre = everyone()

        V_ = [[ar(at_v, 2, T) for at_v in pair] for pair in ((9216, 10240), (11264, 12288), (5120, 19456))]
        Q = ar(13312, 4, T)
        KC, KSL, KW, VCT = (AR[:, 15360 + T * i:15360 + T * (i + 1)] for i in range(4))
        VT = ar(17408, 4, 256)
        GT, GX = ar(18432, 4, 24), ar(18528, 4, 24)
        CM, CS = ar(18624, 32), ar(18656, 32)
        HIDc = ar(18688, 2, 64)
        KCC = ar(18816, 64)
        VC = ar(18880, 128)
        ST4 = ar(19008, 7, 4)
        E1, E2, E3 = ar(19040, 2, 2), ar(19048, 2, 2), ar(19056, 2, 2)
        RT = ar(19064, 4)
        WK2, WV2 = ar(19072, 2, 128), ar(19328, 2, 64)
        PT = HX[:, 0:4096].rearrange("p (h k t) -> p h k t", h=2, k=4)
        XBp = HX[:, 0:1984].rearrange("p (s i g c) -> p s i g c", s=2, i=16, g=2)
        PB = HX[:, 4096:6144].rearrange("p (a t) -> p a t", t=T)
        XAp = HX[:, 4096:5120].rearrange("p (g t) -> p g t", t=T)
        CEf = HX[:, 6144:7168]
        CE = CEf.rearrange("p (a b c) -> p a b c", b=8, c=32)
        PTC = HX[:, 7168:8192].rearrange("p (a b) -> p a b", b=T)
        t_wg = load(AR[:, 19072:19456], D["small_w"], act, t_pre)

        def w_in_tiles():
            for c in range(12):
                w = wchunk("w_inA", c, 8)
                b = take()
                t = dense3(PS[b][:, :], w, HNHk, HNLk, xt_mix)
                wrelease(w[2], t)
                yield b, t, need_rs()

        tiles = w_in_tiles()
        ut = []
        for m in range(4):
            b, t, r = next(tiles)
            a = TT(dve, U[:, m, :], PS[b][:, :], RS, M_, t, r, t_pre)
            give(b, a)
            ut.append(a)
        b = take()
        for j in range(4):
            t = tr(PS[b][:, P * j:P * j + P], RS[:, P * j:P * j + P], IDENT, r, t_const, sig=j == 3)
        t_rt = A(act, RT, PS[b][:, :].rearrange("p (j x) -> p j x", j=4)[:, :, 0], ACT.Copy, t, t_pre)
        give(b, t_rt)

        ot = [None] * 8

        def s5():
            temps = [SQ[:, 0, :], SQ[:, 1, :], RR, ACC]
            temp_free = [[sq_free[0], sq_free[1], acc_free[0]] for _ in range(4)]
            c_done = [None] * 3
            bY = None

            def f4(x):
                return x.rearrange("p (c t) -> p c t", t=P)

            def tables(t16):
                return bc(TC[:, t16, :], 1, [P, 4, P]), bc(TSN[:, t16, :], 1, [P, 4, P])

            def drive(b, j):
                t16 = 2 * b + j
                y4, rows = t16 // 4, slice(32 * (t16 % 4), 32 * (t16 % 4) + 32)
                bR = take()
                tR = mm(PS[bR][:, :], SBr[rows, y4, :], U[rows, y4, :], True, True, ut[y4], t_sb, sig=True)
                bI = take()
                tI = mm(PS[bI][:, :], SBi[rows, y4, :], U[rows, y4, :], True, True, sig=True)
                vr, vi = V_[b % 3][0][:, j, :], V_[b % 3][1][:, j, :]
                c4, s4 = tables(t16)
                k1, k2 = 2 * j, 2 * j + 1
                t1, t2 = temps[k1], temps[k2]
                d1 = TT(dve, f4(vr), f4(PS[bR][:, :]), c4, M_, tR, c_done[b % 3], t_s5, t_pre)
                d2 = TT(dve, f4(t1), f4(PS[bI][:, :]), s4, M_, tI, temp_free[k1])
                d3 = TT(dve, f4(vi), f4(PS[bI][:, :]), c4, M_)
                d4 = TT(dve, f4(t2), f4(PS[bR][:, :]), s4, M_, temp_free[k2])
                give(bR, d4)
                give(bI, d3)
                e1 = TT(pool, vr, vr, t1, A_, d1, d2)
                e2 = TT(pool, vi, vi, t2, S_, d3, d4)
                temp_free[k1], temp_free[k2] = [e1], [e2]
                return e1, e2

            def scan(b, c, vt, carry):
                cols = slice(P * c, P * c + P)
                for j in range(2):
                    rho = RHO[:, 2 * b + j:2 * b + j + 1].to_broadcast([P, P])
                    for z in range(2):
                        v = V_[b % 3][z][:, j, cols]
                        ini = 0.0 if c == 0 else E3[:, z, j:j + 1]
                        sc = dve(lambda e, v=v, rho=rho, ini=ini: e.tensor_tensor_scan(
                            out=v, data0=rho, data1=v, initial=ini, op0=M_, op1=A_), vt[j][z], carry)
                if c == 3:
                    return sc, None
                lr_, li_ = V_[b % 3][0][:, :, P * c + P - 1], V_[b % 3][1][:, :, P * c + P - 1]
                ce, se = TC[:, 2 * b:2 * b + 2, P - 1], TSN[:, 2 * b:2 * b + 2, P - 1]
                TT(dve, E1[:, 0, :], lr_, ce, M_, sc)
                TT(dve, E1[:, 1, :], lr_, se, M_)
                TT(dve, E2[:, 0, :], li_, se, M_)
                t = TT(dve, E2[:, 1, :], li_, ce, M_)
                TT(dve, E3[:, 0, :], E1[:, 0, :], E2[:, 0, :], S_, t)
                return sc, TT(dve, E3[:, 1, :], E1[:, 1, :], E2[:, 1, :], A_)

            def back(b, j, sc):
                vr, vi = V_[b % 3][0][:, j, :], V_[b % 3][1][:, j, :]
                c4, s4 = tables(2 * b + j)
                k1, k2 = 2 * j, 2 * j + 1
                t1, t2 = temps[k1], temps[k2]
                d1 = TT(pool, f4(t1), f4(vr), s4, M_, sc, temp_free[k1])
                d2 = TT(pool, f4(t2), f4(vi), s4, M_, temp_free[k2])
                d3 = TT(pool, f4(vr), f4(vr), c4, M_, d1)
                d4 = TT(pool, f4(vi), f4(vi), c4, M_, d2)

                def add():
                    e1 = TT(dve, vr, vr, t2, S_, d3)
                    e2 = TT(dve, vi, vi, t1, A_, d4)
                    temp_free[k1], temp_free[k2] = [e2], [e1]
                    return e1, e2
                return add

            def read(b, done):
                nonlocal bY
                y4 = b // 2
                if b % 2 == 0:
                    bY = take()
                for j in range(2):
                    t16 = 2 * b + j
                    r = 32 * (t16 % 4)
                    o = PS[bY][r:r + 32, :]
                    mm(o, CpR[:, t16, :], V_[b % 3][0][:, j, :], True, False, done[j][0])
                    tY = mm(o, CpI[:, t16, :], V_[b % 3][1][:, j, :], False, True, done[j][1], sig=True)
                c_done[b % 3] = tY
                if b % 2:
                    ot[4 + y4] = STT(U[:, y4, :], U[:, y4, :], vec("s5_d", y4), PS[bY][:, :], M_, A_, tY)
                    give(bY, ot[4 + y4])

            vt, adds = {}, {}
            for b in range(-1, 9):
                carry = None
                for c in range(4) if 0 <= b < 8 else (2,):
                    if c == 2:
                        done = [add() for add in adds.pop(b - 1, ())]
                        if done:
                            yield
                        if b + 1 < 8:
                            vt[b + 1] = []
                            for j in range(2):
                                vt[b + 1].append(drive(b + 1, j))
                                yield
                        if done:
                            read(b - 1, done)
                            yield
                    if 0 <= b < 8:
                        sc, carry = scan(b, c, vt[b], carry)
                        yield
                if 0 <= b < 8:
                    adds[b] = [back(b, j, sc) for j in range(2)]
            sq_free[0] = temp_free[0] + temp_free[1]
            sq_free[1] = acc_free[0] = sq_free[0] + temp_free[2] + temp_free[3]

        s5g = s5()

        def s5_step(n=1):
            for _ in range(n):
                next(s5g, None)

        def rope(b, t, dst, scale, q):
            a = STT(TMP[:, q, :], PS[b][:, :], scale, RS, M_, M_, t, r, tmp_free[q])
            give(b, a)
            b2 = take()
            t2 = mm(PS[b2][:, :], ROT, TMP[:, q, :], True, True, a, t_const, sig=True)
            p1 = TT(pool, dst, TMP[:, q, :], COS, M_, a, t_pre)
            d = TT(dve, TMP[:, q, :], PS[b2][:, :], SIN, M_, t2, p1)
            give(b2, d)
            d2 = TT(pool, dst, dst, TMP[:, q, :], A_, d)
            tmp_free[q] = [d2]
            return d2

        s5_step(2)
        qt_, kt = [], {}
        names = [("q", 0), ("q", 1), ("q", 2), ("q", 3), ("kc", KC), ("ksl", KSL), ("kw", KW), ("vc", VCT)]
        pend = None
        for i, (nm, dst) in enumerate(names):
            b, t, r = next(tiles)
            if pend is not None:
                pend()
            s5_step(3)
            if nm == "vc":
                a = TT(dve, VCT, PS[b][:, :], RS, M_, t, r, t_pre)
                give(b, a)
                kt["vc"] = a
                pend = None
            elif nm == "q":
                def pend(b=b, t=t, m=dst, i=i):
                    qt_.append(rope(b, t, Q[:, m, :], 0.125, i % 4))
            else:
                def pend(b=b, t=t, d=dst, nm=nm, i=i):
                    kt[nm] = rope(b, t, d, 1.0, i % 4)
        vtt = [None] * 4
        for z in range(2):
            hi, lo, wi, th, tl = wchunk(f"w_inV{z}", None, 8, P + 24 * z)
            for tt in range(4):
                b = take()
                o = PS[b][:, 0:P + 24 * z]
                for k in range(8):
                    xh, xl = HNH[:, k, P * tt:P * tt + P], HNL[:, k, P * tt:P * tt + P]
                    mm(o, xh, hi[:, k, :], k == 0, False, th, xt_mix[k][0])
                    mm(o, xh, lo[:, k, :], False, False, tl)
                    t = mm(o, xl, hi[:, k, :], False, k == 7, xt_mix[k][1], sig=k == 7)
                vtt[tt] = A(act, VT[:, tt, P * z:P * z + P], PS[b][:, 0:P], ACT.Copy, t, t_rt, t_pre, scale=RT[:, tt:tt + 1])
                a2 = vtt[tt]
                if z:
                    a2 = A(act, GX[:, tt, :], PS[b][:, P:P + 24], ACT.Copy, t, scale=RT[:, tt:tt + 1])
                give(b, a2)
                s5_step(2)
            wrelease(wi, t)
        t_z = t
        gt = A(act, GT, GX, ACT.Sigmoid, a2)

        xa_free = None
        hid_free = None
        kc_t = vc_t = None
        for z, (src, tok, pe_name, wname) in enumerate((("kc", kt["kc"], "pe_k", "wk1"), ("vc", kt["vc"], "pe_v", "wv1"))):
            srct = KC if z == 0 else VCT
            lt = []
            for g in range(2):
                lt.append(load(XAp[0:64, g, :], srct[64 * g:64 * g + 64, :], act, tok, xa_free, t_z))
                lt.append(load(XAp[64:128, g, 0:T - 1], srct[64 * g:64 * g + 64, 1:T], act))
            for g in range(2):
                for a_ in range(2):
                    v = XAp[:, g, :].rearrange("p (c r two) -> p r c two", r=8, two=2)[:, :, a_:a_ + 31, 0]
                    xa_free = TT(dve, XBp[:, z, 8 * a_:8 * a_ + 8, g, :], v,
                                 bc(vec(pe_name, 8 * a_, 8), 2, [P, 8, 31]), A_, lt, t_z)
            s5_step(2)
            bs = [take(), take()]
            for c in range(4):
                w, s, wt = chunk(wname, c, (4, 256))
                for mt in range(2):
                    for i in range(4):
                        ii = 4 * c + i
                        t = mm(PS[bs[mt]][:, 0:62], w[:, i, P * mt:P * mt + P],
                               XBp[:, z, ii, :, :].rearrange("p g c -> p (g c)"), ii == 0, ii == 15, wt, xa_free, sig=i == 3)
                release(s, t)
            for mt in range(2):
                hc = A(act, HIDc[:, mt, 0:62], PS[bs[mt]][:, 0:62], ACT.Gelu_apprx_tanh, t, hid_free, t_pre)
                give(bs[mt], hc)
            b = take()
            if z == 0:
                for mt in range(2):
                    t = mm(PS[b][:, 0:62], WK2[:, mt, :], HIDc[:, mt, 0:62], mt == 0, mt == 1, hc, t_wg, sig=mt == 1)
                kc_t = A(act, KCC[:, 0:62], PS[b][:, 0:62], ACT.Copy, t, t_pre)
                give(b, kc_t)
            else:
                for g in range(2):
                    for mt in range(2):
                        t = mm(PS[b][0:31, 64 * g:64 * g + 64], HIDc[:, mt, 31 * g:31 * g + 31], WV2[:, mt, :],
                               mt == 0, mt == 1, hc, t_wg, sig=mt == 1)
                vc_t = A(act, VC[0:31, :], PS[b][0:31, 0:128], ACT.Copy, t, t_pre)
                give(b, vc_t)
            hid_free = t
            s5_step(2)

        cneg = const("cneg").rearrange("p (q c) -> p q c", c=32)
        c01 = const("c01").rearrange("p (q c) -> p q c", c=32)
        cet = []
        for qt in range(4):
            ce = CE[:, qt, :, :].rearrange("p (i f) c -> p f i c", f=2)
            for hf in range(2):
                b = take()
                r = slice(64 * hf, 64 * hf + 64)
                for i in range(4):
                    t = mm(PS[b][:, 32 * i:32 * i + 31], Q[r, i, P * qt:P * qt + P], KCC[r, 31 * hf:31 * hf + 31],
                           True, True, qt_[i], kc_t, sig=i == 3)
                v = PS[b][:, 0:128].rearrange("p (h c) -> p h c", c=32)[:, :, 0:31]
                d = TT(dve, ce[:, hf, :, 0:31], v, bc(cneg[:, qt, 0:31], 1, [P, 4, 31]), A_, t, t_z)
                give(b, d)
        CEa = CEf.rearrange("p (a c) -> p a c", c=32)[:, :, 0:31]
        sh = [P, 32, 31]
        t = dve(lambda e: e.tensor_reduce(CM, CEa, AXX, ALU.max), d)
        t = TT(dve, CEa, CEa, bc(CM, 2, sh), S_, t)
        t = A(act, CEa, CEa, ACT.Exp, t)
        for qt in range(4):
            t2 = TT(dve, CE[:, qt, :, 0:31], CE[:, qt, :, 0:31], bc(c01[:, qt, 0:31], 1, [P, 8, 31]), M_, t)
        t = dve(lambda e: e.tensor_reduce(CS, CEa, AXX, A_), t2)
        t = TS(dve, CS, CS, 1e-30, None, ALU.max, None, t)
        t = RECIP(CS, CS, t)
        CS4 = CS.rearrange("p (q h) -> p q h", h=8)
        t = TT(dve, CS4, CS4, GT[:, :, 0:8], M_, t, gt)
        ce_t = TT(dve, CEa, CEa, bc(CS, 2, sh), M_, t)
        s5_step(2)

        xb_done = pe.last
        pt_free = [[xb_done], [xb_done]]
        ptc_free = [None, None]
        p_free = [[xa_free] for _ in range(4)]
        unit = [0]
        bOs = {}

        def compressed(i):
            for hf in range(2):
                b = take()
                for qt in range(4):
                    t = tr(PS[b][0:31, P * qt:P * qt + P], CE[:, qt, 2 * i + hf, 0:31], IDENT, ce_t, t_const, sig=qt == 3)
                a = A(act, PTC[0:31, hf, :], PS[b][0:31, :], ACT.Copy, t, ptc_free[hf], t_z)
                give(b, a)
                yield
                ptc_free[hf] = mm(PS[bOs[i]][64 * hf:64 * hf + 64, :], VC[0:31, 64 * hf:64 * hf + 64], PTC[0:31, hf, :],
                                  False, True, a, vc_t, sig=True)

        def scores(i, kind, qt, hf):
            nk = P * (qt + 1)
            r = slice(64 * hf, 64 * hf + 64)
            K_ = KSL if kind == 1 else KW
            b = take()
            t = mm(PS[b][:, 0:nk], Q[r, i, P * qt:P * qt + P], K_[r, 0:nk], True, True,
                   kt["ksl"], kt["kw"], qt_[i], sig=True)
            u = unit[0] % 4
            unit[0] += 1
            st = ST4[:, u, :]
            d = TT(dve, PS[b][:, nk - P:nk], PS[b][:, nk - P:nk], const("causal"), A_, t)
            d = dve(lambda e: e.tensor_reduce(st[:, 0:1], PS[b][:, 0:nk], AXX, ALU.max, negate=True), d, p_free[u])
            a = A(act, PB[:, u, 0:nk], PS[b][:, 0:nk], ACT.Exp, d, p_free[u], bias=st[:, 0:1], accum_out=st[:, 1:2])
            give(b, a)

            def scale():
                d = RECIP(st[:, 2:3], st[:, 1:2], a)
                d = TT(dve, st[:, 3:4], st[:, 2:3], GT[:, qt, 8 * kind + 2 * i + hf:8 * kind + 2 * i + hf + 1], M_, d, gt)
                return TS(dve, PB[:, u, 0:nk], PB[:, u, 0:nk], st[:, 3:4], None, M_, None, d)
            return u, scale

        def flip(i, kind, qt, hf, u, tok):
            b = take()
            for kb in range(qt + 1):
                t = tr(PS[b][:, P * kb:P * kb + P], PB[:, u, P * kb:P * kb + P], IDENT, tok, sig=kb == qt)
            p_free[u] = [t]
            a = A(act, PT[:, hf, 0:qt + 1, P * qt:P * qt + P],
                  PS[b][:, 0:P * (qt + 1)].rearrange("p (k t) -> p k t", t=P), ACT.Copy, t, pt_free[hf])
            give(b, a)
            return a

        def values(i, kind, hf, a):
            if i not in bOs:
                bOs[i] = take()
            for kb in range(4):
                t = mm(PS[bOs[i]][64 * hf:64 * hf + 64, P * kb:T], VT[:, kb, P * (kind - 1) + 64 * hf:P * (kind - 1) + 64 * hf + 64],
                       PT[:, hf, kb, P * kb:T], kind == 1 and kb == 0, False, a, vtt[kb], sig=kb == 3)
            pt_free[hf] = [t]

        scaled, turned, todo = [], [], []
        work = [(i, kind, qt, hf) for i in range(4) for kind in (1, 2) for qt in range(4) for hf in range(2)]
        closing = []
        for x in work + [None] * 6:
            if x is not None:
                scaled.append((x,) + scores(*x))
            if len(scaled) > 1 or x is None and scaled:
                y, u, scale = scaled.pop(0)
                turned.append((y, u, scale()))
            if len(turned) > 2 or x is None and turned:
                y, u, tok = turned.pop(0)
                todo.append((y, flip(*y, u, tok)))
            if len(todo) > 1 or x is None and todo:
                (i, kind, qt, hf), a = todo.pop(0)
                if qt == 3:
                    values(i, kind, hf, a)
                    if kind == 2 and hf == 1:
                        closing.append((i, compressed(i)))
            if closing:
                i, c = closing[0]
                if next(c, 0) == 0:
                    closing.pop(0)
                    ot[i] = A(act, Q[:, i, :], PS[bOs[i]][:, :], ACT.Copy, ptc_free[0], ptc_free[1])
                    give(bOs[i], ot[i])
            s5_step()
        while closing:
            i, c = closing.pop(0)
            for _ in c:
                pass
            ot[i] = A(act, Q[:, i, :], PS[bOs[i]][:, :], ACT.Copy, ptc_free[0], ptc_free[1])
            give(bOs[i], ot[i])
        s5_step(100)

        for m in range(4):
            ot[4 + m] = A(act, U[:, m, :], U[:, m, :], ACT.Gelu_apprx_tanh, ot[4 + m])
        sg = []
        for m in range(4):
            w, s, wt = chunk("w_glu", m, (4, P))
            b = take()
            t = dense(PS[b][:, :], [w[:, k, :] for k in range(4)], [U[:, k, :] for k in range(4)], wt, ot[4:8])
            release(s, t)
            a = A(act, TMP[:, m, :], PS[b][:, :], ACT.Sigmoid, t, tmp_free[m], bias=vec("b_glu", m))
            give(b, a)
            sg.append(a)
        for m in range(4):
            ot[4 + m] = TT(dve, U[:, m, :], U[:, m, :], TMP[:, m, :], M_, sg[m], t)
            tmp_free[m] = [ot[4 + m]]

        att_done = everyone()
        xt = [None] * KD
        post = next_norm("norm_ffn2", xt, lambda: att_done)
        rhs = [Q[:, i, :] for i in range(4)] + [U[:, i, :] for i in range(4)]
        for m in range(KD):
            w, s, wt = chunk("w_out", m, (8, P))
            b = take()
            t = dense(PS[b][:, :], [w[:, k, :] for k in range(8)], rhs, wt, ot)
            release(s, t)
            HT[m] = TT(dve, H[:, m, :], PS[b][:, :], H[:, m, :], A_, t, HT[m])
            give(b, HT[m])
            post(m)
        xt_ple = [None] * KD
        ffn("w13b", "w2b", xt, next_norm("norm_ple", xt_ple, lambda: x13[0]), pre=[t, att_done])

        WP = ar(0, 2, 1024)
        PT_ = ar(2048, 2, T)
        ACC2 = ar(3072, T)
        t_wp = load(AR[:, 0:2048], D["w_ple"], act, t_pre, att_done)
        t_p = load(PT_, D["pT"], act)
        for m in range(KD):
            b2 = take()
            t2 = dense(PS[b2][:, :], [WP[:, k, P * m:P * m + P] for k in range(2)], [PT_[:, k, :] for k in range(2)], t_wp, [t_p] * 2)
            w = wchunk("w_pg", m, 8)
            b = take()
            t = dense3(PS[b][:, :], w, HNHk, HNLk, xt_ple)
            wrelease(w[2], t)
            r = need_rs()
            q = m % 4
            d = TT(dve, TMP[:, q, :], PS[b][:, :], RS, M_, r, t, tmp_free[q])
            give(b, d)
            a = A(act, TMP[:, q, :], TMP[:, q, :], ACT.Sigmoid, d)
            d = TT(dve, TMP[:, q, :], PS[b2][:, :], TMP[:, q, :], M_, a, t2)
            give(b2, d)
            HT[m] = TT(dve, H[:, m, :], H[:, m, :], TMP[:, q, :], A_, d, HT[m])
            tmp_free[q] = [HT[m]]
            ta = square(m, ACC, HT[m])
            tb = square(m, ACC2, HT[m], vec("norm_final", m))
        ple_done = t

        t = TT(dve, MOD[:, :], MOD[:, :], vec("b_ada"), A_, dve.last)
        for l in range(2):
            t = TS(dve, GS[:, 8 * l:8 * l + 8], MOD[:, 24 * l + 8:24 * l + 16], 1.0, None, A_, None, t)
            t = TT(dve, GS[:, 8 * l:8 * l + 8], GS[:, 8 * l:8 * l + 8], vec("norm_g", 8 * l, 8), M_, t)
        GF = GS[:, 16:24]
        t_mod = TT(dve, GF, GS[:, 0:8], vec("norm_final"), M_, t)

        t1 = colsum(ACC, ta)
        r1, stat_free[0] = rstd(RS, STAT[:, :], 1024.0, t1)
        t2 = colsum(ACC2, tb)
        d = TT(dve, RR, STAT[:, :], RS, M_, t2, r1)
        stat_free[0] = d
        d = TT(dve, RR, RR, RS, M_, d)
        d = TS(dve, RR, RR, 1.0 / 1024, EPS, M_, A_, d)
        a = A(act, RR, RR, ACT.Sqrt, d)
        d = RECIP(RR, RR, a)
        t_rr = TT(dve, RR, RR, RS, M_, d)
        acc_free[0] = [t1, t2]

        for l in range(2):
            if l:
                t1 = colsum(ACC, ta)
                acc_free[0] = t1
                t_rr, stat_free[0] = rstd(RR, STAT[:, :], 1024.0, t1)
            hnt = []
            for k in range(KD):
                gain = GF[:, k:k + 1] if l == 0 else GS[:, 8 + k:9 + k]
                shift = MOD[:, 24 * l + k:24 * l + k + 1]
                q = k % 4
                d = STT(TMP[:, q, :], H[:, k, :], gain, RR, M_, M_, t_rr, t_mod, HT[k], tmp_free[q])
                h = A(act, HNH[:, k, :], TMP[:, q, :], ACT.Identity, d, ple_done, bias=shift)
                d = STT(HNL[:, k, :], TMP[:, q, :], shift, HNH[:, k, :].bitcast(F32), A_, S_, h)
                tmp_free[q] = [d]
                hnt.append((h, d))
            if l == 0:
                for k in range(KD):
                    HT[k] = STT(H[:, k, :], H[:, k, :], vec("norm_final", k), RS, M_, M_, hnt[k][1])
            start = everyone()
            Y = ar(0, 8, T)
            XM = ar(4096, 8, 515)
            XR = ar(4096, 8, T)
            XC = ar(8224, 8, T)
            V2 = ar(8224, 4, 1024)
            Q2 = ar(12320, 8, T)
            K2 = ar(16416, 8, T)
            WIF = ar(20512, 24, 8)
            GV = ar(20704, 8, 8)
            ET = ar(20768, 4, 4)
            t_wif = load(AR[:, 20512:20704], D["w_if"][l], act, start)

            def proj(part, m):
                w = wchunk("w_in2", 40 * l + 8 * part + m, 8)
                b = take()
                t = dense3(PS[b][:, :], w, HNHk, HNLk, hnt)
                wrelease(w[2], t)
                return b, t

            def conv(dst, x, kind, m, *tokens):
                cw = lambda i: vec(kind + "_conv_w", 32 * l + 8 * i + m)
                t = TS(dve, dst, x[:, 3:3 + T], cw(3), vec(kind + "_conv_b", 8 * l + m), M_, A_, *tokens)
                for i in range(3):
                    t = STT(dst, x[:, i:i + T], cw(i), dst, M_, A_, t)
                return t

            RX, IX, CX = Q2, K2, XC
            XP = [AR[:, 1024 * z:1024 * z + 515] for z in range(2)]
            wax = ar(2048, 2, 8, P)
            t_wax = load(AR[:, 2048:4096], D["rg_w"][l], act, start)
            t_xp = [pool(lambda e, x=x: e.memset(x[:, 0:3], 0.0), start) for x in XP][-1]
            t_pad = pool(lambda e: e.memset(XM[:, :, 0:3], 0.0), start)
            xp_free = [[], []]
            rt, itk, ct, yt = [], [], [], []
            pend = []

            def gates(hh, c):
                for z, (dst, bn, lst) in enumerate(((RX, "rg_b_a", rt), (IX, "rg_b_x", itk))):
                    b = take()
                    t = mm(PS[b][:, :], wax[:, z, hh, :], CX[:, hh, :], True, True, c, t_wax, sig=True)
                    a = A(act, dst[:, hh, :], PS[b][:, :], ACT.Sigmoid, t, start, bias=vec(bn, 8 * l + hh))
                    give(b, a)
                    lst.append(a)
                return t

            for hh in range(8):
                b, t = proj(0, hh)
                x = XP[hh % 2]
                a = A(act, x[:, 3:515], PS[b][:, :], ACT.Copy, t, t_xp, xp_free[hh % 2], start)
                give(b, a)
                d = conv(CX[:, hh, :], x, "rg", hh, a, start)
                xp_free[hh % 2] = [d]
                ct.append(d)
                pend.append((hh, d))
                if len(pend) > 1:
                    gates(*pend.pop(0))
            xmt = []
            ax = []
            for m in range(8):
                b, t = proj(2, m)
                if m == 0:
                    t_g = gates(*pend.pop(0))
                a = A(act, XM[:, m, 3:515], PS[b][:, :], ACT.Copy, t, t_pad, start)
                give(b, a)
                xmt.append(a)
                hh = m
                ca = CA[:, 8 * l + hh:8 * l + hh + 1]
                p1 = TT(pool, IX[:, hh, :], IX[:, hh, :], CX[:, hh, :], M_, itk[hh], ct[hh])
                q = hh % 4
                th = A(act, TMP[:, q, :], RX[:, hh, :], ACT.Tanh, rt[hh], t_ca, tmp_free[q], scale=ca)
                a = A(act, RX[:, hh, :], RX[:, hh, :], ACT.Exp, th, scale=ca)
                a2 = A(act, CX[:, hh, :], RX[:, hh, :], ACT.Square, a, p1, t_g)
                d = STT(CX[:, hh, :], CX[:, hh, :], 1.0, TMP[:, q, :], A_, M_, a2)
                tmp_free[q] = [d]
                ax.append((d, p1, a))
            hst = []
            for hh in range(8):
                d, p1, a = ax[hh]
                a2 = A(act, CX[:, hh, :], CX[:, hh, :], ACT.Sqrt, d, scale=-1.0)
                p2 = TT(pool, IX[:, hh, :], IX[:, hh, :], CX[:, hh, :], M_, a2, p1)
                hst.append(dve(lambda e, hh=hh, RX=RX, IX=IX, CX=CX: e.tensor_tensor_scan(
                    out=CX[:, hh, :], data0=RX[:, hh, :], data1=IX[:, hh, :], initial=0.0, op0=M_, op1=A_), p2, a))
            rg_done = [dve.last]
            xct = []
            for m in range(8):
                b, t = proj(1, m)
                q = m % 2
                a = A(act, TMP[:, q, :], PS[b][:, :], ACT.Sigmoid, t, tmp_free[q])
                d = TT(dve, TMP[:, q, :], TMP[:, q, :], PS[b][:, :], M_, a)
                give(b, d)
                d = TT(dve, Y[:, m, :], TMP[:, q, :], CX[:, m, :], M_, d, hst[m], t_g)
                tmp_free[q] = [d]
                yt.append(d)
                d = conv(XC[:, m, :], XM[:, m, :], "ml", m, xmt[m], d)
                q = 2 + m % 2
                a = A(act, TMP[:, q, :], XC[:, m, :], ACT.Sigmoid, d, tmp_free[q])
                tmp_free[q] = [TT(pool, XC[:, m, :], XC[:, m, :], TMP[:, q, :], M_, a)]
                xct.append(tmp_free[q][0])

            qtk, ktk = [], []
            for z, (dst, lst) in enumerate(((Q2, qtk), (K2, ktk))):
                for c in range(2):
                    w, s, wt = chunk("ml_wqk", 4 * l + 2 * z + c, (4, 256))
                    for h in (2 * c, 2 * c + 1):
                        for mt in range(2):
                            m = 2 * h + mt
                            b = take()
                            t = dense(PS[b][:, :], [w[:, 2 * (h % 2) + kk, P * mt:P * mt + P] for kk in range(2)],
                                      [XC[:, 2 * h + kk, :] for kk in range(2)], wt, [xct[2 * h], xct[2 * h + 1]])
                            a = A(act, dst[:, m, :], PS[b][:, :], ACT.Copy, t, rg_done)
                            give(b, a)
                            lst.append(a)
                    release(s, t)
            t_qk = t
            v2t = [[None, None] for _ in range(4)]
            for c in range(2):
                w, s, wt = chunk("ml_wv", 2 * l + c, (4, 256))
                for tt in range(4):
                    b = take()
                    for h in (2 * c, 2 * c + 1):
                        for kk in range(2):
                            t = mm(PS[b][:, 256 * (h % 2):256 * (h % 2) + 256], XM[:, 2 * h + kk, 3 + P * tt:3 + P * tt + P],
                                   w[:, 2 * (h % 2) + kk, :], kk == 0, kk == 1, wt, xmt[2 * h + kk], sig=kk == 1)
                    a = A(act, V2[:, tt, T * c:T * c + T], PS[b][:, :], ACT.Copy, t, t_qk)
                    give(b, a)
                    v2t[tt][c] = a
                release(s, t)
            b = take()
            for c in range(2):
                w, s, wt = chunk("ml_wvT", 2 * l + c, (4, 256))
                for h in (2 * c, 2 * c + 1):
                    for mt in range(2):
                        m = 2 * h + mt
                        for kk in range(2):
                            t = mm(PS[b][:, 8 * m:8 * m + 8], w[:, 2 * (h % 2) + kk, P * mt:P * mt + P], WIF[:, 16 + 2 * h + kk, :],
                                   kk == 0, kk == 1, wt, t_wif, sig=kk == 1)
                release(s, t)
            gv = A(act, GV, PS[b][:, 0:64].rearrange("p (a b) -> p a b", b=8), ACT.Copy, t, start)
            give(b, gv)
            b = take()
            lhs = [WIF[:, k, :] for k in range(16)] + [GV[:, k, :] for k in range(8)]
            rhs = [Q2[:, k, :] for k in range(8)] + [K2[:, k, :] for k in range(8)] + [XM[:, k, 3:515] for k in range(8)]
            t = dense(PS[b][0:8, :], lhs, rhs, t_wif, qtk + ktk + [gv] + xmt[1:])
            t_qkv = t
            GB = XR[0:8, 0, :]
            FE, FC, EE, MM, NM, ZR = (XR[:, i, :] for i in range(1, 7))
            ln_ = XR[:, 7, :]
            a = A(act, GB, PS[b][0:8, :], ACT.Identity, t, t_vec, bias=VEC[0:8, VEC_AT["b_if"][0] + l:VEC_AT["b_if"][0] + l + 1])
            give(b, a)
            bi, bf = take(), take()
            ti = mm(PS[bi][:, :], const("sel_i")[0:8, :], GB, True, True, a, t_const, sig=True)
            tf = mm(PS[bf][:, :], const("sel_f")[0:8, :], GB, True, True, sig=True)
            zt = pool(lambda e: e.memset(ZR, 0.0), t_qkv)
            d = A(act, ln_, PS[bf][:, :], ACT.Abs, tf, t_qkv)
            a = A(act, ln_, ln_, ACT.Exp, d, scale=-1.0)
            a = A(act, ln_, ln_, ACT.Ln, a, bias=1.0)
            d = STT(FE, PS[bf][:, :], 0.0, ln_, ALU.min, S_, a)
            give(bf, d)
            d = dve(lambda e: e.tensor_tensor_scan(out=FC, data0=FE, data1=ZR, initial=0.0, op0=A_, op1=A_), d, zt)
            te = TT(dve, EE, PS[bi][:, :], FC, S_, ti, d)
            give(bi, te)
            d = dve(lambda e: e.tensor_tensor_scan(out=MM, data0=EE, data1=ZR, initial=0.0, op0=ALU.max, op1=ALU.max), te)
            nmt = TS(dve, NM, MM, -1.0, None, M_, None, d)
            mt_ = TT(dve, MM, MM, FC, A_, nmt)
            b = take()
            for j in range(4):
                t = tr(PS[b][:, P * j:P * j + P], EE[:, P * j:P * j + P], IDENT, te, sig=j == 3)
            et = A(act, ET, PS[b][:, :].rearrange("p (j h x) -> p j h x", j=4, h=4)[:, :, :, 0], ACT.Copy, t, start)
            give(b, et)

            WB = [XR[:, 0, :], XR[:, 1, :]]
            SBF = [XR[:, 6, :], XR[:, 7, :]]
            wb_free = [[nmt, ti, tf], [nmt]]
            s_free = [[d, zt, nmt], [nmt]]
            n = 0
            cellt = []
            for h in range(4):
                r = slice(32 * h, 32 * h + 1)
                bM, bE = take(), take()
                tM = mm(PS[bM][:, :], const("ones")[r, :], NM[r, :], True, True, nmt, sig=True)
                tE = mm(PS[bE][:, :], const("ones")[r, :], MM[r, :], True, True, mt_, sig=True)
                em = A(act, TMP[:, 2, :], PS[bE][:, :], ACT.Exp, tE, tmp_free[2], scale=-1.0)
                give(bE, em)
                bD, bN0, bN1 = take(), take(), take()
                jobs = []

                def score(j):
                    b = take()
                    for kk in range(2):
                        t = mm(PS[b][:, P * j:T], K2[:, 2 * h + kk, P * j:P * j + P], Q2[:, 2 * h + kk, P * j:T], kk == 0, kk == 1,
                               qtk[2 * h + kk], ktk[2 * h + kk], sig=kk == 1)
                    q = (4 * h + j) % 2
                    diag = WB[q][:, P * j:P * j + P]
                    d = TS(dve, diag, PS[bM][:, P * j:P * j + P], ET[:, j, h:h + 1], 0.0, A_, ALU.min, tM, et, wb_free[q])
                    a = A(act, diag, diag, ACT.Exp, d)
                    a0 = a
                    if j < 3:
                        a0 = A(act, WB[q][:, P * j + P:T], PS[bM][:, P * j + P:T], ACT.Exp, tM, et, wb_free[q], bias=ET[:, j, h:h + 1])
                    p = pool(lambda e: e.affine_select(out=WB[q][:, P * j:P * j + P], in_=WB[q][:, P * j:P * j + P],
                                                       compare_op=ALU.is_ge, fill=0.0, base=0, pattern=[[1, P]],
                                                       channel_multiplier=-1), a)
                    a = [a0, d]
                    d = STT(SBF[q][:, P * j:T], PS[b][:, P * j:T], 1.0 / 16, WB[q][:, P * j:T], M_, M_, t, p, a0, s_free[q])
                    wb_free[q] = [d]
                    give(b, d)
                    return j, q, d, a

                def reduce_(j, q, d, a):
                    x = SBF[q][:, P * j:T]
                    mm(PS[bD][:, P * j:T], ONES, x, j == 0, j == 3, d)
                    mm(PS[bN0][:, P * j:T], V2[:, j, 256 * h:256 * h + P], x, j == 0, j == 3, v2t[j][h // 2])
                    t = mm(PS[bN1][:, P * j:T], V2[:, j, 256 * h + P:256 * h + 256], x, j == 0, j == 3, sig=True)
                    s_free[q] = [t]
                    return t

                for j in range(4):
                    jobs.append(score(j))
                    if j:
                        reduce_(*jobs.pop(0))
                give(bM, jobs[0][3])
                t = reduce_(*jobs.pop(0))
                ab = A(act, TMP[:, 3, :], PS[bD][:, :], ACT.Abs, t, tmp_free[3])
                give(bD, ab)
                d = TT(dve, TMP[:, 2, :], TMP[:, 2, :], TMP[:, 3, :], ALU.max, ab, em)
                tmp_free[3] = [d]
                d = RECIP(TMP[:, 2, :], TMP[:, 2, :], d)
                for z, bN in enumerate((bN0, bN1)):
                    d = TT(dve, Q2[:, 2 * h + z, :], PS[bN][:, :], TMP[:, 2, :], M_, d, t)
                    give(bN, d)
                    cellt.append(d)
                tmp_free[2] = [d]
            cells_done = pe.last

            yp = []
            for m in range(8):
                h = A(act, YRH[:, m, :], Y[:, m, :], ACT.Copy, yt[m], cells_done)
                yp.append((h, TT(dve, YRL[:, m, :], Y[:, m, :], YRH[:, m, :].bitcast(F32), S_, h)))

            hst, zt_ = [], []
            RH = XR
            rht = []
            sqt = [None, None]
            for h in range(4):
                for j in range(2):
                    m = 2 * h + j
                    b, t = proj(3, m)
                    q = m % 2
                    a = A(act, TMP[:, q, :], PS[b][:, :], ACT.Sigmoid, t, tmp_free[q])
                    give(b, a)
                    p = TT(pool, Q2[:, m, :], Q2[:, m, :], TMP[:, q, :], M_, a, cellt[m], cells_done)
                    tmp_free[q] = [p]
                    hst.append(p)
                s0 = A(act, SQ[:, 0, :], Q2[:, 2 * h, :], ACT.Square, hst[2 * h], sq_free[0], sqt[0])
                s1 = A(act, SQ[:, 1, :], Q2[:, 2 * h + 1, :], ACT.Square, hst[2 * h + 1], sq_free[1], sqt[0])
                p = TT(pool, SQ[:, 0, :], SQ[:, 0, :], SQ[:, 1, :], A_, s0, s1)
                for j in range(2):
                    m = 2 * h + j
                    b, t = proj(4, m)
                    a = A(act, K2[:, m, :], PS[b][:, :], ACT.Sigmoid, t, cells_done)
                    d = TT(dve, K2[:, m, :], K2[:, m, :], PS[b][:, :], M_, a)
                    give(b, d)
                    zt_.append(d)
                b = take()
                sqt[0] = mm(PS[b][:, :], ONES, SQ[:, 0, :], True, True, p, sig=True)
                d = TS(dve, RH[:, h, :], PS[b][:, :], 1.0 / 256, EPS, M_, A_, sqt[0], cells_done)
                give(b, d)
                rht.append(d)
            sq_free = [sqt[0], sqt[0]]
            proj_done = pe.last
            for h in range(4):
                a = A(act, RH[:, h, :], RH[:, h, :], ACT.Sqrt, rht[h])
                d = RECIP(RH[:, h, :], RH[:, h, :], a)
                for j in range(2):
                    m = 2 * h + j
                    d2 = STT(Q2[:, m, :], Q2[:, m, :], vec("ml_norm_g", 8 * l + m), RH[:, h, :], M_, M_, d, sqt[0])
                    d2 = TT(dve, Q2[:, m, :], Q2[:, m, :], K2[:, m, :], M_, d2, zt_[m])
                    hi = A(act, HNH[:, m, :], Q2[:, m, :], ACT.Copy, d2, proj_done)
                    yp.append((hi, TT(dve, HNL[:, m, :], Q2[:, m, :], HNH[:, m, :].bitcast(F32), S_, hi)))
            yh = [YRH[:, k, :] for k in range(8)] + HNHk
            yl = [YRL[:, k, :] for k in range(8)] + HNLk
            for m in range(KD):
                b = take()
                for c in range(2):
                    w = wchunk("w_out2", 16 * l + 2 * m + c, 8)
                    t = dense3(PS[b][:, :], w, yh, yl, yp, 8 * c, 8, c == 0, c == 1)
                    wrelease(w[2], t)
                HT[m] = STT(H[:, m, :], PS[b][:, :], MOD[:, 24 * l + 16 + m:24 * l + 17 + m], H[:, m, :], M_, A_, t, HT[m])
                give(b, HT[m])
                ta = square(m, ACC, HT[m])
            ple_done = t

        t1 = colsum(ACC, ta)
        r1, _ = rstd(RS, STAT[:, :], 1024.0, t1)
        OUT = ar(0, 8, T)
        HT = [STT(OUT[:, k, :], H[:, k, :], vec("final_g", k), RS, M_, M_, r1, everyone()) for k in range(KD)]
        nout = 0
        for c in range(4):
            sp.wait(HT[2 * c], HT[2 * c + 1])
            sp.ops.append(lambda e, c=c: e.dma_start(out[:, 2 * c:2 * c + 2, :], OUT[:, 2 * c:2 * c + 2, :]).then_inc(s_out, 16))
            nout += 16
        sp.ops.append(lambda e: e.wait_ge(s_out, nout))

        block = ctx.enter_context(nc.Block())

        def play(q):
            def run(e):
                for op in q.ops:
                    op(e)
            return run

        block.sync(play(sp))
        block.scalar(play(act))
        block.vector(play(dve))
        block.gpsimd(play(pool))
        block.tensor(play(pe))


def _tiles(w, mc):
    k, m = w.shape
    return np.ascontiguousarray(w.reshape(k // P, P, m // mc, mc).transpose(2, 1, 0, 3).reshape(m // mc, P, -1))


def _cols(v):
    return v.reshape(-1, P).T


def _consts():
    half = 32
    inv = (np.float32(10000.0) ** (-np.arange(half, dtype=np.float32) / np.float32(half))).astype(np.float32)
    ang = (np.arange(T, dtype=np.float32)[:, None] * inv[None, :]).astype(np.float64)
    cos, sin = np.cos(ang).T, np.sin(ang).T
    c = {}
    c["cos"] = np.tile(cos, (4, 1))
    c["sin"] = np.concatenate([-sin, sin, -sin, sin], 0)
    c["ident"] = np.eye(P)
    c["ones"] = np.ones((P, P))
    c["rot"] = np.eye(P)[np.arange(P) ^ 32]
    i = np.arange(P)
    c["causal"] = np.where(i[None, :] <= i[:, None], 0.0, NEG)
    tok = np.arange(4)[None, :, None] * P + i[:, None, None]
    end = np.arange(32)[None, None, :] * 16 + 31
    ok = (end <= tok) & (np.arange(32)[None, None, :] < 31)
    c["cneg"] = np.where(ok, 0.0, NEG).reshape(P, 128)
    c["c01"] = ok.astype(np.float32).reshape(P, 128)
    for z, n in enumerate(("sel_i", "sel_f")):
        s = np.zeros((P, P))
        for h in range(4):
            s[4 * z + h, 32 * h] = 1.0
        c[n] = s
    return np.ascontiguousarray(np.concatenate([c[n] for n, _ in CONST_COLS], 1).astype(np.float32))


def _layout(I):
    f = np.float32
    A = {}
    A["xT"] = np.ascontiguousarray(I["x"][0].T.reshape(8, P, T).transpose(1, 0, 2))
    A["pT"] = np.ascontiguousarray(I["p"][0, 0].T.reshape(2, P, T).transpose(1, 0, 2))
    for z, n in (("a", "ffn1"), ("b", "ffn2")):
        w1, w3 = (_tiles(I[f"{n}_w{k}"][0], P) for k in (1, 3))
        A["w13" + z] = np.ascontiguousarray(np.stack([w1, w3], 1).reshape(44, P, 1024))
        w2 = I[f"{n}_w2"][0]
        A["w2" + z] = np.concatenate([_tiles(w2[1408 * k:1408 * k + 1408], P) for k in range(2)], 0)
    perm = np.concatenate([h * 64 + np.arange(64) for i in range(4) for h in (i, 4 + i)])
    heads = [h for i in range(4) for h in (i, 4 + i)]
    w = I["w_in"][0]
    part = lambda k: w[:, 512 + 128 * k:640 + 128 * k]
    A["w_inA"] = _tiles(np.concatenate([w[:, 1304:1816], w[:, perm], part(0), part(2), part(4), part(1)], 1), P)
    wg = w[:, 1280:1304].reshape(1024, 8, 3)[:, heads, :].transpose(0, 2, 1).reshape(1024, 24)
    A["w_inV0"] = _tiles(part(3), P)[0]
    A["w_inV1"] = _tiles(np.concatenate([part(5), wg], 1), P + 24)[0]
    wk2 = I["cmp_wk2"][0]
    A["small_w"] = np.ascontiguousarray(np.concatenate(
        [_tiles(np.concatenate([wk2, wk2], 1), P)[0], _tiles(I["cmp_wv2"][0], 64)[0]], 1))
    for n in ("wk1", "wv1"):
        a = I["cmp_" + n][0]
        A[n] = np.concatenate([_tiles(a[512 * k:512 * k + 512], 256) for k in range(4)], 0)
    bc = np.zeros((P, 2048), f)
    for z, n in enumerate(("s5_b_re", "s5_b_im")):
        b = I[n][0]
        for g in range(32):
            y4, j, g2 = g // 8, (g % 8) // 2, g % 2
            bc[32 * j + 16 * g2:32 * j + 16 * g2 + 16, 512 * z + P * y4 + 64 * g2:512 * z + P * y4 + 64 * g2 + 64] = b[g].T
    for z, n in enumerate(("s5_c_re", "s5_c_im")):
        c = I[n][0]
        for g in range(32):
            t, g2 = g // 2, g % 2
            at = 1024 + 512 * z + 32 * t + 16 * g2
            bc[64 * g2:64 * g2 + 64, at:at + 16] = c[g].T
    A["s5_bc"] = bc
    A["w_glu"] = _tiles(I["s5_w_glu"][0], P)
    wo = I["w_out"][0]
    A["w_out"] = _tiles(np.concatenate([wo[:512][perm], wo[512:]], 0), P)
    A["w_pg"] = _tiles(I["w_ple_gate"][0], P)
    A["w_ple"] = _tiles(I["w_ple"][0], 1024)[0]
    A["c"] = np.ascontiguousarray(I["c_2"].reshape(1024))
    wa = np.concatenate([I["w_ada_2"][l].T.reshape(24, P, 1024) for l in range(2)], 0)
    A["w_ada"] = np.ascontiguousarray(wa)
    A["w_in2"] = np.concatenate([_tiles(I["w_in_2"][l], P) for l in range(2)], 0)
    A["rg_w"] = np.ascontiguousarray(np.stack([np.concatenate(
        [I[n][l].transpose(1, 0, 2).reshape(P, 1024) for n in ("rg_w_a_2", "rg_w_x_2")], 1) for l in range(2)]))

    def heads4(a):
        return a.reshape(2, 4, P, 256).transpose(0, 2, 1, 3).reshape(2, P, 1024)
    A["ml_wqk"] = np.ascontiguousarray(np.concatenate([heads4(I[n][l]) for l in range(2) for n in ("ml_w_q_2", "ml_w_k_2")]))
    A["ml_wv"] = np.ascontiguousarray(np.concatenate([heads4(I["ml_w_v_2"][l]) for l in range(2)]))
    A["ml_wvT"] = np.ascontiguousarray(np.concatenate([heads4(I["ml_w_v_2"][l].transpose(0, 2, 1)) for l in range(2)]))
    A["w_if"] = np.ascontiguousarray(np.stack([I["ml_w_if_2"][l].reshape(24, P, 8).transpose(1, 0, 2).reshape(P, 192) for l in range(2)]))
    A["w_out2"] = np.concatenate([_tiles(I["w_out_2"][l], P).reshape(8, P, 2, 1024).transpose(0, 2, 1, 3).reshape(16, P, 1024)
                                  for l in range(2)], 0)
    two = lambda a: np.concatenate([_cols(a[l]) for l in range(2)], 1)
    conv = lambda a: np.concatenate([_cols(a[l, i]) for l in range(2) for i in range(4)], 1)
    bif = np.zeros((P, 2), f)
    bif[0:8, :] = I["ml_b_if_2"].T
    V = {
        "norm_ffn1": _cols(I["norm_ffn1"][0]), "norm_mix": _cols(I["norm_mix"][0]), "norm_ffn2": _cols(I["norm_ffn2"][0]),
        "norm_ple": _cols(I["norm_ple"][0]), "norm_final": _cols(I["norm_final"]),
        "a_re": _cols(I["s5_a_re"][0]), "a_im": _cols(I["s5_a_im"][0]), "log_dt": _cols(np.repeat(I["s5_log_dt"][0], 64)),
        "s5_d": _cols(I["s5_d"][0]), "b_glu": _cols(I["s5_b_glu"][0]), "pe_k": _cols(I["cmp_pe_k"][0]), "pe_v": _cols(I["cmp_pe_v"][0]),
        "norm_g": two(I["norm_g_2"]), "b_ada": two(I["b_ada_2"]),
        "rg_conv_w": conv(I["rg_conv_w_2"]), "rg_conv_b": two(I["rg_conv_b_2"]), "rg_b_a": two(I["rg_b_a_2"]), "rg_b_x": two(I["rg_b_x_2"]),
        "rg_lam": two(I["rg_lambda_2"]), "ml_conv_w": conv(I["ml_conv_w_2"]), "ml_conv_b": two(I["ml_conv_b_2"]),
        "ml_norm_g": two(I["ml_norm_g_2"]), "final_g": _cols(I["final_g_2"]), "b_if": bif,
    }
    A["vecs"] = np.ascontiguousarray(np.concatenate([V[n] for n, _ in VEC_COLS], 1))
    A["consts"] = _consts()
    return A


def kernel(**inputs):
    import concourse.bacc as bacc
    from concourse.bass_utils import run_bass_kernel_spmd

    I = {k: np.asarray(v) for k, v in inputs.items()}
    nc = bacc.Bacc("TRN2", target_bir_lowering=False, num_devices=1)
    arrays, D = {}, {}
    for name, a in _layout(I).items():
        arrays[f"in_{name}"] = a
        D[name] = nc.dram_tensor(f"in_{name}", a.shape, mybir.dt.from_np(a.dtype), kind="ExternalInput").ap()
    out = nc.dram_tensor("out_0", (P, 8, T), F32, kind="ExternalOutput").ap()
    program(nc, D, out)
    r = run_bass_kernel_spmd(nc, [arrays], core_ids=[0])
    o = r.results[0]["out_0"]
    return np.ascontiguousarray(o.transpose(1, 0, 2).reshape(1024, T).T)[None]
```

```python
from contextlib import ExitStack

import numpy as np

import concourse.bass as bass
from concourse import mybir

ALU = mybir.AluOpType
ACT = mybir.ActivationFunctionType
F32 = mybir.dt.float32
F32R = mybir.dt.float32r
AXX = mybir.AxisListType.X

P = 128
T = 512
KD = 8
NEG = -1e30
EPS = 1e-6

VEC_COLS = [
    ("norm_ffn1", 8), ("norm_mix", 8), ("norm_ffn2", 8), ("norm_ple", 8), ("norm_final", 8),
    ("a_re", 16), ("a_im", 16), ("log_dt", 16), ("s5_d", 4), ("b_glu", 4), ("pe_k", 16), ("pe_v", 16),
    ("norm_g", 16), ("b_ada", 48), ("rg_conv_w", 64), ("rg_conv_b", 16), ("rg_b_a", 16), ("rg_b_x", 16),
    ("rg_lam", 16), ("ml_conv_w", 64), ("ml_conv_b", 16), ("ml_norm_g", 16), ("final_g", 8), ("b_if", 2),
]
VEC_AT = {}
_n = 0
for _name, _w in VEC_COLS:
    VEC_AT[_name] = (_n, _w)
    _n += _w
NVEC = _n

CONV_AT = {3: (0, 1), 4: (2, 3), 5: (4,), 6: (5,), 10: (6,), 11: (7,)}

CONST_COLS = [("cos", T), ("sin", T), ("ident", P), ("ones", P), ("rot", P), ("causal", P),
              ("cneg", 128), ("c01", 128), ("sel_i", P), ("sel_f", P)]
CONST_AT = {}
_n = 0
for _name, _w in CONST_COLS:
    CONST_AT[_name] = (_n, _w)
    _n += _w
NCONST = _n


def adas(half, i):
    if half == 0:
        return 0 if i < 2 else 2 if i < 11 else 1
    return 2 if i < 11 else 0


def out2_order():
    return [(m, c) for c in range(2) for m in range(5)] + [(m, c) for m in range(5, 8) for c in range(2)]


def plan():
    out = []

    def ffn(z):
        for half in range(2):
            for mi in range(11):
                out.extend(("w13" + z, (half * 11 + mi) * 2 + x, 1024, True) for x in range(2))
            out.extend(("w2" + z, half * 8 + m, 1408, True) for m in range(8))

    ffn("a")
    out.extend(("w_inA", c, 1024, True) for c in range(8))
    for c in range(4):
        out.extend([("w_inA", 8 + c, 1024, True), ("wk1", c, 1024, False)])
    out.extend(("w_inV", z, 1120, True) for z in range(2))
    out.extend(("wv1", c, 1024, False) for c in range(4))
    out.extend(("w_glu", m, 512, False) for m in range(4))
    out.extend(("w_out", m, 1024, True) for m in range(8))
    ffn("b")
    out.extend(("w_pg", m, 1024, True) for m in range(8))
    for l in range(2):
        for part in (0, 2, 1):
            out.extend(("w_in2", 40 * l + 8 * part + m, 1024, True) for m in range(8))
        out.extend(("ml_wqk", 4 * l + c, 1024, True) for c in (0, 2, 1, 3))
        out.extend(("ml_wv", 2 * l + c, 1024, False) for c in range(2))
        out.extend(("ml_wvT", 2 * l + c, 1024, False) for c in range(2))
        out.extend(("w_in2", 40 * l + 8 * part + m, 1024, True) for part in (3, 4) for m in range(8))
        out.extend(("w_out2", 16 * l + 2 * m + c, 1024, True) for m, c in out2_order())
    return out


class Queue:

    def __init__(self, sem):
        self.sem, self.n, self.ops, self.seen = sem, 0, [], {}

    def wait(self, *tokens):
        for t in tokens:
            if t is None:
                continue
            if isinstance(t, list):
                self.wait(*t)
                continue
            sem, value = t
            if self.seen.get(id(sem), 0) < value:
                self.seen[id(sem)] = value
                self.ops.append(lambda e, s=sem, v=value: e.wait_ge(s, v))

    def __call__(self, fn, *tokens, sig=True):
        self.wait(*tokens)
        if sig:
            self.n += 1
            self.ops.append(lambda e: fn(e).then_inc(self.sem, 1))
            return (self.sem, self.n)
        self.ops.append(fn)
        return None

    @property
    def last(self):
        return (self.sem, self.n)


def program(nc, D, out):
    ctx = ExitStack()
    with ctx:
        def sem(name):
            return ctx.enter_context(nc.semaphore(name))

        at = [0]
        base = (nc.sbuf_base + 31) // 32 * 32

        def place(name, offset, n, dt=F32):
            return nc.alloc_sbuf_tensor_at(name, [P, n], dt, offset=base + 4 * offset)

        def sb(name, n, dt=F32):
            at[0] += (n + 7) // 8 * 8
            return place(name, at[0] - (n + 7) // 8 * 8, n, dt)

        def tiles_(t):
            return t[:, :].rearrange("p (k t) -> p k t", t=T)

        H = tiles_(sb("H", KD * T))
        at_hn = at[0]
        HNH, HNL = tiles_(sb("HNH", KD * T, F32R)), tiles_(sb("HNL", KD * T, F32R))
        HX = place("HX", at_hn, 2 * KD * T)
        at_tmp = at[0]
        TMP = tiles_(sb("TMP", 4 * T))
        SQ = tiles_(sb("SQ", 2 * T))
        ACC = sb("ACC", T)[:, :]
        TMPH = tiles_(place("TMPH", at_tmp, 7 * T, F32R))
        RSf = sb("RS", 2 * T)
        RS, RR = RSf[:, 0:T], RSf[:, T:2 * T]
        CONST = sb("CONST", NCONST)
        VEC = sb("VEC", NVEC)
        MOD = sb("MOD", 48)
        GS = sb("GS", 40)
        TOK = sb("TOK", 16)[:, :]
        LA = sb("LA", 6 * 16)
        NAR = 20800
        at_ar = at[0]
        AR = sb("AR", NAR)
        NSLOT, SLOT = 3, 1408
        RAW = sb("RAW", NSLOT * SLOT)
        NW = 3
        WHI, WLO = sb("WHI", NW * SLOT, F32R), sb("WLO", NW * SLOT, F32R)
        assert base + 4 * at[0] <= 229344, at[0]
        HIDH, HIDL = tiles_(place("HIDH", at_ar + 7168, 11 * T, F32R)), tiles_(place("HIDL", at_ar + 7168 + 11 * T, 11 * T, F32R))
        YRH, YRL = tiles_(place("YRH", at_ar, 8 * T, F32R)), tiles_(place("YRL", at_ar + 8224, 8 * T, F32R))
        OH, OL = tiles_(place("OH", at_ar, 8 * T, F32R)), tiles_(place("OL", at_ar + 15360, 8 * T, F32R))
        PS = [ctx.enter_context(nc.psum_tensor(f"PS{b}", [P, T], F32)) for b in range(8)]

        def const(name):
            a, w = CONST_AT[name]
            return CONST[:, a:a + w]

        def vec(name, i=None, n=1):
            a, w = VEC_AT[name]
            return VEC[:, a:a + w] if i is None else VEC[:, a + i:a + i + n]

        COS, SIN, IDENT, ONES, ROT = (const(n) for n in ("cos", "sin", "ident", "ones", "rot"))

        pe, act, dve, pool = (Queue(sem(f"s_{n}")) for n in ("pe", "act", "dve", "pool"))
        sp = Queue(sem("s_sp"))
        s_out = sem("s_out")

        slot_sem = [sem(f"s_slot{i}") for i in range(NSLOT)]
        slot_free = [[] for _ in range(NSLOT)]
        w_free = [[] for _ in range(NW)]
        order = plan()
        got = []
        asked = [0]
        nsplit = [0]

        def fetch():
            k = len(got)
            name, i, n, split = order[k]
            s = k % NSLOT
            assert slot_free[s] is not None, (k, name)
            src = D[name] if i is None else D[name][i]
            raw = RAW[:, s * SLOT:s * SLOT + n]
            sp.wait(slot_free[s])
            slot_free[s] = None
            sp.ops.append(lambda e: e.dma_start(raw, src).then_inc(slot_sem[s], 16))
            tok = (slot_sem[s], 16 * (k // NSLOT + 1))
            if not split:
                got.append((raw, s, tok))
                return
            w = nsplit[0] % NW
            nsplit[0] += 1
            assert w_free[w] is not None, (k, name)
            hi, lo = WHI[:, w * SLOT:w * SLOT + n], WLO[:, w * SLOT:w * SLOT + n]
            th = A(act, hi, raw, ACT.Copy, tok, w_free[w])
            tl = TT(dve, lo, raw, hi.bitcast(F32), ALU.subtract, th)
            w_free[w] = None
            slot_free[s] = [tl]
            got.append((hi, lo, w, th, tl))

        def ahead():
            k = asked[0]
            while len(got) < len(order) and len(got) < k + 3 and slot_free[len(got) % NSLOT] is not None:
                if order[len(got)][3] and w_free[nsplit[0] % NW] is None:
                    break
                fetch()

        def ask(name, i, split):
            k = asked[0]
            assert order[k][0] == name and order[k][1] == i and order[k][3] == split, (k, order[k], name, i)
            while len(got) <= k:
                fetch()
            asked[0] += 1
            ahead()
            return got[k]

        def shaped(v, shape):
            if len(shape) == 2:
                return v.rearrange("p (a b) -> p a b", b=shape[1])
            return v

        def chunk(name, i, shape):
            raw, s, tok = ask(name, i, False)
            return shaped(raw, shape), s, tok

        def release(s, *tokens):
            slot_free[s] = list(tokens)
            ahead()

        def wchunk(name, i, k, m=P):
            hi, lo, w, th, tl = ask(name, i, True)
            return shaped(hi, (k, m)), shaped(lo, (k, m)), w, th, tl

        def wrelease(w, *tokens):
            w_free[w] = list(tokens)
            ahead()

        own = [0]

        def load(dst, src, q=sp, *tokens):
            s = sem(f"s_ld{own[0]}")
            own[0] += 1
            q.wait(*tokens)
            q.ops.append(lambda e: e.dma_start(dst, src).then_inc(s, 16))
            return (s, 16)

        banks = [(b, []) for b in range(7)]
        STAT = PS[7]

        def take():
            b, tokens = banks.pop(0)
            pe.wait(*tokens)
            return b

        def give(b, *tokens):
            banks.append((b, list(tokens)))

        def mm(o, l, r, start=True, stop=True, *tokens, sig=False):
            return pe(lambda e: e.matmul(o, l, r, start=start, stop=stop, skip_group_check=True), *tokens, sig=sig)

        def tr(o, i, ident, *tokens, sig=False):
            return pe(lambda e: e.transpose(o, i, ident), *tokens, sig=sig)

        def dense(o, lhs, rhs, wtok, xtoks):
            n = len(lhs)
            t = None
            for k in range(n):
                t = mm(o, lhs[k], rhs[k], k == 0, k == n - 1, wtok if k == 0 else None, xtoks[k], sig=k == n - 1)
            return t

        def dense3(o, w, xh, xl, xt, off=0, n=None, start=True, stop=True):
            hi, lo, _, th, tl = w
            n = n or len(xh)
            for ks in (range(n - 1), (n - 1,)):
                for k in ks:
                    mm(o, hi[:, k, :], xh[off + k], start and k == 0, False, th, xt[off + k][0])
                    mm(o, lo[:, k, :], xh[off + k], False, False, tl)
                for k in ks:
                    t = mm(o, hi[:, k, :], xl[off + k], False, stop and k == n - 1, xt[off + k][1], sig=k == n - 1)
            return t

        def A(q, o, i, f, *tokens, **kw):
            return q(lambda e: e.activation(o, i, f, **kw), *tokens)

        def TT(q, o, a, b, op, *tokens):
            return q(lambda e: e.tensor_tensor(o, a, b, op), *tokens)

        def TS(q, o, a, s1, s2, op0, op1, *tokens):
            if op1 is None:
                return q(lambda e: e.tensor_scalar(o, a, s1, None, op0), *tokens)
            return q(lambda e: e.tensor_scalar(o, a, s1, s2, op0, op1), *tokens)

        def STT(o, a, s, b, op0, op1, *tokens):
            return dve(lambda e: e.scalar_tensor_tensor(out=o, in0=a, scalar=s, in1=b, op0=op0, op1=op1), *tokens)

        def RECIP(o, i, *tokens):
            return dve(lambda e: e.reciprocal(o, i), *tokens)

        def bc(ap, axis, shape):
            return ap.unsqueeze(axis).to_broadcast(shape)

        M_, A_, S_ = ALU.mult, ALU.add, ALU.subtract

        def everyone():
            return [pe.last, act.last, dve.last, pool.last]

        def ar(at, *shape):
            n = int(np.prod(shape))
            assert at + n <= NAR, (at, shape)
            v = AR[:, at:at + n]
            if len(shape) == 2:
                v = v.rearrange("p (a b) -> p a b", b=shape[1])
            if len(shape) == 3:
                v = v.rearrange("p (a b c) -> p a b c", b=shape[1], c=shape[2])
            return v

        t_xs = [None] * KD

        def load_x(k, q):
            t_xs[k] = load(H[:, k:k + 1, :], D["xT"][:, k:k + 1, :], q)

        load_x(0, act)
        t_vec = load(VEC[:, :], D["vecs"], act)
        for k in range(2, KD, 2):
            load_x(k, act)
        fetch()
        for k in range(1, KD, 2):
            load_x(k, sp)
        t_const = load(CONST[:, :], D["consts"], pool, t_xs[4:])
        HT = list(t_xs)
        HNHk, HNLk = [HNH[:, k, :] for k in range(KD)], [HNL[:, k, :] for k in range(KD)]

        sq_free = [None, None]
        acc_free = [None]
        first = {}

        def square(k, acc, tok, scale=1.0):
            if k == 0:
                first[id(acc)] = A(act, acc, H[:, k, :], ACT.Square, tok, acc_free[0], scale=scale)
                return first[id(acc)]
            t = A(act, SQ[:, k % 2, :], H[:, k, :], ACT.Square, tok, sq_free[k % 2], scale=scale)
            sq_free[k % 2] = TT(pool, acc, acc, SQ[:, k % 2, :], A_, t, first[id(acc)], pool.last)
            return sq_free[k % 2]

        def square_last(tok):
            return A(act, SQ[:, 1, :], H[:, KD - 1, :], ACT.Square, tok, sq_free[1])

        stat_free = [None]

        def colsum(acc, tok):
            t = mm(STAT[:, :], ONES, acc, True, True, tok, t_const, stat_free[0], sig=True)
            return t

        def rstd(dst, src, n, *tokens):
            t = TS(dve, dst, src, 1.0 / n, EPS, M_, A_, *tokens)
            back = t
            t = A(act, dst, dst, ACT.Sqrt, t)
            return RECIP(dst, dst, t), back

        def token_sums(b, at_, tiles, ready):
            for j in range(4):
                for i, a in enumerate(tiles):
                    t = mm(PS[b][:, at_ + j:at_ + j + 1], a[:, P * j:P * j + P], ONES[:, 0:1], i == 0, i == len(tiles) - 1,
                           ready[i], t_const, sig=j == 3)
            return t

        def token_rstd(dst, src, s, *tokens):
            d = TS(dve, s, src, 1.0 / 1024, EPS, M_, A_, *tokens)
            a = A(act, s, s, ACT.Sqrt, d)
            return RECIP(dst, s, a)

        def spread(dst, at_, tok, free):
            b = take()
            for j in range(4):
                t = mm(PS[b][:, P * j:P * j + P], TOK[:, at_ + j:at_ + j + 1].to_broadcast([P, P]), IDENT, True, True, tok, sig=j == 3)
            a = A(act, dst, PS[b][:, :], ACT.Copy, t, free)
            give(b, a)
            return a

        def rstd_last(dst, ta, tl, free):
            b = take()
            t = token_sums(b, 0, [ACC, SQ[:, 1, :]], [ta, tl])
            acc_free[0], sq_free[1] = t, t
            d = token_rstd(TOK[:, 4:8], PS[b][:, 0:4], TOK[:, 0:4], t)
            give(b, d)
            return spread(dst, 4, d, free)

        rs = {"tok": None, "acc": None}

        def split_x(k, gain, tok, *free):
            h = A(act, HNH[:, k, :], H[:, k, :], ACT.Copy, tok, t_vec, *free, scale=gain)
            l = STT(HNL[:, k, :], H[:, k, :], gain, HNH[:, k, :].bitcast(F32), M_, S_, h)
            return h, l

        def need_rs(*readers):
            if rs["acc"] is not None:
                t = colsum(ACC, rs["acc"])
                rs["acc"] = None
                rs["tok"], stat_free[0] = rstd(RS, STAT[:, :], 1024.0, t, *readers)
                acc_free[0] = t
            return rs["tok"]

        def next_norm(name, xt, free):
            def post(m):
                xt[m] = split_x(m, vec(name, m), HT[m], free())
                t = square(m, ACC, HT[m])
                if m == KD - 1:
                    rs["acc"] = t
            return post

        CB = ar(5120, 1024)
        ada_at = [0]
        ada_c = []

        def ada_load(t):
            return load(CB, D["c"].partition_broadcast(P), pool, t)

        def ada_start(t, t_c):
            t_cs = A(act, STMP[:, 0:1024], CB, ACT.Silu, t_c, t)
            ada_c.append(dve(lambda e: e.tensor_copy(CB, STMP[:, 0:1024]), t_cs))
            return ada_c[0]

        ada_sem = [sem(f"s_ada{i}") for i in range(2)]
        ada_free = [[], []]

        def ada():
            c = ada_at[0]
            ada_at[0] += 1
            w = STMP[:, 1024 * (c % 2):1024 * (c % 2) + 1024]
            pool.wait(ada_free[c % 2], ada_c)
            pool.ops.append(lambda e: e.dma_start(w, D["w_ada"][c]).then_inc(ada_sem[c % 2], 16))
            t = dve(lambda e: e.tensor_tensor_reduce(
                out=w, in0=w, in1=CB, scale=1.0, scalar=0.0, op0=M_, op1=A_,
                accum_out=MOD[:, c:c + 1]), (ada_sem[c % 2], 16 * (c // 2 + 1)), ada_c)
            ada_free[c % 2] = [t]

        tmp_free = [[], [], [], []]
        HIDHk, HIDLk = [HIDH[:, k, :] for k in range(11)], [HIDL[:, k, :] for k in range(11)]

        def ffn(w13, w2, xt, post, pre=None, side=lambda half, i: None):
            hid_free = pre
            for half in range(2):
                hidt = []
                for mi in range(11):
                    bs = []
                    for z in range(2):
                        w = wchunk(w13, (half * 11 + mi) * 2 + z, 8)
                        b = take()
                        t = dense3(PS[b][:, :], w, HNHk, HNLk, xt)
                        wrelease(w[2], t)
                        bs.append((b, t))
                    x13[0] = t
                    q = mi % 3
                    r = need_rs()
                    (bA, tA), (bB, tB) = bs
                    d = TT(dve, TMP[:, q, :], PS[bA][:, :], RS, M_, r, tA, tmp_free[q])
                    give(bA, d)
                    a = A(act, TMP[:, q, :], TMP[:, q, :], ACT.Silu, d)
                    d = TT(dve, TMP[:, q, :], TMP[:, q, :], PS[bB][:, :], M_, a, tB)
                    give(bB, d)
                    h = A(act, HIDH[:, mi, :], TMP[:, q, :], ACT.Copy, d, hid_free)
                    l = TT(dve, HIDL[:, mi, :], TMP[:, q, :], HIDH[:, mi, :].bitcast(F32), S_, h)
                    tmp_free[q] = [l]
                    hidt.append((h, l))
                    side(half, mi)
                for m in range(KD):
                    w = wchunk(w2, half * 8 + m, 11)
                    b = take()
                    t = dense3(PS[b][:, :], w, HIDHk, HIDLk, hidt)
                    wrelease(w[2], t)
                    d = TT(dve, TMP[:, 3, :], PS[b][:, :], RS, M_, t, tmp_free[3])
                    give(b, d)
                    HT[m] = STT(H[:, m, :], TMP[:, 3, :], 0.5, H[:, m, :], M_, A_, d, HT[m])
                    tmp_free[3] = [HT[m]]
                    if half:
                        post(m)
                    side(half, 11 + m)
                hid_free = t
            return t

        x13 = [None]

        TC, TSN = ar(0, 16, P), ar(2048, 16, P)
        SBr, SBi = ar(4096, 4, P), ar(4608, 4, P)
        CR, CI = ar(5120, 16, 32), ar(5632, 16, 32)
        CpR, CpI = ar(6144, 16, 32), ar(6656, 16, 32)
        U = ar(7168, 4, T)
        SMALL = AR[:, 20512:20512 + 256]
        RHO = AR[:, 20784:20800]
        t_sb = load(AR[:, 4096:6144], D["s5_bc"], pool)

        def sm(i):
            return SMALL[:, 16 * i:16 * i + 16]

        STMP = ar(18432, 2048)

        def s5_params():
            dt, x, th, k, r, cs, sn, t1, t2, arr, aii, br, bi, den = (sm(i) for i in range(14))
            lr, li = vec("a_re"), vec("a_im")
            t = A(act, dt, vec("log_dt"), ACT.Exp, t_vec)
            t = TT(dve, x, lr, dt, M_, t)
            t_rho = A(act, RHO, x, ACT.Exp, t)
            t = TT(dve, th, li, dt, M_, t)
            yield
            magic = 1.5 * 2.0 ** 23
            t = TS(dve, k, th, float(1 / (2 * np.pi)), None, M_, None, t)
            t = TS(dve, k, k, magic, None, A_, None, t)
            t = TS(dve, k, k, magic, None, S_, None, t)
            c1 = 6.28125
            c2 = float(np.float32(2 * np.pi - c1))
            c2 = float(np.frombuffer((np.frombuffer(np.float32(c2).tobytes(), np.uint32) & np.uint32(0xFFFFE000)).tobytes(), np.float32)[0])
            c3 = float(2 * np.pi - c1 - c2)
            t = STT(r, k, -c1, th, M_, A_, t)
            t = STT(r, k, -c2, r, M_, A_, t)
            t = STT(r, k, -c3, r, M_, A_, t)
            t = TS(dve, r, r, 3.1415925, -3.1415925, ALU.min, ALU.max, t)
            yield
            t_s = A(act, sn, r, ACT.Sin, t)
            t = A(act, t1, r, ACT.Abs, t)
            t = TS(dve, t1, t1, -1.0, float(np.pi / 2), M_, A_, t)
            t = A(act, cs, t1, ACT.Sin, t)
            yield
            t = TT(dve, arr, RHO, cs, M_, t, t_rho)
            t = TT(dve, aii, RHO, sn, M_, t_s, t)
            t = TS(dve, arr, arr, -1.0, None, A_, None, t)
            t = TT(dve, t1, lr, lr, M_, t)
            t = TT(dve, t2, li, li, M_, t)
            t = TT(dve, den, t1, t2, A_, t)
            yield
            t = RECIP(den, den, t)
            t = TT(dve, t1, arr, lr, M_, t)
            t = TT(dve, t2, aii, li, M_, t)
            t = TT(dve, br, t1, t2, A_, t)
            t = TT(dve, br, br, den, M_, t)
            t = TT(dve, t1, aii, lr, M_, t)
            t = TT(dve, t2, arr, li, M_, t)
            t = TT(dve, bi, t1, t2, S_, t)
            t = TT(dve, bi, bi, den, M_, t)
            yield
            b3 = [P, 16, 32]
            w1 = STMP[:, 0:512].rearrange("p (a b) -> p a b", b=32)
            w2 = STMP[:, 512:1024].rearrange("p (a b) -> p a b", b=32)
            t = TT(dve, w1, CR, bc(br, 2, b3), M_, t, t_sb)
            t = TT(dve, w2, CI, bc(bi, 2, b3), M_, t)
            t = TT(dve, CpR, w1, w2, S_, t)
            t = TT(dve, w1, CR, bc(bi, 2, b3), M_, t)
            t = TT(dve, w2, CI, bc(br, 2, b3), M_, t)
            t = TT(dve, CpI, w1, w2, A_, t)
            t = TS(dve, CpI, CpI, -1.0, None, M_, None, t)
            yield
            t = dve(lambda e: e.tensor_copy(TC[:, :, 0:1], cs.unsqueeze(2)), t)
            t = dve(lambda e: e.tensor_copy(TSN[:, :, 0:1], sn.unsqueeze(2)), t)
            d = 1
            while d < P:
                sh = [P, 16, d]
                v1 = STMP[:, 0:16 * d].rearrange("p (a b) -> p a b", b=d)
                v2 = STMP[:, 1024:1024 + 16 * d].rearrange("p (a b) -> p a b", b=d)
                c0, s0, c1_, s1_ = TC[:, :, 0:d], TSN[:, :, 0:d], TC[:, :, d - 1:d], TSN[:, :, d - 1:d]
                cw, sw = c1_.to_broadcast(sh), s1_.to_broadcast(sh)
                for o, (x1, x2), op in ((TC, (cw, sw), S_), (TSN, (sw, cw), A_)):
                    t = TT(dve, v1, c0, x1, M_, t)
                    t = TT(dve, v2, s0, x2, M_, t)
                    t = TT(dve, o[:, :, d:2 * d], v1, v2, op, t)
                d *= 2
                yield
            s5_ready.append(t)

        def softplus_neg(dst, x):
            y, z, z2, acc, t1 = (LA[:, 16 * i:16 * i + 16] for i in range(5))
            t = A(act, y, x, ACT.Abs, t_vec, dve.last)
            t = A(act, y, y, ACT.Exp, t, scale=-1.0)
            t = TS(dve, z, y, 2.0, None, A_, None, t)
            t = RECIP(z, z, t)
            t = TT(dve, z, z, y, M_, t)
            t = TT(dve, z2, z, z, M_, t)
            t = TS(dve, acc, z2, 1.0 / 19, 1.0 / 17, M_, A_, t)
            for n in (15, 13, 11, 9, 7, 5, 3, 1):
                t = TT(dve, acc, acc, z2, M_, t)
                t = TS(dve, acc, acc, 1.0 / n, None, A_, None, t)
            t = TT(dve, acc, acc, z, M_, t)
            t = TS(dve, t1, x, -1.0, 0.0, M_, ALU.max, t)
            return STT(dst, acc, 2.0, t1, M_, A_, t)

        CA = LA[:, 80:96]
        xt = [None] * KD
        post = next_norm("norm_ffn1", xt, lambda: None)
        for k in range(KD):
            post(k)
            if k in (2, 5):
                fetch()
        s5_ready = []
        params = s5_params()
        ca_ready, c_ready = [], []

        def side(half, i):
            if half == 0 and i < 10:
                next(params, None)
                next(params, None)
            if (half, i) == (0, 11):
                t = softplus_neg(CA, vec("rg_lam"))
                ca_ready.append(TS(dve, CA, CA, -8.0, None, M_, None, t))

        def side2(half, i):
            if (half, i) == (0, 0):
                c_ready.append(ada_load(att_done))
            if (half, i) == (0, 1):
                ada_start(att_done, c_ready[0])
            for _ in range(adas(half, i)):
                ada()

        xt_mix = [None] * KD
        ffn("w13a", "w2a", xt, next_norm("norm_mix", xt_mix, lambda: x13[0]), side=side)
        t_s5, t_ca = s5_ready[0], ca_ready[0]
        t_pre = everyone()

        V_ = [[ar(at_v, 2, T) for at_v in pair] for pair in ((9216, 10240), (11264, 12288))]
        XAp = ar(5120, 2, T)
        XBp = ar(19456, 16, 2, 31)
        CEf = ar(5120, 1024)
        CE = CEf.rearrange("p (a b c) -> p a b c", b=8, c=32)
        Q = ar(13312, 4, T)
        KC, KSL, KW, VCT = (AR[:, 15360 + T * i:15360 + T * (i + 1)] for i in range(4))
        VT = ar(17408, 4, 256)
        GT, GX = ar(18432, 4, 24), ar(18528, 4, 24)
        CM, CS = ar(18624, 32), ar(18656, 32)
        HIDc = ar(18688, 2, 64)
        KCC = ar(18816, 64)
        VC = ar(18880, 128)
        ST4 = ar(19008, 7, 4)
        E1, E2, E3 = ar(19040, 2, 2), ar(19048, 2, 2), ar(19056, 2, 2)
        RT = ar(19064, 4)
        WK2, WV2 = ar(19072, 2, 128), ar(19328, 2, 64)
        PTb = [HX[:, 2048 * i:2048 * i + 2048].rearrange("p (k t) -> p k t", t=T) for i in range(3)] + [TMP]
        PB = HX[:, 6144:8192].rearrange("p (a t) -> p a t", t=T)
        PTC = [KC, VCT]
        t_wg = load(AR[:, 19072:19456], D["small_w"], act, t_pre)

        def w_in_tiles():
            for c in range(12):
                w = wchunk("w_inA", c, 8)
                b = take()
                t = dense3(PS[b][:, :], w, HNHk, HNLk, xt_mix)
                wrelease(w[2], t)
                yield b, t, need_rs()

        tiles = w_in_tiles()
        ut = []
        for m in range(4):
            b, t, r = next(tiles)
            a = TT(dve, U[:, m, :], PS[b][:, :], RS, M_, t, r, t_pre)
            give(b, a)
            ut.append(a)
        b = take()
        for j in range(4):
            t = tr(PS[b][:, P * j:P * j + P], RS[:, P * j:P * j + P], IDENT, r, t_const, sig=j == 3)
        t_rt = A(act, RT, PS[b][:, :].rearrange("p (j x) -> p j x", j=4)[:, :, 0], ACT.Copy, t, t_pre)
        give(b, t_rt)

        ot = [None] * 8

        def s5():
            temps = [SQ[:, 0, :], SQ[:, 1, :], RR, ACC]
            temp_free = [[sq_free[0], sq_free[1], acc_free[0]] for _ in range(4)]
            c_done = [None] * 2
            d_at = VEC_AT["s5_d"][0]

            def f4(x):
                return x.rearrange("p (c t) -> p c t", t=P)

            def tables(t16):
                return bc(TC[:, t16, :], 1, [P, 4, P]), bc(TSN[:, t16, :], 1, [P, 4, P])

            def drive(b, j):
                t16 = 2 * b + j
                y4, rows = t16 // 4, slice(32 * (t16 % 4), 32 * (t16 % 4) + 32)
                bR = take()
                tR = mm(PS[bR][:, :], SBr[rows, y4, :], U[rows, y4, :], True, True, ut[y4], t_sb, sig=True)
                bI = take()
                tI = mm(PS[bI][:, :], SBi[rows, y4, :], U[rows, y4, :], True, True, sig=True)
                vr, vi = V_[b % 2][0][:, j, :], V_[b % 2][1][:, j, :]
                c4, s4 = tables(t16)
                k1, k2 = 2 * j, 2 * j + 1
                t1, t2 = temps[k1], temps[k2]
                d1 = TT(dve, f4(vr), f4(PS[bR][:, :]), c4, M_, tR, c_done[b % 2], t_s5, t_pre)
                d2 = TT(dve, f4(t1), f4(PS[bI][:, :]), s4, M_, tI, temp_free[k1])
                d3 = TT(dve, f4(vi), f4(PS[bI][:, :]), c4, M_)
                d4 = TT(dve, f4(t2), f4(PS[bR][:, :]), s4, M_, temp_free[k2])
                give(bR, d4)
                give(bI, d3)
                e1 = TT(pool, vr, vr, t1, A_, d1, d2)
                e2 = TT(pool, vi, vi, t2, S_, d3, d4)
                temp_free[k1], temp_free[k2] = [e1], [e2]
                return e1, e2

            def scan(b, c, vt, carry):
                cols = slice(P * c, P * c + P)
                for j in range(2):
                    rho = RHO[:, 2 * b + j:2 * b + j + 1].to_broadcast([P, P])
                    for z in range(2):
                        v = V_[b % 2][z][:, j, cols]
                        ini = 0.0 if c == 0 else E3[:, z, j:j + 1]
                        sc = dve(lambda e, v=v, rho=rho, ini=ini: e.tensor_tensor_scan(
                            out=v, data0=rho, data1=v, initial=ini, op0=M_, op1=A_), vt[j][z], carry)
                if c == 3:
                    return sc, None
                lr_, li_ = V_[b % 2][0][:, :, P * c + P - 1], V_[b % 2][1][:, :, P * c + P - 1]
                ce, se = TC[:, 2 * b:2 * b + 2, P - 1], TSN[:, 2 * b:2 * b + 2, P - 1]
                TT(dve, E1[:, 0, :], lr_, ce, M_, sc)
                TT(dve, E1[:, 1, :], lr_, se, M_)
                TT(dve, E2[:, 0, :], li_, se, M_)
                t = TT(dve, E2[:, 1, :], li_, ce, M_)
                TT(dve, E3[:, 0, :], E1[:, 0, :], E2[:, 0, :], S_, t)
                return sc, TT(dve, E3[:, 1, :], E1[:, 1, :], E2[:, 1, :], A_)

            def back(b, j, sc):
                vr, vi = V_[b % 2][0][:, j, :], V_[b % 2][1][:, j, :]
                c4, s4 = tables(2 * b + j)
                k1, k2 = 2 * j, 2 * j + 1
                t1, t2 = temps[k1], temps[k2]
                d1 = TT(pool, f4(t1), f4(vr), s4, M_, sc, temp_free[k1])
                d2 = STT(f4(t2), f4(vi), -1.0, s4, M_, M_, sc, temp_free[k2])
                d3 = TT(pool, f4(vr), f4(vr), c4, M_, d1)
                d4 = TT(pool, f4(vi), f4(vi), c4, M_, d2)
                return (CpR, t2, d2), (CpI, t1, d1), (CpR, vr, d3), (CpI, vi, d4)

            def read(b, done):
                y4 = b // 2
                rows = slice(64 * (b % 2), 64 * (b % 2) + 64)
                bY = take()
                for z in range(4):
                    for j in range(2):
                        t16 = 2 * b + j
                        r = 32 * (t16 % 4)
                        Cp, x, tok = done[j][z]
                        tY = mm(PS[bY][r:r + 32, :], Cp[:, t16, :], x, z == 0, z == 3, tok, sig=True)
                c_done[b % 2] = tY
                for k in range(4):
                    temp_free[k] = [tY]
                ot[4 + y4] = STT(U[rows, y4, :], U[rows, y4, :], VEC[rows, d_at + y4:d_at + y4 + 1], PS[bY][rows, :], M_, A_, tY)
                give(bY, ot[4 + y4])

            vt, turned_ = {}, {}
            for b in range(-1, 9):
                carry = sc = None
                for c in range(4 if 0 <= b < 8 else 0):
                    sc, carry = scan(b, c, vt[b], carry)
                    yield
                if b >= 1:
                    read(b - 1, turned_.pop(b - 1))
                    yield
                if b + 1 < 8:
                    vt[b + 1] = []
                    for j in range(2):
                        vt[b + 1].append(drive(b + 1, j))
                        yield
                if sc is not None:
                    yield
                    turned_[b] = []
                    for j in range(2):
                        turned_[b].append(back(b, j, sc))
                        yield
            sq_free[0] = temp_free[0] + temp_free[1]
            sq_free[1] = acc_free[0] = sq_free[0] + temp_free[2] + temp_free[3]

        s5g = s5()

        def s5_step(n=1):
            for _ in range(n):
                next(s5g, None)

        def rope(b, t, dst, scale, q):
            a = STT(TMP[:, q, :], PS[b][:, :], scale, RS, M_, M_, t, r, tmp_free[q])
            give(b, a)

            def rest():
                b2 = take()
                t2 = mm(PS[b2][:, :], ROT, TMP[:, q, :], True, True, a, t_const, sig=True)
                p1 = TT(pool, dst, TMP[:, q, :], COS, M_, a, t_pre)
                d = TT(dve, TMP[:, q, :], PS[b2][:, :], SIN, M_, t2, p1)
                give(b2, d)
                d2 = TT(pool, dst, dst, TMP[:, q, :], A_, d)
                tmp_free[q] = [d2]
                return d2
            return rest

        xa = [None]
        xbt, xb_free, hidc_free, cmp_t = {}, [None], [None], {}

        def pairs_of(z):
            src, tok = (KC, kt["kc"]) if z == 0 else (VCT, kt["vc"])
            lt = []
            for g in range(2):
                lt.append(load(XAp[0:64, g, :], src[64 * g:64 * g + 64, :], act, tok, xa[0], t_pre))
                lt.append(load(XAp[64:128, g, 0:T - 1], src[64 * g:64 * g + 64, 1:T], act))
            return lt

        def positions(z, lt):
            for g in range(2):
                for a_ in range(2):
                    v = XAp[:, g, :].rearrange("p (c r two) -> p r c two", r=8, two=2)[:, :, a_:a_ + 31, 0]
                    xa[0] = TT(dve, XBp[:, 8 * a_:8 * a_ + 8, g, :], v,
                               bc(vec(("pe_k", "pe_v")[z], 8 * a_, 8), 2, [P, 8, 31]), A_, lt, xb_free[0], t_pre)
            xbt[z] = xa[0]

        def compress(z):
            bs = [take(), take()]
            for c in range(4):
                if c:
                    yield
                w, s, wt = chunk(("wk1", "wv1")[z], c, (4, 256))
                for mt in range(2):
                    for i in range(4):
                        ii = 4 * c + i
                        t = mm(PS[bs[mt]][:, 0:62], w[:, i, P * mt:P * mt + P],
                               XBp[:, ii, :, :].rearrange("p g c -> p (g c)"), ii == 0, ii == 15, wt, xbt[z], sig=i == 3)
                release(s, t)
            xb_free[0] = t
            for mt in range(2):
                hc = A(act, HIDc[:, mt, 0:62], PS[bs[mt]][:, 0:62], ACT.Gelu_apprx_tanh, t, hidc_free[0], t_pre)
                give(bs[mt], hc)

            def rest():
                b = take()
                if z == 0:
                    for mt in range(2):
                        t = mm(PS[b][:, 0:62], WK2[:, mt, :], HIDc[:, mt, 0:62], mt == 0, mt == 1, hc, t_wg, sig=mt == 1)
                    cmp_t[z] = A(act, KCC[:, 0:62], PS[b][:, 0:62], ACT.Copy, t, t_pre)
                else:
                    for g in range(2):
                        for mt in range(2):
                            t = mm(PS[b][0:31, 64 * g:64 * g + 64], HIDc[:, mt, 31 * g:31 * g + 31], WV2[:, mt, :],
                                   mt == 0, mt == 1, hc, t_wg, sig=mt == 1)
                    cmp_t[z] = A(act, VC[0:31, :], PS[b][0:31, 0:128], ACT.Copy, t, t_pre)
                give(b, cmp_t[z])
                hidc_free[0] = t
            yield rest

        s5_step(2)
        qt_, kt = [], {}
        names = [("kc", KC), ("vc", VCT), ("ksl", KSL), ("kw", KW), ("q", 0), ("q", 1), ("q", 2), ("q", 3)]
        pend = []

        def turn():
            nm, rest = pend.pop(0)
            t = rest()
            if nm == "q":
                qt_.append(t)
            else:
                kt[nm] = t
            return nm

        for i, (nm, dst) in enumerate(names):
            b, t, r = next(tiles)
            if nm == "vc":
                kt["vc"] = TT(dve, VCT, PS[b][:, :], RS, M_, t, r, t_pre)
                give(b, kt["vc"])
            else:
                pend.append((nm, rope(b, t, Q[:, dst, :] if nm == "q" else dst, 0.125 if nm == "q" else 1.0, i % 4)))
            if (nm == "vc" or len(pend) > 1) and turn() == "kc":
                lt = pairs_of(0)
            if i == 3:
                positions(0, lt)
                lt = pairs_of(1)
            if i == 4:
                packed = compress(0)
            if i >= 4:
                rest = next(packed)
            s5_step(3)
        positions(1, lt)
        turn()
        vtt = [None] * 4
        bs = [take() for _ in range(4)]
        for z in range(2):
            hi, lo, wi, th, tl = wchunk("w_inV", z, 4, 280)
            for tt in range(4):
                o = PS[bs[tt]][:, 0:280]
                for k in range(4):
                    kk = 4 * z + k
                    xh, xl = HNH[:, kk, P * tt:P * tt + P], HNL[:, kk, P * tt:P * tt + P]
                    mm(o, xh, hi[:, k, :], kk == 0, False, th, xt_mix[kk][0])
                    mm(o, xh, lo[:, k, :], False, False, tl)
                    t = mm(o, xl, hi[:, k, :], False, kk == 7, xt_mix[kk][1], sig=k == 3)
                if z:
                    vtt[tt] = A(act, VT[:, tt, :], PS[bs[tt]][:, 0:256], ACT.Copy, t, t_rt, t_pre, scale=RT[:, tt:tt + 1])
                    a2 = A(act, GX[:, tt, :], PS[bs[tt]][:, 256:280], ACT.Copy, t, scale=RT[:, tt:tt + 1])
                    give(bs[tt], a2)
                s5_step()
            wrelease(wi, t)
            if z == 0:
                rest()
        t_z = t
        packed = compress(1)
        gt = A(act, GT, GX, ACT.Sigmoid, a2)

        ce_t = [None]

        def weigh():
            cneg = const("cneg").rearrange("p (q c) -> p q c", c=32)
            c01 = const("c01").rearrange("p (q c) -> p q c", c=32)
            for qt in range(4):
                ce = CE[:, qt, :, :].rearrange("p (i f) c -> p f i c", f=2)
                for hf in range(2):
                    b = take()
                    r = slice(64 * hf, 64 * hf + 64)
                    for i in range(4):
                        t = mm(PS[b][:, 32 * i:32 * i + 31], Q[r, i, P * qt:P * qt + P], KCC[r, 31 * hf:31 * hf + 31],
                               True, True, qt_[i], cmp_t[0], sig=i == 3)
                    v = PS[b][:, 0:128].rearrange("p (h c) -> p h c", c=32)[:, :, 0:31]
                    d = TT(dve, ce[:, hf, :, 0:31], v, bc(cneg[:, qt, 0:31], 1, [P, 4, 31]), A_, t, xa[0])
                    give(b, d)
                yield
            CEa = CEf.rearrange("p (a c) -> p a c", c=32)[:, :, 0:31]
            sh = [P, 32, 31]
            t = dve(lambda e: e.tensor_reduce(CM, CEa, AXX, ALU.max), d)
            t = TT(dve, CEa, CEa, bc(CM, 2, sh), S_, t)
            t = A(act, CEa, CEa, ACT.Exp, t)
            yield
            for qt in range(4):
                t2 = TT(dve, CE[:, qt, :, 0:31], CE[:, qt, :, 0:31], bc(c01[:, qt, 0:31], 1, [P, 8, 31]), M_, t)
            t = dve(lambda e: e.tensor_reduce(CS, CEa, AXX, A_), t2)
            t = TS(dve, CS, CS, 1e-30, None, ALU.max, None, t)
            t = RECIP(CS, CS, t)
            yield
            CS4 = CS.rearrange("p (q h) -> p q h", h=8)
            t = TT(dve, CS4, CS4, GT[:, :, 0:8], M_, t, gt)
            ce_t[0] = TT(dve, CEa, CEa, bc(CS, 2, sh), M_, t)

        pt_free = [[t_z], [t_z], [t_z], list(tmp_free)]
        ptc_free = [xa[0], xa[0]]
        p_free = [[t_z] for _ in range(4)]
        unit = [0]
        bOs = {}

        def scores(i, kind, qt):
            nk = P * (qt + 1)
            K_ = KSL if kind == 1 else KW
            bs = [take(), take()]
            for hf in range(2):
                r = slice(64 * hf, 64 * hf + 64)
                mm(PS[bs[hf]][:, 0:nk], Q[r, i, P * qt:P * qt + P], K_[r, 0:nk], True, False,
                   kt["ksl"], kt["kw"], qt_[i])
            out_ = []
            for hf in range(2):
                b = bs[hf]
                t = mm(PS[b][:, nk - P:nk], IDENT, const("causal"), False, True, t_const, sig=True)
                u = unit[0] % 4
                unit[0] += 1
                st = ST4[:, u, :]
                d = dve(lambda e, b=b, st=st: e.tensor_reduce(st[:, 0:1], PS[b][:, 0:nk], AXX, ALU.max, negate=True), t, p_free[u])
                a = A(act, PB[:, u, 0:nk], PS[b][:, 0:nk], ACT.Exp, d, p_free[u], bias=st[:, 0:1], accum_out=st[:, 1:2])
                give(b, a)
                out_.append((hf, u, st, a))

            def scale():
                rs_ = [(hf, u, st, RECIP(st[:, 2:3], st[:, 1:2], a)) for hf, u, st, a in out_]
                return [(hf, u, TS(dve, PB[:, u, 0:nk], PB[:, u, 0:nk], st[:, 2:3],
                                   GT[:, qt, 8 * kind + 2 * i + hf:8 * kind + 2 * i + hf + 1], M_, M_, d, gt)) for hf, u, st, d in rs_]
            return scale

        def flip(i, kind, qt, scaled):
            out_ = []
            for hf, u, tok in scaled:
                b = take()
                for kb in range(qt + 1):
                    t = tr(PS[b][:, P * kb:P * kb + P], PB[:, u, P * kb:P * kb + P], IDENT, tok, t_const, sig=kb == qt)
                p_free[u] = [t]
                n = 2 * (kind % 2) + hf
                assert pt_free[n] is not None
                a = A(act, PTb[n][:, 0:qt + 1, P * qt:P * qt + P],
                      PS[b][:, 0:P * (qt + 1)].rearrange("p (k t) -> p k t", t=P), ACT.Copy, t, pt_free[n])
                give(b, a)
                out_.append(a)
            return out_

        def values(i, kind, a):
            n = 2 * (kind % 2)
            if kind == 1:
                bOs[i] = take()
            if kind == 2:
                tt_ = []
                for hf in range(2):
                    b = take()
                    for qt in range(4):
                        t = tr(PS[b][0:31, P * qt:P * qt + P], CE[:, qt, 2 * i + hf, 0:31], IDENT, ce_t[0], t_const, sig=qt == 3)
                    tt_.append(A(act, PTC[hf][0:31, :], PS[b][0:31, :], ACT.Copy, t, ptc_free[hf]))
                    give(b, tt_[hf])
            for kb in range(4):
                for hf in range(2):
                    t = mm(PS[bOs[i]][64 * hf:64 * hf + 64, P * kb:T], VT[:, kb, P * (kind - 1) + 64 * hf:P * (kind - 1) + 64 * hf + 64],
                           PTb[n + hf][:, kb, P * kb:T], kind == 1 and kb == 0, False, a[hf], vtt[kb], sig=True)
                if kb == 3:
                    pt_free[n] = pt_free[n + 1] = [t]
                if kb % 2:
                    yield
            if kind == 2:
                for hf in range(2):
                    ptc_free[hf] = mm(PS[bOs[i]][64 * hf:64 * hf + 64, :], VC[0:31, 64 * hf:64 * hf + 64], PTC[hf][0:31, :],
                                      False, True, tt_[hf], cmp_t[1], sig=True)
                ot[i] = A(act, Q[:, i, :], PS[bOs[i]][:, :], ACT.Copy, ptc_free[0], ptc_free[1])
                give(bOs[i], ot[i])

        live, closing = [], []
        work = [(i, kind, qt) for i in range(4) for kind in (1, 2) for qt in range(4)]
        side_work = weigh()
        for n, x in enumerate(work + [None] * 2):
            if closing and next(closing[0], 0) == 0:
                closing.pop(0)
            if len(live) > 1 or x is None:
                (i, kind, qt), sc = live.pop(0)
                a = flip(i, kind, qt, sc if isinstance(sc, list) else sc())
                if qt == 3:
                    pt_free[2 * (kind % 2)] = pt_free[2 * (kind % 2) + 1] = None
                    closing.append(values(i, kind, a))
            if x is not None:
                if live:
                    live[-1] = (live[-1][0], live[-1][1]())
                live.append((x, scores(*x)))
            if n < 4:
                rest = next(packed)
            if n == 4:
                rest()
            if n > 1:
                next(side_work, None)
            s5_step(2)
        for c in closing:
            for _ in c:
                pass
        tmp_free = [[x for y in pt_free for x in y] for _ in range(4)]
        s5_step(100)

        tables_done = [pool.last, dve.last]
        ov_done = pe.last
        parts = []

        def part(k, x, tok):
            h = A(act, OH[:, k, :], x, ACT.Copy, tok, tables_done, ov_done)
            parts.append((h, TT(dve, OL[:, k, :], x, OH[:, k, :].bitcast(F32), S_, h)))

        for m in range(4):
            ot[4 + m] = A(act, U[:, m, :], U[:, m, :], ACT.Gelu_apprx_tanh, ot[4 + m])
        for m in range(4):
            part(m, Q[:, m, :], ot[m])
        sg = []
        for m in range(4):
            w, s, wt = chunk("w_glu", m, (4, P))
            b = take()
            t = dense(PS[b][:, :], [w[:, k, :] for k in range(4)], [U[:, k, :] for k in range(4)], wt, ot[4:8])
            release(s, t)
            a = A(act, TMP[:, m, :], PS[b][:, :], ACT.Sigmoid, t, tmp_free[m], bias=vec("b_glu", m))
            give(b, a)
            sg.append(a)
        for m in range(4):
            ot[4 + m] = TT(dve, U[:, m, :], U[:, m, :], TMP[:, m, :], M_, sg[m], t)
            tmp_free[m] = [ot[4 + m]]
        for m in range(4):
            part(4 + m, U[:, m, :], ot[4 + m])

        att_done = everyone()
        xt = [None] * KD
        post = next_norm("norm_ffn2", xt, lambda: att_done)
        ohs, ols = [OH[:, k, :] for k in range(8)], [OL[:, k, :] for k in range(8)]
        for m in range(KD):
            w = wchunk("w_out", m, 8)
            b = take()
            t = dense3(PS[b][:, :], w, ohs, ols, parts)
            wrelease(w[2], t)
            HT[m] = TT(dve, H[:, m, :], PS[b][:, :], H[:, m, :], A_, t, HT[m])
            give(b, HT[m])
            post(m)
        xt_ple = [None] * KD
        WP = ar(0, 2, 1024)
        PT_ = ar(2048, 2, T)
        t_wp = load(AR[:, 0:2048], D["w_ple"], act, att_done, t)
        t_p = load(PT_, D["pT"], act)
        ffn("w13b", "w2b", xt, next_norm("norm_ple", xt_ple, lambda: x13[0]), pre=[t, att_done], side=side2)

        ACC2 = ar(3072, T)
        ple = {}

        def ple_squares(m):
            if m == 0:
                t2 = A(act, ACC2, H[:, 0, :], ACT.Square, HT[0], scale=vec("norm_final", 0))
                return square(0, ACC, HT[0]), t2
            if m == KD - 1:
                return square_last(HT[m]), A(act, TMP[:, 3, :], H[:, m, :], ACT.Square, tmp_free[3], scale=vec("norm_final", m))
            q = 2 + m % 2
            ta = square(m, ACC, HT[m])
            t2 = A(act, TMP[:, q, :], H[:, m, :], ACT.Square, tmp_free[q], scale=vec("norm_final", m))
            tmp_free[q] = [TT(pool, ACC2, ACC2, TMP[:, q, :], A_, t2, ple[0][1], pool.last)]
            return ta, tmp_free[q][0]

        for m in range(KD):
            b2 = take()
            t2 = dense(PS[b2][:, :], [WP[:, k, P * m:P * m + P] for k in range(2)], [PT_[:, k, :] for k in range(2)], t_wp, [t_p] * 2)
            w = wchunk("w_pg", m, 8)
            b = take()
            t = dense3(PS[b][:, :], w, HNHk, HNLk, xt_ple)
            r = need_rs()
            q = m % 2
            d = TT(dve, TMP[:, q, :], PS[b][:, :], RS, M_, r, t, tmp_free[q])
            give(b, d)
            a = A(act, TMP[:, q, :], TMP[:, q, :], ACT.Sigmoid, d)
            d = TT(dve, TMP[:, q, :], PS[b2][:, :], TMP[:, q, :], M_, a, t2)
            give(b2, d)
            if m:
                ple[m - 1] = ple_squares(m - 1)
            HT[m] = TT(dve, H[:, m, :], H[:, m, :], TMP[:, q, :], A_, d, HT[m])
            tmp_free[q] = [HT[m]]
            wrelease(w[2], t)
        ple[KD - 1] = ple_squares(KD - 1)
        ple_done = t

        t = TT(dve, MOD[:, :], MOD[:, :], vec("b_ada"), A_, dve.last)
        for l in range(2):
            t = TS(dve, GS[:, 8 * l:8 * l + 8], MOD[:, 24 * l + 8:24 * l + 16], 1.0, None, A_, None, t)
            t = TT(dve, GS[:, 8 * l:8 * l + 8], GS[:, 8 * l:8 * l + 8], vec("norm_g", 8 * l, 8), M_, t)
        GF = GS[:, 16:24]
        t_mod = TT(dve, GF, GS[:, 0:8], vec("norm_final"), M_, t)

        b = take()
        t1 = token_sums(b, 0, [ACC, SQ[:, 1, :]], [ple[6][0], ple[7][0]])
        t2 = token_sums(b, 4, [ACC2, TMP[:, 3, :]], [ple[6][1], ple[7][1]])
        acc_free[0], sq_free[1], tmp_free[3] = t1, t1, [t2]
        R1, R2, S2 = TOK[:, 8:12], TOK[:, 12:16], TOK[:, 4:8]
        r1 = token_rstd(R1, PS[b][:, 0:4], TOK[:, 0:4], t1, t2)
        d = TT(dve, S2, PS[b][:, 4:8], R1, M_, t2, r1)
        give(b, d)
        d = TT(dve, S2, S2, R1, M_, d)
        d = token_rstd(R2, S2, S2, d)
        d = TT(dve, R2, R2, R1, M_, d)
        t_rr = spread(RR, 12, d, None)
        t_rs = spread(RS, 8, r1, ple_done)

        for l in range(2):
            if l:
                t_rr = rstd_last(RR, ta, tl, None)
            hnt = []
            scaled_ = []
            for k in range(KD + 1):
                if k < KD:
                    gain = GF[:, k:k + 1] if l == 0 else GS[:, 8 + k:9 + k]
                    q = k % 4
                    scaled_.append(STT(TMP[:, q, :], H[:, k, :], gain, RR, M_, M_, t_rr, t_mod, HT[k], tmp_free[q]))
                if k:
                    q = (k - 1) % 4
                    shift = MOD[:, 24 * l + k - 1:24 * l + k]
                    h = A(act, HNH[:, k - 1, :], TMP[:, q, :], ACT.Identity, scaled_[k - 1], ple_done, bias=shift)
                    d = STT(HNL[:, k - 1, :], TMP[:, q, :], shift, HNH[:, k - 1, :].bitcast(F32), A_, S_, h)
                    tmp_free[q] = [d]
                    hnt.append((h, d))
            start = everyone()
            Y = ar(8224, 8, T)
            XM = ar(4096, 8, 515)
            XR = ar(4096, 8, T)
            XC = ar(0, 8, T)
            V2 = ar(0, 4, 1024)
            Q2 = ar(12320, 8, T)
            K2 = ar(16416, 8, T)
            WIF = RSf[:, 0:768].rearrange("p (a b) -> p a b", b=32)
            GV = RSf[:, 768:1024].rearrange("p (a b) -> p a b", b=32)
            ET = ar(20768, 4, 4)

            def proj(part, m):
                w = wchunk("w_in2", 40 * l + 8 * part + m, 8)
                b = take()
                t = dense3(PS[b][:, :], w, HNHk, HNLk, hnt)
                wrelease(w[2], t)
                return b, t

            def proj_pair(part, m):
                ws = [wchunk("w_in2", 40 * l + 8 * part + m + i, 8) for i in range(2)]
                bs = [take(), take()]
                ts = []
                for k in range(8):
                    for (hi, lo, _, th, tl), b in zip(ws, bs):
                        mm(PS[b][:, :], hi[:, k, :], HNHk[k], k == 0, False, th, hnt[k][0])
                        mm(PS[b][:, :], lo[:, k, :], HNHk[k], False, False, tl)
                for (hi, lo, w, th, tl), b in zip(ws, bs):
                    for k in range(8):
                        t = mm(PS[b][:, :], hi[:, k, :], HNLk[k], False, k == 7, hnt[k][1], sig=k == 7)
                    wrelease(w, t)
                    ts.append((b, t))
                return ts

            def conv(dst, x, kind, m, *tokens):
                cw = lambda i: vec(kind + "_conv_w", 32 * l + 8 * i + m)
                t = TS(dve, dst, x[:, 3:3 + T], cw(3), vec(kind + "_conv_b", 8 * l + m), M_, A_, *tokens)
                for i in range(3):
                    t = STT(dst, x[:, i:i + T], cw(i), dst, M_, A_, t)
                return t

            RX, IX, CX = Q2, K2, Y
            XP = [AR[:, 1024 * z:1024 * z + 515] for z in range(2)]
            wax = ar(2048, 2, 8, P)
            t_wax = load(AR[:, 2048:4096], D["rg_w"][l], act, start)
            t_xp = [pool(lambda e, x=x: e.memset(x[:, 0:3], 0.0), start) for x in XP][-1]
            t_pad = pool(lambda e: e.memset(XM[:, :, 0:3], 0.0), start)
            xp_free = [[], []]
            rt, itk, ct, yt = [], [], [], []
            pend = []

            def gates(hh, c):
                for z, (dst, bn, lst) in enumerate(((RX, "rg_b_a", rt), (IX, "rg_b_x", itk))):
                    b = take()
                    t = mm(PS[b][:, :], wax[:, z, hh, :], CX[:, hh, :], True, True, c, t_wax, sig=True)
                    a = A(act, dst[:, hh, :], PS[b][:, :], ACT.Sigmoid, t, start, bias=vec(bn, 8 * l + hh))
                    give(b, a)
                    lst.append(a)
                return t

            two_ = proj_pair(0, 0)
            for hh in range(8):
                b, t = two_[hh] if hh < 2 else proj(0, hh)
                x = XP[hh % 2]
                a = A(act, x[:, 3:515], PS[b][:, :], ACT.Copy, t, t_xp, xp_free[hh % 2], start)
                give(b, a)
                d = conv(CX[:, hh, :], x, "rg", hh, a, start)
                xp_free[hh % 2] = [d]
                ct.append(d)
                pend.append((hh, d))
                if len(pend) > 3:
                    gates(*pend.pop(0))
                if l == 0:
                    HT[hh] = STT(H[:, hh, :], H[:, hh, :], vec("norm_final", hh), RS, M_, M_, hnt[hh][1], t_rs)
            t_wif = load(RSf[:, 0:768], D["w_if"][l], pool, start, dve.last)
            xmt = []
            ax, cvt = [], []

            def conv_x(c):
                cvt.append(conv(XC[:, c, :], XM[:, c, :], "ml", c, xmt[c], t_g))

            for m in range(8):
                b, t = proj(2, m)
                if pend:
                    t_g = gates(*pend.pop(0))
                a = A(act, XM[:, m, 3:515], PS[b][:, :], ACT.Copy, t, t_pad, start)
                give(b, a)
                xmt.append(a)
                hh = m
                ca = CA[:, 8 * l + hh:8 * l + hh + 1]
                p1 = TT(pool, IX[:, hh, :], IX[:, hh, :], CX[:, hh, :], M_, itk[hh], ct[hh])
                q = hh % 4
                th = A(act, TMP[:, q, :], RX[:, hh, :], ACT.Tanh, rt[hh], t_ca, tmp_free[q], scale=ca)
                a = A(act, RX[:, hh, :], RX[:, hh, :], ACT.Exp, th, scale=ca)
                a2 = A(act, CX[:, hh, :], RX[:, hh, :], ACT.Square, a, p1)
                d = STT(CX[:, hh, :], CX[:, hh, :], 1.0, TMP[:, q, :], A_, M_, a2)
                tmp_free[q] = [d]
                ax.append((d, p1, a))
                for c in CONV_AT.get(m, ()):
                    conv_x(c)
            hst = []
            for hh in range(8):
                d, p1, a = ax[hh]
                a2 = A(act, CX[:, hh, :], CX[:, hh, :], ACT.Sqrt, d, scale=-1.0)
                p2 = TT(pool, IX[:, hh, :], IX[:, hh, :], CX[:, hh, :], M_, a2, p1)
                hst.append(dve(lambda e, hh=hh, RX=RX, IX=IX, CX=CX: e.tensor_tensor_scan(
                    out=CX[:, hh, :], data0=RX[:, hh, :], data1=IX[:, hh, :], initial=0.0, op0=M_, op1=A_), p2, a))
            rg_done = [dve.last]
            xct = []

            def silu_x(m, tok):
                a = A(act, IX[:, m, :], XC[:, m, :], ACT.Sigmoid, tok, hst[m])
                xct.append(TT(pool, XC[:, m, :], XC[:, m, :], IX[:, m, :], M_, a))

            at_hi = (4, 5, 0, 1, 6, 2, 3, 4)
            xhi = [TMPH[:, i, :] for i in at_hi]
            xcs = []

            def split_c(m, q):
                free = (tmp_free + sq_free + acc_free)[at_hi[m]]
                h = A(act, xhi[m], XC[:, m, :], ACT.Copy, xct[m], free)
                xcs.append((h, TT(q, YRH[:, m, :], XC[:, m, :], xhi[m].bitcast(F32), S_, h)))

            for m in range(8):
                b, t = proj(1, m)
                a = A(act, RX[:, m, :], PS[b][:, :], ACT.Sigmoid, t, hst[m])
                d = TT(dve, RX[:, m, :], RX[:, m, :], PS[b][:, :], M_, a)
                give(b, d)
                yt.append(TT(dve, Y[:, m, :], Y[:, m, :], RX[:, m, :], M_, d))
                for c in CONV_AT.get(8 + m, ()):
                    conv_x(c)
                silu_x(m, cvt[m])
                if m:
                    split_c(m - 1, dve)

            qtk, ktk = [None] * 8, [None] * 8
            xlo = [YRH[:, m, :] for m in range(8)]
            for c in range(2):
                ws = [wchunk("ml_wqk", 4 * l + 2 * z + c, 4, 256) for z in range(2)]
                for h in (2 * c, 2 * c + 1):
                    for (hi, lo, wi, th, tl), dst, lst in zip(ws, (Q2, K2), (qtk, ktk)):
                        for mt in range(2):
                            m = 2 * h + mt
                            b = take()
                            cols = slice(P * mt, P * mt + P)
                            for kk in range(2):
                                k, x = 2 * (h % 2) + kk, 2 * h + kk
                                mm(PS[b][:, :], hi[:, k, cols], xhi[x], kk == 0, False, th, xcs[x][0])
                                mm(PS[b][:, :], lo[:, k, cols], xhi[x], False, False, tl)
                            for kk in range(2):
                                k, x = 2 * (h % 2) + kk, 2 * h + kk
                                t = mm(PS[b][:, :], hi[:, k, cols], xlo[x], False, kk == 1, xcs[x][1], sig=kk == 1)
                            lst[m] = A(act, dst[:, m, :], PS[b][:, :], ACT.Copy, t, yt[-1], xct[-1])
                            give(b, lst[m])
                        if h % 2:
                            wrelease(wi, t)
                    if h == 0:
                        sq_free[0] = t
                        split_c(7, dve)
            tmp_free = [[t] for _ in range(4)]
            sq_free[:] = [t, t]
            acc_free[0] = t
            t_qk = t
            v2t = [[None, None] for _ in range(4)]
            for c in range(2):
                w, s, wt = chunk("ml_wv", 2 * l + c, (4, 256))
                for tt in range(4):
                    b = take()
                    for h in (2 * c, 2 * c + 1):
                        for kk in range(2):
                            t = mm(PS[b][:, 256 * (h % 2):256 * (h % 2) + 256], XM[:, 2 * h + kk, 3 + P * tt:3 + P * tt + P],
                                   w[:, 2 * (h % 2) + kk, :], kk == 0, kk == 1, wt, xmt[2 * h + kk], sig=kk == 1)
                    a = A(act, V2[:, tt, T * c:T * c + T], PS[b][:, :], ACT.Copy, t, t_qk)
                    give(b, a)
                    v2t[tt][c] = a
                release(s, t)
            b = take()
            for c in range(2):
                w, s, wt = chunk("ml_wvT", 2 * l + c, (4, 256))
                for h in (2 * c, 2 * c + 1):
                    for mt in range(2):
                        m = 2 * h + mt
                        for kk in range(2):
                            t = mm(PS[b][:, 32 * m:32 * m + 32], w[:, 2 * (h % 2) + kk, P * mt:P * mt + P], WIF[:, 16 + 2 * h + kk, :],
                                   kk == 0, kk == 1, wt, t_wif, sig=kk == 1)
                release(s, t)
            gv = A(act, GV, PS[b][:, 0:256].rearrange("p (a b) -> p a b", b=32), ACT.Copy, t, start)
            give(b, gv)
            b = take()
            lhs = [WIF[:, k, :] for k in range(16)] + [GV[:, k, :] for k in range(8)]
            rhs = [Q2[:, k, :] for k in range(8)] + [K2[:, k, :] for k in range(8)] + [XM[:, k, 3:515] for k in range(8)]
            for k, tok in enumerate(qtk + ktk + [gv] + xmt[1:]):
                o = PS[b][32 * (k % 4):32 * (k % 4) + 32, :]
                t = mm(o, lhs[k], rhs[k], k < 4, k >= 20, t_wif, tok, sig=k >= 20)
            t_qkv = t
            OG = [TMP[:, 0, :], TMP[:, 1, :], SQ[:, 0, :], SQ[:, 1, :], RS, RR, TMP[:, 2, :], TMP[:, 3, :]]
            og_free = [tmp_free[0], tmp_free[1], sq_free[0], sq_free[1], None, None]
            ogt = []

            def out_gate(m, *free):
                b, t = proj(3, m)
                a = A(act, OG[m], PS[b][:, :], ACT.Sigmoid, t, *free)
                give(b, a)
                ogt.append(a)

            GB = XR[:, 0, :]
            FE, FC, EE, MM, NM, ZR = (XR[:, i, :] for i in range(1, 7))
            ln_ = XR[:, 7, :]
            a = A(act, GB, PS[b][:, :], ACT.Identity, t, t_vec, bias=vec("b_if", l))
            give(b, a)
            bi, bf = take(), take()
            ti = mm(PS[bi][:, :], const("sel_i"), GB, True, True, a, t_const, sig=True)
            tf = mm(PS[bf][:, :], const("sel_f"), GB, True, True, sig=True)
            zt = pool(lambda e: e.memset(ZR, 0.0), t_qkv)
            d = A(act, ln_, PS[bf][:, :], ACT.Abs, tf, t_qkv)
            a = A(act, ln_, ln_, ACT.Exp, d, scale=-1.0)
            a = A(act, ln_, ln_, ACT.Ln, a, bias=1.0)
            d = STT(FE, PS[bf][:, :], 0.0, ln_, ALU.min, S_, a)
            give(bf, d)
            d = dve(lambda e: e.tensor_tensor_scan(out=FC, data0=FE, data1=ZR, initial=0.0, op0=A_, op1=A_), d, zt)
            te = TT(dve, EE, PS[bi][:, :], FC, S_, ti, d)
            give(bi, te)
            d = dve(lambda e: e.tensor_tensor_scan(out=MM, data0=EE, data1=ZR, initial=0.0, op0=ALU.max, op1=ALU.max), te)
            nmt = TS(dve, NM, MM, -1.0, None, M_, None, d)
            mt_ = TT(dve, MM, MM, FC, A_, nmt)
            for m in range(3):
                out_gate(m, og_free[m])
            b = take()
            for j in range(4):
                t = tr(PS[b][:, P * j:P * j + P], EE[:, P * j:P * j + P], IDENT, te, sig=j == 3)
            et = A(act, ET, PS[b][:, :].rearrange("p (j h x) -> p j h x", j=4, h=4)[:, :, :, 0], ACT.Copy, t, start)
            give(b, et)

            sqt = []

            def gated(h):
                ps = [TT(pool, Q2[:, m, :], Q2[:, m, :], OG[m], M_, ogt[m], cellt[m], t_cell) for m in (2 * h, 2 * h + 1)]
                ss = [A(act, OG[m], Q2[:, m, :], ACT.Square, p) for m, p in zip((2 * h, 2 * h + 1), ps)]
                sqt.append(TT(pool, OG[2 * h], OG[2 * h], OG[2 * h + 1], A_, *ss))

            WB = [XR[:, 0, :], XR[:, 1, :]]
            SBF = [XR[:, 6, :], XR[:, 7, :]]
            wb_free = [[nmt, ti, tf], [nmt]]
            s_free = [[d, zt, nmt], [nmt]]
            cellt = []
            AB = XR[:, 2, :]
            finish, ab_free = None, [mt_]
            for h in range(4):
                r = slice(32 * h, 32 * h + 1)
                bM, bE = take(), take()
                tM = mm(PS[bM][:, :], const("ones")[r, :], NM[r, :], True, True, nmt, sig=True)
                tE = mm(PS[bE][:, :], const("ones")[r, :], MM[r, :], True, True, mt_, sig=True)
                EM = TMP[:, 2 + h % 2, :]
                em = A(act, EM, PS[bE][:, :], ACT.Exp, tE, tmp_free[2 + h % 2], scale=-1.0)
                give(bE, em)
                jobs = []

                def score(j):
                    b = take()
                    for kk in range(2):
                        t = mm(PS[b][:, P * j:T], K2[:, 2 * h + kk, P * j:P * j + P], Q2[:, 2 * h + kk, P * j:T], kk == 0, kk == 1,
                               qtk[2 * h + kk], ktk[2 * h + kk], sig=kk == 1)
                    q = (4 * h + j) % 2
                    diag = WB[q][:, P * j:P * j + P]
                    d = TS(dve, diag, PS[bM][:, P * j:P * j + P], ET[:, j, h:h + 1], 0.0, A_, ALU.min, tM, et, wb_free[q])
                    a = A(act, diag, diag, ACT.Exp, d)
                    a0 = a
                    if j < 3:
                        a0 = A(act, WB[q][:, P * j + P:T], PS[bM][:, P * j + P:T], ACT.Exp, tM, et, wb_free[q], bias=ET[:, j, h:h + 1])
                    p = pool(lambda e: e.affine_select(out=WB[q][:, P * j:P * j + P], in_=WB[q][:, P * j:P * j + P],
                                                       compare_op=ALU.is_ge, fill=0.0, base=0, pattern=[[1, P]],
                                                       channel_multiplier=-1), a)
                    a = [a0, d]
                    d = STT(SBF[q][:, P * j:T], PS[b][:, P * j:T], 1.0 / 16, WB[q][:, P * j:T], M_, M_, t, p, a0, s_free[q])
                    wb_free[q] = [d]
                    give(b, d)
                    return j, q, d, a

                def reduce_(j, q, d, a):
                    x = SBF[q][:, P * j:T]
                    mm(PS[bD][:, P * j:T], ONES, x, j == 0, j == 3, d)
                    mm(PS[bN0][:, P * j:T], V2[:, j, 256 * h:256 * h + P], x, j == 0, j == 3, v2t[j][h // 2])
                    t = mm(PS[bN1][:, P * j:T], V2[:, j, 256 * h + P:256 * h + 256], x, j == 0, j == 3, sig=True)
                    s_free[q] = [t]
                    return t

                jobs.append(score(0))
                jobs.append(score(1))
                if finish is not None:
                    finish()
                    out_gate(h + 2, og_free[h + 2])
                    if h > 1:
                        gated(h - 2)
                bD, bN0, bN1 = take(), take(), take()
                reduce_(*jobs.pop(0))
                for j in (2, 3):
                    jobs.append(score(j))
                    reduce_(*jobs.pop(0))
                give(bM, jobs[0][3])
                t_cell = reduce_(*jobs.pop(0))

                def finish(h=h, t=t_cell, EM=EM, em=em, bD=bD, bNs=(bN0, bN1)):
                    ab = A(act, AB, PS[bD][:, :], ACT.Abs, t, ab_free)
                    give(bD, ab)
                    d = TT(dve, EM, EM, AB, ALU.max, ab, em)
                    ab_free[:] = [d]
                    d = RECIP(EM, EM, d)
                    for z, bN in enumerate(bNs):
                        d = TT(dve, Q2[:, 2 * h + z, :], PS[bN][:, :], EM, M_, d, t)
                        give(bN, d)
                        cellt.append(d)
                    tmp_free[2 + h % 2] = [d]
            finish()
            gated(2)
            cells_done = t_cell

            yp = []
            for m in range(8):
                h = A(act, YRH[:, m, :], Y[:, m, :], ACT.Copy, yt[m], cells_done)
                yp.append((h, TT(dve, YRL[:, m, :], Y[:, m, :], YRH[:, m, :].bitcast(F32), S_, h)))

            RH = XR
            out_gate(6, tmp_free[2])
            out_gate(7, tmp_free[3])
            gated(3)
            normed = []
            for m in range(8):
                b, t = proj(4, m)
                a = A(act, K2[:, m, :], PS[b][:, :], ACT.Sigmoid, t, cells_done)
                d = TT(dve, K2[:, m, :], K2[:, m, :], PS[b][:, :], M_, a)
                give(b, d)
                if m % 2 == 0:
                    h = m // 2
                    b = take()
                    ts = mm(PS[b][:, :], ONES, OG[m], True, True, sqt[h], sig=True)
                    r = TS(dve, RH[:, h, :], PS[b][:, :], 1.0 / 256, EPS, M_, A_, ts, cells_done)
                    give(b, r)
                    a = A(act, RH[:, h, :], RH[:, h, :], ACT.Sqrt, r)
                    r = RECIP(RH[:, h, :], RH[:, h, :], a)
                d2 = STT(Q2[:, m, :], Q2[:, m, :], vec("ml_norm_g", 8 * l + m), RH[:, h, :], M_, M_, r)
                normed.append(TT(dve, Q2[:, m, :], Q2[:, m, :], K2[:, m, :], M_, d2, d))
            proj_done = t
            tmp_free = [[ts] for _ in range(4)]
            sq_free[:] = [ts, ts]
            for m in range(8):
                hi = A(act, HNH[:, m, :], Q2[:, m, :], ACT.Copy, normed[m], proj_done)
                yp.append((hi, TT(dve, HNL[:, m, :], Q2[:, m, :], HNH[:, m, :].bitcast(F32), S_, hi)))
            yh = [YRH[:, k, :] for k in range(8)] + HNHk
            yl = [YRL[:, k, :] for k in range(8)] + HNLk
            bo = {}
            for m, c in out2_order():
                if c == 0:
                    bo[m] = take()
                b = bo[m]
                w = wchunk("w_out2", 16 * l + 2 * m + c, 8)
                t = dense3(PS[b][:, :], w, yh, yl, yp, 8 * c, 8, c == 0, c == 1)
                wrelease(w[2], t)
                if c == 0:
                    continue
                HT[m] = STT(H[:, m, :], PS[b][:, :], MOD[:, 24 * l + 16 + m:24 * l + 17 + m], H[:, m, :], M_, A_, t, HT[m])
                give(b, HT[m])
                if m < KD - 1:
                    ta = square(m, ACC, HT[m])
                else:
                    tl = square_last(HT[m])
            ple_done = t

        r1 = rstd_last(RS, ta, tl, None)
        OUT = ar(0, 8, T)
        nout = 0
        done = everyone()
        for k in range(KD):
            if k % 4 == 3:
                g = TS(pool, OUT[:, k, :], H[:, k, :], vec("final_g", k), None, M_, None, HT[k], done)
                t = TT(pool, OUT[:, k, :], OUT[:, k, :], RS, M_, r1, g)
            else:
                t = STT(OUT[:, k, :], H[:, k, :], vec("final_g", k), RS, M_, M_, r1, done)
            q = sp if k % 2 else act
            q.wait(t)
            q.ops.append(lambda e, k=k: e.dma_start(out[:, k:k + 1, :], OUT[:, k:k + 1, :]).then_inc(s_out, 16))
            nout += 16
        sp.ops.append(lambda e: e.wait_ge(s_out, nout))

        block = ctx.enter_context(nc.Block())

        def play(q):
            def run(e):
                for op in q.ops:
                    op(e)
            return run

        block.sync(play(sp))
        block.scalar(play(act))
        block.vector(play(dve))
        block.gpsimd(play(pool))
        block.tensor(play(pe))


def _tiles(w, mc):
    k, m = w.shape
    return np.ascontiguousarray(w.reshape(k // P, P, m // mc, mc).transpose(2, 1, 0, 3).reshape(m // mc, P, -1))


def _cols(v):
    return v.reshape(-1, P).T


def _consts():
    half = 32
    inv = (np.float32(10000.0) ** (-np.arange(half, dtype=np.float32) / np.float32(half))).astype(np.float32)
    ang = (np.arange(T, dtype=np.float32)[:, None] * inv[None, :]).astype(np.float64)
    cos, sin = np.cos(ang).T, np.sin(ang).T
    c = {}
    c["cos"] = np.tile(cos, (4, 1))
    c["sin"] = np.concatenate([-sin, sin, -sin, sin], 0)
    c["ident"] = np.eye(P)
    c["ones"] = np.ones((P, P))
    c["rot"] = np.eye(P)[np.arange(P) ^ 32]
    i = np.arange(P)
    c["causal"] = np.where(i[None, :] <= i[:, None], 0.0, NEG)
    tok = np.arange(4)[None, :, None] * P + i[:, None, None]
    end = np.arange(32)[None, None, :] * 16 + 31
    ok = (end <= tok) & (np.arange(32)[None, None, :] < 31)
    c["cneg"] = np.where(ok, 0.0, NEG).reshape(P, 128)
    c["c01"] = ok.astype(np.float32).reshape(P, 128)
    for z, n in enumerate(("sel_i", "sel_f")):
        s = np.zeros((P, P))
        for h in range(4):
            s[4 * z + h::32, 32 * h] = 1.0
        c[n] = s
    return np.ascontiguousarray(np.concatenate([c[n] for n, _ in CONST_COLS], 1).astype(np.float32))


def _layout(I):
    f = np.float32
    A = {}
    A["xT"] = np.ascontiguousarray(I["x"][0].T.reshape(8, P, T).transpose(1, 0, 2))
    A["pT"] = np.ascontiguousarray(I["p"][0, 0].T.reshape(2, P, T).transpose(1, 0, 2))
    for z, n in (("a", "ffn1"), ("b", "ffn2")):
        w1, w3 = (_tiles(I[f"{n}_w{k}"][0], P) for k in (1, 3))
        A["w13" + z] = np.ascontiguousarray(np.stack([w1, w3], 1).reshape(44, P, 1024))
        w2 = I[f"{n}_w2"][0]
        A["w2" + z] = np.concatenate([_tiles(w2[1408 * k:1408 * k + 1408], P) for k in range(2)], 0)
    perm = np.concatenate([h * 64 + np.arange(64) for i in range(4) for h in (i, 4 + i)])
    heads = [h for i in range(4) for h in (i, 4 + i)]
    w = I["w_in"][0]
    part = lambda k: w[:, 512 + 128 * k:640 + 128 * k]
    A["w_inA"] = _tiles(np.concatenate([w[:, 1304:1816], part(0), part(1), part(2), part(4), w[:, perm]], 1), P)
    wg = w[:, 1280:1304].reshape(1024, 8, 3)[:, heads, :].transpose(0, 2, 1).reshape(1024, 24)
    wv = np.concatenate([part(3), part(5), wg], 1)
    A["w_inV"] = np.concatenate([_tiles(wv[512 * z:512 * z + 512], 280) for z in range(2)], 0)
    wk2 = I["cmp_wk2"][0]
    A["small_w"] = np.ascontiguousarray(np.concatenate(
        [_tiles(np.concatenate([wk2, wk2], 1), P)[0], _tiles(I["cmp_wv2"][0], 64)[0]], 1))
    for n in ("wk1", "wv1"):
        a = I["cmp_" + n][0]
        A[n] = np.concatenate([_tiles(a[512 * k:512 * k + 512], 256) for k in range(4)], 0)
    bc = np.zeros((P, 2048), f)
    for z, n in enumerate(("s5_b_re", "s5_b_im")):
        b = I[n][0]
        for g in range(32):
            y4, j, g2 = g // 8, (g % 8) // 2, g % 2
            bc[32 * j + 16 * g2:32 * j + 16 * g2 + 16, 512 * z + P * y4 + 64 * g2:512 * z + P * y4 + 64 * g2 + 64] = b[g].T
    for z, n in enumerate(("s5_c_re", "s5_c_im")):
        c = I[n][0]
        for g in range(32):
            t, g2 = g // 2, g % 2
            at = 1024 + 512 * z + 32 * t + 16 * g2
            bc[64 * g2:64 * g2 + 64, at:at + 16] = c[g].T
    A["s5_bc"] = bc
    A["w_glu"] = _tiles(I["s5_w_glu"][0], P)
    wo = I["w_out"][0]
    A["w_out"] = _tiles(np.concatenate([wo[:512][perm], wo[512:]], 0), P)
    A["w_pg"] = _tiles(I["w_ple_gate"][0], P)
    A["w_ple"] = _tiles(I["w_ple"][0], 1024)[0]
    A["c"] = np.ascontiguousarray(I["c_2"].reshape(1024))
    wa = np.concatenate([I["w_ada_2"][l].T.reshape(24, P, 1024) for l in range(2)], 0)
    A["w_ada"] = np.ascontiguousarray(wa)
    A["w_in2"] = np.concatenate([_tiles(I["w_in_2"][l], P) for l in range(2)], 0)
    A["rg_w"] = np.ascontiguousarray(np.stack([np.concatenate(
        [I[n][l].transpose(1, 0, 2).reshape(P, 1024) for n in ("rg_w_a_2", "rg_w_x_2")], 1) for l in range(2)]))

    def heads4(a):
        return a.reshape(2, 4, P, 256).transpose(0, 2, 1, 3).reshape(2, P, 1024)
    A["ml_wqk"] = np.ascontiguousarray(np.concatenate([heads4(I[n][l]) for l in range(2) for n in ("ml_w_q_2", "ml_w_k_2")]))
    A["ml_wv"] = np.ascontiguousarray(np.concatenate([heads4(I["ml_w_v_2"][l]) for l in range(2)]))
    A["ml_wvT"] = np.ascontiguousarray(np.concatenate([heads4(I["ml_w_v_2"][l].transpose(0, 2, 1)) for l in range(2)]))
    wif = np.zeros((2, P, 24, 32), f)
    wif[:, :, :, 0:8] = np.stack([I["ml_w_if_2"][l].reshape(24, P, 8).transpose(1, 0, 2) for l in range(2)])
    A["w_if"] = wif.reshape(2, P, 768)
    A["w_out2"] = np.concatenate([_tiles(I["w_out_2"][l], P).reshape(8, P, 2, 1024).transpose(0, 2, 1, 3).reshape(16, P, 1024)
                                  for l in range(2)], 0)
    two = lambda a: np.concatenate([_cols(a[l]) for l in range(2)], 1)
    conv = lambda a: np.concatenate([_cols(a[l, i]) for l in range(2) for i in range(4)], 1)
    bif = np.zeros((P, 2), f)
    bif[0:8, :] = I["ml_b_if_2"].T
    V = {
        "norm_ffn1": _cols(I["norm_ffn1"][0]), "norm_mix": _cols(I["norm_mix"][0]), "norm_ffn2": _cols(I["norm_ffn2"][0]),
        "norm_ple": _cols(I["norm_ple"][0]), "norm_final": _cols(I["norm_final"]),
        "a_re": _cols(I["s5_a_re"][0]), "a_im": _cols(I["s5_a_im"][0]), "log_dt": _cols(np.repeat(I["s5_log_dt"][0], 64)),
        "s5_d": _cols(I["s5_d"][0]), "b_glu": _cols(I["s5_b_glu"][0]), "pe_k": _cols(I["cmp_pe_k"][0]), "pe_v": _cols(I["cmp_pe_v"][0]),
        "norm_g": two(I["norm_g_2"]), "b_ada": two(I["b_ada_2"]),
        "rg_conv_w": conv(I["rg_conv_w_2"]), "rg_conv_b": two(I["rg_conv_b_2"]), "rg_b_a": two(I["rg_b_a_2"]), "rg_b_x": two(I["rg_b_x_2"]),
        "rg_lam": two(I["rg_lambda_2"]), "ml_conv_w": conv(I["ml_conv_w_2"]), "ml_conv_b": two(I["ml_conv_b_2"]),
        "ml_norm_g": two(I["ml_norm_g_2"]), "final_g": _cols(I["final_g_2"]), "b_if": bif,
    }
    A["vecs"] = np.ascontiguousarray(np.concatenate([V[n] for n, _ in VEC_COLS], 1))
    A["consts"] = _consts()
    return A


def kernel(**inputs):
    import concourse.bacc as bacc
    from concourse.bass_utils import run_bass_kernel_spmd

    I = {k: np.asarray(v) for k, v in inputs.items()}
    nc = bacc.Bacc("TRN2", target_bir_lowering=False, num_devices=1)
    arrays, D = {}, {}
    for name, a in _layout(I).items():
        arrays[f"in_{name}"] = a
        D[name] = nc.dram_tensor(f"in_{name}", a.shape, mybir.dt.from_np(a.dtype), kind="ExternalInput").ap()
    out = nc.dram_tensor("out_0", (P, 8, T), F32, kind="ExternalOutput").ap()
    program(nc, D, out)
    r = run_bass_kernel_spmd(nc, [arrays], core_ids=[0])
    o = r.results[0]["out_0"]
    return np.ascontiguousarray(o.transpose(1, 0, 2).reshape(1024, T).T)[None]
```
